# Optimizing a Trainium2 kernel written in Bass

```python
import jax, jax.numpy as jnp
from jax import lax
import numpy as np

D_MODEL = 1024
BATCH = 1
SEQ = 512
DEPTH = 1

MEM_LEN = 256
N_MIXERS = 4
GROUP_WIDTH = D_MODEL // N_MIXERS
N_HEADS = 4
HEAD_DIM = GROUP_WIDTH // N_HEADS
GLA_KEY_DIM = HEAD_DIM // 2
GLA_LOWRANK = 16
GLA_GATE_NORM = 16.0
GDN_CONV = 4
CHUNK = 64
ROPE_BASE = 10000.0
XATTN_HEADS = 4
XATTN_HEAD_DIM = D_MODEL // XATTN_HEADS
D_FF = 2816
FFN_CONV = 3
EPS = 1e-6

IN_SPLITS = (
    GROUP_WIDTH, GROUP_WIDTH, GROUP_WIDTH, GROUP_WIDTH,
    GROUP_WIDTH, GROUP_WIDTH, GROUP_WIDTH, N_HEADS, N_HEADS, GROUP_WIDTH,
    N_HEADS * GLA_KEY_DIM, N_HEADS * GLA_KEY_DIM, GROUP_WIDTH, GLA_LOWRANK, GROUP_WIDTH,
    GROUP_WIDTH, GROUP_WIDTH, GROUP_WIDTH, GROUP_WIDTH,
)
IN_WIDTH = sum(IN_SPLITS)


def _rmsnorm(x, w):
    xf = x.astype(jnp.float32)
    y = xf * lax.rsqrt(jnp.mean(xf * xf, axis=-1, keepdims=True) + EPS)
    return (y * w.astype(jnp.float32)).astype(x.dtype)

def _norm_f32(x):
    return x * lax.rsqrt(jnp.mean(x * x, axis=-1, keepdims=True) + EPS)

def _l2norm(x):
    return x * lax.rsqrt(jnp.sum(x * x, axis=-1, keepdims=True) + EPS)

def _rope(x, positions):
    d = x.shape[-1]
    freqs = ROPE_BASE ** (-jnp.arange(0, d, 2, dtype=jnp.float32) / d)
    ang = positions.astype(jnp.float32)[..., None] * freqs
    cos, sin = jnp.cos(ang)[:, :, None, :], jnp.sin(ang)[:, :, None, :]
    x1, x2 = jnp.split(x, 2, axis=-1)
    return jnp.concatenate([x1 * cos - x2 * sin, x1 * sin + x2 * cos], axis=-1)

def _causal_dwconv(x, w):
    k, c = w.shape
    return lax.conv_general_dilated(
        x, w[:, None, :].astype(x.dtype), window_strides=(1,), padding=[(k - 1, 0)],
        dimension_numbers=('NWC', 'WIO', 'NWC'), feature_group_count=c)

def _to_chunks(t):
    b, tt, h = t.shape[:3]
    t = t.reshape((b, tt // CHUNK, CHUNK, h) + t.shape[3:])
    return jnp.moveaxis(t, 3, 1)

def _from_chunks(t):
    b, h, n, c, d = t.shape
    return jnp.moveaxis(t, 1, 3).reshape(b, n * c, h, d)

def _retention_chunked(q, k, v, log_gamma):
    c = q.shape[3]
    idx = jnp.arange(c, dtype=jnp.float32)
    lg = log_gamma[:, None]
    rel = idx[:, None] - idx[None, :]
    decay = jnp.where(rel >= 0, jnp.exp(lg[:, :, None] * jnp.maximum(rel, 0.0)), 0.0)
    scores = jnp.einsum('bhncd,bhnsd->bhncs', q, k) * decay[None, :, None]
    o_intra = jnp.einsum('bhncs,bhnsv->bhncv', scores, v)
    q_decay = jnp.exp(lg * (idx + 1.0))
    k_decay = jnp.exp(lg * (c - 1.0 - idx))
    chunk_decay = jnp.exp(log_gamma * c)
    kv = jnp.einsum('bhncd,bhncv->bhndv', k * k_decay[None, :, None, :, None], v)

    def step(state, inp):
        kv_n, q_n = inp
        o = jnp.einsum('bhcd,bhdv->bhcv', q_n, state) * q_decay[None, :, :, None]
        state = state * chunk_decay[None, :, None, None] + kv_n
        return state, o

    b, h, _, _, dk = q.shape
    s0 = jnp.zeros((b, h, dk, v.shape[-1]), jnp.float32)
    _, o_inter = lax.scan(step, s0, (jnp.moveaxis(kv, 2, 0), jnp.moveaxis(q, 2, 0)))
    return o_intra + jnp.moveaxis(o_inter, 0, 2)

def _gated_delta_chunked(q, k, v, beta, g):
    c = q.shape[3]
    gc = jnp.cumsum(g, axis=-1)
    causal = jnp.tril(jnp.ones((c, c), dtype=bool))
    strict = jnp.tril(jnp.ones((c, c), dtype=bool), k=-1)
    ratio = jnp.exp(jnp.where(causal, gc[..., :, None] - gc[..., None, :], -jnp.inf))
    kk = jnp.where(strict, jnp.einsum('bhncd,bhnsd->bhncs', k, k) * ratio, 0.0)
    a_mat = jnp.eye(c, dtype=jnp.float32) + beta[..., None] * kk
    gamma = jnp.exp(gc)
    u_v = lax.linalg.triangular_solve(a_mat, beta[..., None] * v, left_side=True, lower=True, unit_diagonal=True)
    w_k = lax.linalg.triangular_solve(a_mat, (beta * gamma)[..., None] * k, left_side=True, lower=True, unit_diagonal=True)
    qk = jnp.einsum('bhncd,bhnsd->bhncs', q, k) * ratio
    q_g = q * gamma[..., None]
    k_tail = k * jnp.exp(gc[..., -1:] - gc)[..., None]
    chunk_decay = jnp.exp(gc[..., -1])

    def step(state, inp):
        uv_n, w_n, qk_n, qg_n, kt_n, cd_n = inp
        u = uv_n - jnp.einsum('bhcd,bhdv->bhcv', w_n, state)
        o = jnp.einsum('bhcd,bhdv->bhcv', qg_n, state) + jnp.einsum('bhcs,bhsv->bhcv', qk_n, u)
        state = cd_n[..., None, None] * state + jnp.einsum('bhcd,bhcv->bhdv', kt_n, u)
        return state, o

    b, h, _, _, dk = q.shape
    s0 = jnp.zeros((b, h, dk, v.shape[-1]), jnp.float32)
    xs = tuple(jnp.moveaxis(t, 2, 0) for t in (u_v, w_k, qk, q_g, k_tail, chunk_decay))
    _, o = lax.scan(step, s0, xs)
    return jnp.moveaxis(o, 0, 2)

def _gated_linear_chunked(q, k, v, log_f):
    c = q.shape[3]
    gc = jnp.cumsum(log_f, axis=3)
    causal = jnp.tril(jnp.ones((c, c), dtype=bool))[:, :, None]

    def step(state, inp):
        q_n, k_n, v_n, g_n = inp
        diff = g_n[:, :, :, None, :] - g_n[:, :, None, :, :]
        decay = jnp.exp(jnp.where(causal, diff, -jnp.inf))
        scores = jnp.einsum('bhcd,bhsd,bhcsd->bhcs', q_n, k_n, decay)
        o = jnp.einsum('bhcs,bhsv->bhcv', scores, v_n) + jnp.einsum('bhcd,bhdv->bhcv', q_n * jnp.exp(g_n), state)
        k_tail = k_n * jnp.exp(g_n[:, :, -1:] - g_n)
        state = jnp.exp(g_n[:, :, -1])[..., None] * state + jnp.einsum('bhcd,bhcv->bhdv', k_tail, v_n)
        return state, o

    b, h, _, _, dk = q.shape
    s0 = jnp.zeros((b, h, dk, v.shape[-1]), jnp.float32)
    xs = tuple(jnp.moveaxis(t, 2, 0) for t in (q, k, v, gc))
    _, o = lax.scan(step, s0, xs)
    return jnp.moveaxis(o, 0, 2)

def _hybrid_mixer(h, positions, w_in, gdn_conv_w, gdn_a_log, gdn_dt_bias, gdn_norm_w,
                  gla_gk_up, gla_gk_bias, gla_norm_w, hgrn_lb, hgrn_norm_w, w_out):
    b, t, _ = h.shape
    f32 = jnp.float32
    z = jnp.matmul(h, w_in).astype(f32)
    split_points = [int(p) for p in np.cumsum(IN_SPLITS)[:-1]]
    (rq, rk, rv, rg, bq, bk, bv, ba, bb, bg,
     cq, ck, cv, c_lr, cg, dq, df, di, dg) = jnp.split(z, split_points, axis=-1)

    def heads(a):
        return a.reshape(b, t, N_HEADS, -1)

    q_a = _rope(heads(rq), positions)
    k_a = _rope(heads(rk), positions) * HEAD_DIM ** -0.5
    log_gamma = jnp.log(1.0 - jnp.exp2(-5.0 - jnp.arange(N_HEADS, dtype=f32)))
    o_a = _from_chunks(_retention_chunked(_to_chunks(q_a), _to_chunks(k_a), _to_chunks(heads(rv)), log_gamma))
    o_a = _norm_f32(o_a) * jax.nn.silu(heads(rg))

    qkv = jax.nn.silu(_causal_dwconv(jnp.concatenate([bq, bk, bv], axis=-1), gdn_conv_w.astype(f32)))
    q_b, k_b, v_b = jnp.split(qkv, 3, axis=-1)
    q_b = _l2norm(heads(q_b)) * HEAD_DIM ** -0.5
    k_b = _l2norm(heads(k_b))
    beta = jax.nn.sigmoid(bb)
    g_b = -jnp.exp(gdn_a_log.astype(f32)) * jax.nn.softplus(ba + gdn_dt_bias.astype(f32))
    o_b = _from_chunks(_gated_delta_chunked(_to_chunks(q_b), _to_chunks(k_b), _to_chunks(heads(v_b)),
                                            _to_chunks(beta), _to_chunks(g_b)))
    o_b = _norm_f32(o_b) * gdn_norm_w.astype(f32) * jax.nn.silu(heads(bg))

    q_c = heads(cq) * GLA_KEY_DIM ** -0.5
    log_f_c = jax.nn.log_sigmoid(jnp.matmul(c_lr, gla_gk_up.astype(f32)) + gla_gk_bias.astype(f32)) / GLA_GATE_NORM
    o_c = _from_chunks(_gated_linear_chunked(_to_chunks(q_c), _to_chunks(heads(ck)), _to_chunks(heads(cv)),
                                             _to_chunks(heads(log_f_c))))
    o_c = _norm_f32(o_c) * gla_norm_w.astype(f32) * jax.nn.silu(heads(cg))

    lb = hgrn_lb.reshape(N_HEADS, HEAD_DIM)
    f_pre = heads(df)
    log_f_d = jnp.logaddexp(jnp.log(lb), jnp.log1p(-lb) + jax.nn.log_sigmoid(f_pre))
    k_d = (1.0 - lb) * jax.nn.sigmoid(-f_pre)
    o_d = _from_chunks(_gated_linear_chunked(_to_chunks(heads(dq)), _to_chunks(k_d), _to_chunks(heads(di)),
                                             _to_chunks(log_f_d)))
    o_d = _norm_f32(o_d) * hgrn_norm_w.astype(f32) * jax.nn.silu(heads(dg))

    o = jnp.concatenate([o_a.reshape(b, t, GROUP_WIDTH), o_b.reshape(b, t, GROUP_WIDTH),
                         o_c.reshape(b, t, GROUP_WIDTH), o_d.reshape(b, t, GROUP_WIDTH)], axis=-1)
    return jnp.matmul(o.astype(h.dtype), w_out)

def _memory_cross_attn(h, mem_n, wq, wk, wv, wo):
    b, t, _ = h.shape
    m = mem_n.shape[1]
    q = jnp.matmul(h, wq).reshape(b, t, XATTN_HEADS, XATTN_HEAD_DIM)
    k = jnp.matmul(mem_n, wk).reshape(b, m, XATTN_HEADS, XATTN_HEAD_DIM)
    v = jnp.matmul(mem_n, wv).reshape(b, m, XATTN_HEADS, XATTN_HEAD_DIM)
    s = jnp.einsum('bthd,bmhd->bhtm', q, k).astype(jnp.float32) * XATTN_HEAD_DIM ** -0.5
    p = jax.nn.softmax(s, axis=-1).astype(v.dtype)
    o = jnp.einsum('bhtm,bmhd->bthd', p, v).reshape(b, t, D_MODEL)
    return jnp.matmul(o, wo)

def _conv_ffn(h, w_up, conv_w, w_down):
    u = _causal_dwconv(jnp.matmul(h, w_up), conv_w)
    gate, val = jnp.split(u, 2, axis=-1)
    return jnp.matmul(jax.nn.silu(gate) * val, w_down)

def first_inputs(seed: int = 0) -> dict:
    key = jax.random.key(seed)
    ks = jax.random.split(key, 26)
    nrm = jax.random.normal

    def gain(k, shape):
        return 1.0 + 0.02 * nrm(k, shape, jnp.float32)

    dt = jnp.exp(jax.random.uniform(ks[6], (DEPTH, N_HEADS), jnp.float32, np.log(1e-3), np.log(1e-1)))
    pos_offset = jax.random.randint(ks[2], (BATCH, 1), 0, 4096, dtype=jnp.int32)
    return {
        'x': nrm(ks[0], (BATCH, SEQ, D_MODEL), jnp.float32),
        'mem': nrm(ks[1], (BATCH, MEM_LEN, D_MODEL), jnp.float32),
        'positions': pos_offset + jnp.arange(SEQ, dtype=jnp.int32)[None, :],
        'mix_norm_w': gain(ks[3], (DEPTH, D_MODEL)),
        'w_in': nrm(ks[4], (DEPTH, D_MODEL, IN_WIDTH), jnp.float32) * D_MODEL ** -0.5,
        'gdn_conv_w': nrm(ks[5], (DEPTH, GDN_CONV, 3 * GROUP_WIDTH), jnp.float32) * GDN_CONV ** -0.5,
        'gdn_a_log': jnp.log(jax.random.uniform(ks[7], (DEPTH, N_HEADS), jnp.float32, 1.0, 16.0)),
        'gdn_dt_bias': dt + jnp.log(-jnp.expm1(-dt)),
        'gdn_norm_w': gain(ks[8], (DEPTH, HEAD_DIM)),
        'gla_gk_up': nrm(ks[9], (DEPTH, GLA_LOWRANK, N_HEADS * GLA_KEY_DIM), jnp.float32) * GLA_LOWRANK ** -0.5,
        'gla_gk_bias': 0.02 * nrm(ks[10], (DEPTH, N_HEADS * GLA_KEY_DIM), jnp.float32),
        'gla_norm_w': gain(ks[11], (DEPTH, HEAD_DIM)),
        'hgrn_lb_logits': 0.1 * nrm(ks[12], (DEPTH, GROUP_WIDTH), jnp.float32),
        'hgrn_norm_w': gain(ks[13], (DEPTH, HEAD_DIM)),
        'w_out': nrm(ks[14], (DEPTH, D_MODEL, D_MODEL), jnp.float32) * D_MODEL ** -0.5,
        'xattn_norm_w': gain(ks[15], (DEPTH, D_MODEL)),
        'mem_norm_w': gain(ks[16], (D_MODEL,)),
        'xattn_wq': nrm(ks[17], (DEPTH, D_MODEL, D_MODEL), jnp.float32) * D_MODEL ** -0.5,
        'xattn_wk': nrm(ks[18], (DEPTH, D_MODEL, D_MODEL), jnp.float32) * D_MODEL ** -0.5,
        'xattn_wv': nrm(ks[19], (DEPTH, D_MODEL, D_MODEL), jnp.float32) * D_MODEL ** -0.5,
        'xattn_wo': nrm(ks[20], (DEPTH, D_MODEL, D_MODEL), jnp.float32) * D_MODEL ** -0.5,
        'ffn_norm_w': gain(ks[21], (DEPTH, D_MODEL)),
        'ffn_up': nrm(ks[22], (DEPTH, D_MODEL, 2 * D_FF), jnp.float32) * D_MODEL ** -0.5,
        'ffn_conv_w': nrm(ks[23], (DEPTH, FFN_CONV, 2 * D_FF), jnp.float32) * FFN_CONV ** -0.5,
        'ffn_down': nrm(ks[24], (DEPTH, D_FF, D_MODEL), jnp.float32) * D_FF ** -0.5,
        'final_norm_w': gain(ks[25], (D_MODEL,)),
    }

def first_block(x, mem, positions, mix_norm_w, w_in, gdn_conv_w, gdn_a_log, gdn_dt_bias, gdn_norm_w,
              gla_gk_up, gla_gk_bias, gla_norm_w, hgrn_lb_logits, hgrn_norm_w, w_out,
              xattn_norm_w, mem_norm_w, xattn_wq, xattn_wk, xattn_wv, xattn_wo,
              ffn_norm_w, ffn_up, ffn_conv_w, ffn_down, final_norm_w):
    lb_all = jnp.cumsum(jax.nn.softmax(hgrn_lb_logits.astype(jnp.float32), axis=0), axis=0)
    lb_all = lb_all - lb_all[0]
    mem_n = _rmsnorm(mem, mem_norm_w)
    h = x
    for l in range(DEPTH):
        h = h + _hybrid_mixer(_rmsnorm(h, mix_norm_w[l]), positions, w_in[l], gdn_conv_w[l], gdn_a_log[l],
                              gdn_dt_bias[l], gdn_norm_w[l], gla_gk_up[l], gla_gk_bias[l], gla_norm_w[l],
                              lb_all[l], hgrn_norm_w[l], w_out[l])
        h = h + _memory_cross_attn(_rmsnorm(h, xattn_norm_w[l]), mem_n, xattn_wq[l], xattn_wk[l],
                                   xattn_wv[l], xattn_wo[l])
        h = h + _conv_ffn(_rmsnorm(h, ffn_norm_w[l]), ffn_up[l], ffn_conv_w[l], ffn_down[l])
    return _rmsnorm(h, final_norm_w)


DEPTH_2 = 2

RNN_WIDTH = 1024
RNN_BLOCKS = 16
RNN_CONV = 4
LRU_C = 8.0
NSA_HEADS = 16
NSA_KV_HEADS = 4
HEAD_DIM_2 = 64
GQA_REP = NSA_HEADS // NSA_KV_HEADS
CMP_BLOCK = 32
CMP_STRIDE = 16
CMP_HIDDEN = 128
SLC_BLOCK = 64
SLC_TOPK = 4
WINDOW = 256
Q_CHUNK = 64
FORCE_BONUS = 1.0e4
ROPE_THETA = 500000.0
ROPE_DIM = HEAD_DIM_2 // 4
SC_WIDTH = D_MODEL
SC_CONV = 3
NEG = -1e30

AB_SPLITS = (RNN_WIDTH, RNN_WIDTH, NSA_HEADS * HEAD_DIM_2) + (NSA_KV_HEADS * HEAD_DIM_2,) * 6 + (3 * NSA_HEADS,)
AB_IN = sum(AB_SPLITS)
AB_MIX = RNN_WIDTH + NSA_HEADS * HEAD_DIM_2


def rms_norm(x, g):
    xf = x.astype(jnp.float32)
    y = xf * lax.rsqrt(jnp.mean(xf * xf, axis=-1, keepdims=True) + EPS)
    return (y * g.astype(jnp.float32)).astype(x.dtype)

def causal_dwconv(x, w, b):
    K, C = w.shape
    y = lax.conv_general_dilated(x, w[:, None, :].astype(x.dtype), window_strides=(1,),
                                 padding=[(K - 1, 0)], dimension_numbers=('NWC', 'WIO', 'NWC'),
                                 feature_group_count=C)
    return y + b.astype(x.dtype)

def rope_partial(x, pos):
    half = ROPE_DIM // 2
    inv = jnp.power(jnp.float32(ROPE_THETA), -jnp.arange(half, dtype=jnp.float32) / half)
    ang = pos.astype(jnp.float32)[:, None] * inv[None, :]
    cos = jnp.cos(ang)[None, :, None, :]
    sin = jnp.sin(ang)[None, :, None, :]
    x1 = x[..., :half].astype(jnp.float32)
    x2 = x[..., half:ROPE_DIM].astype(jnp.float32)
    rot = jnp.concatenate([x1 * cos - x2 * sin, x2 * cos + x1 * sin], axis=-1).astype(x.dtype)
    return jnp.concatenate([rot, x[..., ROPE_DIM:]], axis=-1)

def rg_lru(x, w_r, b_r, w_i, b_i, lam):
    Bsz, T, W = x.shape
    xb = x.reshape(Bsz, T, RNN_BLOCKS, W // RNN_BLOCKS)
    r = jax.nn.sigmoid(jnp.einsum('btnc,ncd->btnd', xb, w_r).reshape(Bsz, T, W) + b_r)
    i = jax.nn.sigmoid(jnp.einsum('btnc,ncd->btnd', xb, w_i).reshape(Bsz, T, W) + b_i)
    log_a = -LRU_C * r.astype(jnp.float32) * jax.nn.softplus(-lam.astype(jnp.float32))
    a = jnp.exp(log_a)
    u = jnp.sqrt(-jnp.expm1(2.0 * log_a)) * (i * x).astype(jnp.float32)

    def combine(left, right):
        a1, b1 = left
        a2, b2 = right
        return a1 * a2, a2 * b1 + b2

    _, h = lax.associative_scan(combine, (a, u), axis=1)
    return h.astype(x.dtype)

def compress(t, pe, w1, w2):
    Bsz, T, G, hd = t.shape
    n_cmp = (T - CMP_BLOCK) // CMP_STRIDE + 1
    idx = np.arange(n_cmp)[:, None] * CMP_STRIDE + np.arange(CMP_BLOCK)[None, :]
    blk = t[:, idx] + pe[:, None, :].astype(t.dtype)
    blk = blk.transpose(0, 1, 3, 2, 4).reshape(Bsz, n_cmp, G, CMP_BLOCK * hd)
    return jax.nn.gelu(blk @ w1) @ w2, idx[:, -1]

def nsa(q, kc, vc, ks, vs, kw, vw, gate_logits, pe_k, pe_v, wk1, wk2, wv1, wv2):
    Bsz, T = q.shape[:2]
    G, R, hd = NSA_KV_HEADS, GQA_REP, HEAD_DIM_2
    scale = HEAD_DIM_2 ** -0.5
    pos = jnp.arange(T)
    q_rot = rope_partial(q, pos)
    ks = rope_partial(ks, pos)
    kw = rope_partial(kw, pos)
    k_cmp, cmp_end = compress(kc, pe_k, wk1, wk2)
    v_cmp, _ = compress(vc, pe_v, wv1, wv2)
    n_cmp = k_cmp.shape[1]
    cmp_end = jnp.asarray(cmp_end)
    n_slc = T // SLC_BLOCK
    k_sel = min(SLC_TOPK, n_slc)
    cs = np.arange(n_cmp) * CMP_STRIDE
    js = np.arange(n_slc) * SLC_BLOCK
    overlap = jnp.asarray(((cs[:, None] < js[None, :] + SLC_BLOCK) &
                           (cs[:, None] + CMP_BLOCK > js[None, :])).astype(np.float32))
    ksb = ks.reshape(Bsz, n_slc, SLC_BLOCK, G, hd).transpose(0, 3, 1, 2, 4)
    vsb = vs.reshape(Bsz, n_slc, SLC_BLOCK, G, hd).transpose(0, 3, 1, 2, 4)
    kwp = jnp.pad(kw, ((0, 0), (WINDOW, 0), (0, 0), (0, 0)))
    vwp = jnp.pad(vw, ((0, 0), (WINDOW, 0), (0, 0), (0, 0)))
    bi = jnp.arange(Bsz)[:, None, None, None]
    gi = jnp.arange(G)[None, :, None, None]
    blk_ids = jnp.arange(n_slc)
    f32 = jnp.float32

    def chunk(args):
        qn, qr, gt, s = args
        t = s + jnp.arange(Q_CHUNK)
        qn5 = qn.reshape(Bsz, Q_CHUNK, G, R, hd)
        qr5 = qr.reshape(Bsz, Q_CHUNK, G, R, hd)
        sc = jnp.einsum('bqgrd,bngd->bgrqn', qn5, k_cmp, preferred_element_type=f32) * scale
        mask_c = cmp_end[None, :] <= t[:, None]
        p_c = jnp.where(mask_c, jax.nn.softmax(jnp.where(mask_c, sc, NEG), axis=-1), 0.0)
        o_c = jnp.einsum('bgrqn,bngd->bqgrd', p_c.astype(v_cmp.dtype), v_cmp, preferred_element_type=f32)
        imp = jnp.einsum('bgrqn,nj->bgqj', p_c, overlap)
        forced = (blk_ids[None, :] == 0) | (blk_ids[None, :] == (t // SLC_BLOCK)[:, None])
        imp = jnp.where(forced, imp + FORCE_BONUS, imp)
        imp = jnp.where(blk_ids[None, :] * SLC_BLOCK <= t[:, None], imp, NEG)
        _, sel = lax.top_k(imp, k_sel)
        kg = ksb[bi, gi, sel]
        vg = vsb[bi, gi, sel]
        ss = jnp.einsum('bqgrd,bgqkld->bgrqkl', qr5, kg, preferred_element_type=f32) * scale
        tok = sel[..., None] * SLC_BLOCK + jnp.arange(SLC_BLOCK)
        mask_s = (tok <= t[None, None, :, None, None])[:, :, None]
        ss = jnp.where(mask_s, ss, NEG)
        p_s = jax.nn.softmax(ss.reshape(ss.shape[:4] + (k_sel * SLC_BLOCK,)), axis=-1).reshape(ss.shape)
        o_s = jnp.einsum('bgrqkl,bgqkld->bqgrd', p_s.astype(vg.dtype), vg, preferred_element_type=f32)
        kwin = lax.dynamic_slice_in_dim(kwp, s, WINDOW + Q_CHUNK, axis=1)
        vwin = lax.dynamic_slice_in_dim(vwp, s, WINDOW + Q_CHUNK, axis=1)
        j = s - WINDOW + jnp.arange(WINDOW + Q_CHUNK)
        mask_w = (j[None, :] <= t[:, None]) & (j[None, :] > t[:, None] - WINDOW) & (j[None, :] >= 0)
        sw = jnp.einsum('bqgrd,bjgd->bgrqj', qr5, kwin, preferred_element_type=f32) * scale
        p_w = jax.nn.softmax(jnp.where(mask_w, sw, NEG), axis=-1)
        o_w = jnp.einsum('bgrqj,bjgd->bqgrd', p_w.astype(vwin.dtype), vwin, preferred_element_type=f32)
        g = jax.nn.sigmoid(gt.astype(f32)).reshape(Bsz, Q_CHUNK, G, R, 3)
        o = g[..., 0:1] * o_c + g[..., 1:2] * o_s + g[..., 2:3] * o_w
        return o.reshape(Bsz, Q_CHUNK, NSA_HEADS * hd).astype(q.dtype)

    n_chunk = T // Q_CHUNK
    to_chunks = lambda a: a.reshape((Bsz, n_chunk, Q_CHUNK) + a.shape[2:]).swapaxes(0, 1)
    starts = jnp.arange(n_chunk) * Q_CHUNK
    out = lax.map(chunk, (to_chunks(q), to_chunks(q_rot), to_chunks(gate_logits), starts))
    return out.swapaxes(0, 1).reshape(Bsz, T, NSA_HEADS * hd)

def mixer_ab(h, w_in, conv_w, conv_b, w_r, b_r, w_i, b_i, lam, pe_k, pe_v, wk1, wk2, wv1, wv2, w_out):
    Bsz, T, _ = h.shape
    splits = np.cumsum(AB_SPLITS)[:-1].tolist()
    xr, gr, q, kc, vc, ks, vs, kw, vw, gl = jnp.split(h @ w_in, splits, axis=-1)
    y_rnn = rg_lru(causal_dwconv(xr, conv_w, conv_b), w_r, b_r, w_i, b_i, lam) * jax.nn.gelu(gr)
    kv = lambda a: a.reshape(Bsz, T, NSA_KV_HEADS, HEAD_DIM_2)
    y_att = nsa(q.reshape(Bsz, T, NSA_HEADS, HEAD_DIM_2), kv(kc), kv(vc), kv(ks), kv(vs), kv(kw), kv(vw),
                gl.reshape(Bsz, T, NSA_HEADS, 3), pe_k, pe_v, wk1, wk2, wv1, wv2)
    return jnp.concatenate([y_rnn, y_att], axis=-1) @ w_out

def mixer_c(h, w_in, conv_w, conv_b, w_out):
    bg, cg, v = jnp.split(h @ w_in, 3, axis=-1)
    return (bg * causal_dwconv(cg * v, conv_w, conv_b)) @ w_out

def conv_ffn(h, w_gate, w_up, conv_w, conv_b, w_down):
    g = causal_dwconv(h @ w_gate, conv_w, conv_b)
    return (jax.nn.silu(g) * (h @ w_up)) @ w_down

def second_inputs(seed: int = 0) -> dict:
    key = jax.random.key(seed)
    keys = iter(jax.random.split(key, 48))
    NE = (DEPTH_2 + 1) // 2
    NO = DEPTH_2 // 2
    f32 = jnp.float32

    def w(shape, fan_in, scale=1.0):
        return jax.random.normal(next(keys), shape, f32) * (scale * fan_in ** -0.5)

    def small(shape):
        return 0.02 * jax.random.normal(next(keys), shape, f32)

    def gain(shape):
        return 1.0 + small(shape)

    x = jax.random.normal(next(keys), (BATCH, SEQ, D_MODEL), f32)
    c = jax.random.normal(next(keys), (BATCH, D_MODEL), f32)
    a_target = jax.random.uniform(next(keys), (NE, RNN_WIDTH), f32, 0.9, 0.999)
    s = a_target ** (1.0 / LRU_C)
    lam = jnp.log(s) - jnp.log1p(-s)
    bw = RNN_WIDTH // RNN_BLOCKS
    return {
        'x': x,
        'c': c,
        'mod_w': w((DEPTH_2, D_MODEL, 6 * D_MODEL), D_MODEL, 0.5),
        'mod_b': small((DEPTH_2, 6 * D_MODEL)),
        'norm_mix_pre': gain((DEPTH_2, D_MODEL)),
        'norm_mix_post': gain((DEPTH_2, D_MODEL)),
        'norm_ffn_pre': gain((DEPTH_2, D_MODEL)),
        'norm_ffn_post': gain((DEPTH_2, D_MODEL)),
        'ab_w_in': w((NE, D_MODEL, AB_IN), D_MODEL),
        'ab_conv_w': w((NE, RNN_CONV, RNN_WIDTH), RNN_CONV),
        'ab_conv_b': small((NE, RNN_WIDTH)),
        'lru_w_r': w((NE, RNN_BLOCKS, bw, bw), bw),
        'lru_b_r': small((NE, RNN_WIDTH)),
        'lru_w_i': w((NE, RNN_BLOCKS, bw, bw), bw),
        'lru_b_i': small((NE, RNN_WIDTH)),
        'lru_lam': lam,
        'cmp_pe_k': small((NE, CMP_BLOCK, HEAD_DIM_2)),
        'cmp_pe_v': small((NE, CMP_BLOCK, HEAD_DIM_2)),
        'cmp_wk1': w((NE, CMP_BLOCK * HEAD_DIM_2, CMP_HIDDEN), CMP_BLOCK * HEAD_DIM_2),
        'cmp_wk2': w((NE, CMP_HIDDEN, HEAD_DIM_2), CMP_HIDDEN),
        'cmp_wv1': w((NE, CMP_BLOCK * HEAD_DIM_2, CMP_HIDDEN), CMP_BLOCK * HEAD_DIM_2),
        'cmp_wv2': w((NE, CMP_HIDDEN, HEAD_DIM_2), CMP_HIDDEN),
        'ab_w_out': w((NE, AB_MIX, D_MODEL), AB_MIX),
        'sc_w_in': w((NO, D_MODEL, 3 * SC_WIDTH), D_MODEL),
        'sc_conv_w': w((NO, SC_CONV, SC_WIDTH), SC_CONV),
        'sc_conv_b': small((NO, SC_WIDTH)),
        'sc_w_out': w((NO, SC_WIDTH, D_MODEL), SC_WIDTH),
        'ffn_w_gate': w((DEPTH_2, D_MODEL, D_FF), D_MODEL),
        'ffn_w_up': w((DEPTH_2, D_MODEL, D_FF), D_MODEL),
        'ffn_conv_w': w((DEPTH_2, FFN_CONV, D_FF), FFN_CONV),
        'ffn_conv_b': small((DEPTH_2, D_FF)),
        'ffn_w_down': w((DEPTH_2, D_FF, D_MODEL), D_FF),
    }

def second_block(x, c, mod_w, mod_b, norm_mix_pre, norm_mix_post, norm_ffn_pre, norm_ffn_post,
              ab_w_in, ab_conv_w, ab_conv_b, lru_w_r, lru_b_r, lru_w_i, lru_b_i, lru_lam,
              cmp_pe_k, cmp_pe_v, cmp_wk1, cmp_wk2, cmp_wv1, cmp_wv2, ab_w_out,
              sc_w_in, sc_conv_w, sc_conv_b, sc_w_out,
              ffn_w_gate, ffn_w_up, ffn_conv_w, ffn_conv_b, ffn_w_down):
    c_act = jax.nn.silu(c)
    for i in range(DEPTH_2):
        mod = c_act @ mod_w[i] + mod_b[i]
        sh_m, sc_m, g_m, sh_f, sc_f, g_f = jnp.split(mod[:, None, :], 6, axis=-1)
        h = rms_norm(x, norm_mix_pre[i]) * (1.0 + sc_m) + sh_m
        if i % 2 == 0:
            e = i // 2
            y = mixer_ab(h, ab_w_in[e], ab_conv_w[e], ab_conv_b[e], lru_w_r[e], lru_b_r[e],
                         lru_w_i[e], lru_b_i[e], lru_lam[e], cmp_pe_k[e], cmp_pe_v[e],
                         cmp_wk1[e], cmp_wk2[e], cmp_wv1[e], cmp_wv2[e], ab_w_out[e])
        else:
            o = i // 2
            y = mixer_c(h, sc_w_in[o], sc_conv_w[o], sc_conv_b[o], sc_w_out[o])
        x = x + (1.0 + g_m) * rms_norm(y, norm_mix_post[i])
        h = rms_norm(x, norm_ffn_pre[i]) * (1.0 + sc_f) + sh_f
        y = conv_ffn(h, ffn_w_gate[i], ffn_w_up[i], ffn_conv_w[i], ffn_conv_b[i], ffn_w_down[i])
        x = x + (1.0 + g_f) * rms_norm(y, norm_ffn_post[i])
    return x


def setup_inputs(seed=0):
    out = dict(first_inputs(seed))
    for name, value in second_inputs(seed + 1).items():
        if name != "x":
            out[name + "_2"] = value
    return out


def reference(
    x, mem, positions, mix_norm_w, w_in, gdn_conv_w, gdn_a_log, gdn_dt_bias, gdn_norm_w,
    gla_gk_up, gla_gk_bias, gla_norm_w, hgrn_lb_logits, hgrn_norm_w, w_out, xattn_norm_w,
    mem_norm_w, xattn_wq, xattn_wk, xattn_wv, xattn_wo, ffn_norm_w, ffn_up, ffn_conv_w,
    ffn_down, final_norm_w, c_2, mod_w_2, mod_b_2, norm_mix_pre_2, norm_mix_post_2,
    norm_ffn_pre_2, norm_ffn_post_2, ab_w_in_2, ab_conv_w_2, ab_conv_b_2, lru_w_r_2, lru_b_r_2,
    lru_w_i_2, lru_b_i_2, lru_lam_2, cmp_pe_k_2, cmp_pe_v_2, cmp_wk1_2, cmp_wk2_2, cmp_wv1_2,
    cmp_wv2_2, ab_w_out_2, sc_w_in_2, sc_conv_w_2, sc_conv_b_2, sc_w_out_2, ffn_w_gate_2,
    ffn_w_up_2, ffn_conv_w_2, ffn_conv_b_2, ffn_w_down_2,
):
    x = first_block(
        x, mem, positions, mix_norm_w, w_in, gdn_conv_w, gdn_a_log, gdn_dt_bias, gdn_norm_w,
        gla_gk_up, gla_gk_bias, gla_norm_w, hgrn_lb_logits, hgrn_norm_w, w_out, xattn_norm_w,
        mem_norm_w, xattn_wq, xattn_wk, xattn_wv, xattn_wo, ffn_norm_w, ffn_up, ffn_conv_w,
        ffn_down, final_norm_w,
    )
    return second_block(
        x, c_2, mod_w_2, mod_b_2, norm_mix_pre_2, norm_mix_post_2, norm_ffn_pre_2,
        norm_ffn_post_2, ab_w_in_2, ab_conv_w_2, ab_conv_b_2, lru_w_r_2, lru_b_r_2, lru_w_i_2,
        lru_b_i_2, lru_lam_2, cmp_pe_k_2, cmp_pe_v_2, cmp_wk1_2, cmp_wk2_2, cmp_wv1_2,
        cmp_wv2_2, ab_w_out_2, sc_w_in_2, sc_conv_w_2, sc_conv_b_2, sc_w_out_2, ffn_w_gate_2,
        ffn_w_up_2, ffn_conv_w_2, ffn_conv_b_2, ffn_w_down_2,
    )


_drawn_inputs = setup_inputs


def setup_inputs(seed=0):
    import zlib

    import numpy as np

    out = dict(_drawn_inputs(seed))
    spreads = {}
    factors = {'gdn_norm_w': 6.518,
     'gla_gk_bias': 8.0,
     'gla_norm_w': 6.05,
     'hgrn_norm_w': 5.979,
     'xattn_norm_w': 8.0,
     'mem_norm_w': 8.0,
     'norm_ffn_post_2': 3.081,
     'lru_b_r_2': 8.0,
     'lru_b_i_2': 7.516,
     'cmp_pe_k_2': 32.809,
     'cmp_pe_v_2': 8.0,
     'sc_conv_b_2': 6.023,
     'ffn_conv_b_2': 3.478,
     'ffn_norm_w': 8.0}
    for name, (base, spread) in spreads.items():
        noise = np.random.default_rng([zlib.crc32(name.encode()), seed]).standard_normal(out[name].shape)
        drawn = base * np.exp(spread * noise) if base else spread * noise
        out[name] = __import__('jax').numpy.asarray(drawn.astype(out[name].dtype))
    for name, factor in factors.items():
        out[name] = (out[name] * factor).astype(out[name].dtype)
    return out
```

```python
from contextlib import ExitStack

import numpy as np

import concourse.bass as bass
from concourse import mybir

ALU = mybir.AluOpType
ACT = mybir.ActivationFunctionType
F32 = mybir.dt.float32
U32 = mybir.dt.uint32
I32 = mybir.dt.int32
AX_X = mybir.AxisListType.X

P = 128
T = 512
D = 1024
KT = D // P
MEM = 256
TT = T // P
FF = 2816
FT = FF // P
HEADS = 4
HD = 64
NQ = 16
NG = 4
NCMP = 31
NBLK = 8
EPS = 1e-6
NEG = -1e30
TWO_PI = 2.0 * np.pi

RING = 8
SLOT_KT = 8
BANKS = 8
PRODUCT_BANKS = 4

PRODUCTS = {
    "mix_in": (31, 8), "mix_out": (8, 8),
    "mem_k": (8, 8), "mem_v": (8, 8),
    "att_q": (8, 8), "att_o": (8, 8),
    "up_0": (2 * FT, 8), "down_0": (8, FT),
    "ab_in": (37, 8), "ab_out": (8, 16),
    "up_1": (2 * FT, 8), "down_1": (8, FT),
    "sc_in": (24, 8), "sc_out": (8, 8),
    "up_2": (2 * FT, 8), "down_2": (8, FT),
}

RQ, RK, RV, BV, CV, DI, RG, BQ, BK, BG, CG, DQ, DF, DG = range(0, 28, 2)
CQ, CK, MISC = 28, 29, 30
XR, GR, NQT, KC, VC, KS, VS, KW, VW, GL = 0, 8, 16, 24, 26, 28, 30, 32, 34, 36


def packed(tables):
    tables = {k: np.ascontiguousarray(v, dtype=np.float32) for k, v in tables.items()}
    at, where = 0, {}
    for k, v in tables.items():
        where[k] = (at, at + v.shape[1])
        at += v.shape[1]
    return np.concatenate(list(tables.values()), axis=1), where


def constants():
    part = np.arange(P)
    tok = np.arange(T)
    c = both = {}
    c["ident"] = np.eye(P)
    c["ones"] = np.ones((P, P))
    c["head_ones"] = (part[:, None] // HD == part[None, :] // HD) * 1.0
    c = first = {}
    rot = np.zeros((P, P))
    for d in range(P):
        if d % HD < HD // 2:
            rot[d + HD // 2, d] = -1.0
        else:
            rot[d - HD // 2, d] = 1.0
    c["rotate_half"] = rot
    c["upto"] = (part[:, None] <= part[None, :]) * 1.0
    c["scan_keep"] = np.broadcast_to((tok % P != 0) * 1.0, (P, T))
    freqs = (np.float32(10000.0) ** (-np.arange(0, HD, 2, dtype=np.float32) / HD)).astype(np.float32)
    c["freq"] = freqs[part % (HD // 2)][:, None]
    log_gamma = np.log(1.0 - np.exp2(-5.0 - np.arange(HEADS)))
    rel = tok[None, :] - part[:, None]
    for h in range(HEADS):
        c[f"decay{h}"] = np.where(rel >= 0, np.exp(log_gamma[h] * np.maximum(rel, 0)), 0.0) * HD ** -0.5
    c = second = {}
    rot = np.zeros((P, P))
    for d in range(P):
        if d % HD < 8:
            rot[d + 8, d] = -1.0
        elif d % HD < 16:
            rot[d - 8, d] = 1.0
    c["rotate_part"] = rot
    inv = (np.float32(500000.0) ** (-np.arange(8, dtype=np.float32) / 8)).astype(np.float32)
    ang = (tok[None, :].astype(np.float32) * inv[part % 8][:, None]).astype(np.float32).astype(np.float64)
    turned = (part % HD < 16)[:, None]
    c["rope_cos"] = np.where(turned, np.cos(ang), 1.0)
    c["rope_sin"] = np.where(turned, np.sin(ang), 0.0)
    c["causal"] = np.where(part[None, :] <= part[:, None], 0.0, NEG)
    near = part[:, None] + 256 - np.arange(384)[None, :]
    c["window"] = np.where((near >= 0) & (near < 256), 0.0, NEG)
    for i in range(TT):
        t = i * P + part[:, None]
        n = np.arange(32)[None, :]
        seen = (16 * n + 31 <= t) & (n < NCMP)
        c[f"cmp_bias{i}"] = np.where(seen, 0.0, NEG)
        c[f"cmp_seen{i}"] = seen * 1.0
        j = np.arange(NBLK)[None, :]
        forced = (j == 0) | (j == t // HD)
        c[f"block_bias{i}"] = np.where(64 * j <= t, np.where(forced, 1.0e4, 0.0), NEG)
    j, i = np.meshgrid(np.arange(NBLK), np.arange(NBLK), indexing="ij")
    c["earlier"] = np.broadcast_to((i < j).reshape(1, 64) * 1.0, (P, 64))
    return packed(both), packed(first), packed(second)


def level_masks():
    s, t = np.arange(P)[:, None], np.arange(P)[None, :]
    out = [((s // (2 * b) == t // (2 * b)) & (s % (2 * b) < b) & (t % (2 * b) >= b)) for b in LEVELS]
    out.append(s == t)
    return np.stack(out, axis=1).astype(np.float32)


LEVELS = (1, 2, 4, 8, 16, 32, 64)

VECTORS = {
    "mix_norm": KT, "att_norm": KT, "mem_norm": KT, "ffn_norm": KT, "final_norm": KT,
    "gdn_conv": 4 * 6, "gdn_norm": 1, "gla_norm": 1, "hgrn_norm": 1, "gla_bias": 1,
    "a_log": HEADS, "dt_bias": HEADS, "ffn_conv_0": 3 * 2 * FT,
    "mix_pre_0": KT, "mix_post_0": KT, "ffn_pre_0": KT, "ffn_post_0": KT,
    "mix_pre_1": KT, "mix_post_1": KT, "ffn_pre_1": KT, "ffn_post_1": KT,
    "ab_conv": 4 * KT, "ab_conv_b": KT, "lru_b_r": KT, "lru_b_i": KT, "lru_lam": KT,
    "sc_conv": 3 * KT, "sc_conv_b": KT,
    "ffn_conv_1": 3 * FT, "ffn_conv_b_1": FT, "ffn_conv_2": 3 * FT, "ffn_conv_b_2": FT,
    "mod_b_0": 48, "mod_b_1": 48, "cond": KT, "pe_k": 16, "pe_v": 16,
}


class Link:

    def __init__(self, engine, semaphore):
        self.engine, self.semaphore, self.count = engine, semaphore, 0

    def __call__(self, instruction):
        self.count += 1
        instruction.then_inc(self.semaphore, 1)
        self.engine.wait_ge(self.semaphore, self.count)


class Kernel:

    def __init__(self, nc, ctx, dram):
        self.nc, self.ctx, self.dram = nc, ctx, dram
        self.psum = ctx.enter_context(nc.psum_tensor("psum", [P, BANKS, T], F32))
        self.ring = self.sb("ring", [P, RING, SLOT_KT, P])
        self.weights_landed = [ctx.enter_context(nc.semaphore(f"weights_landed{s}")) for s in range(RING)]
        self.weights_used = ctx.enter_context(nc.semaphore("weights_used"))
        self.stored = ctx.enter_context(nc.semaphore("stored"))
        self.stage_sems, self.in_use = ctx.enter_context(ExitStack()), []
        self.tiles, self.first_tile = [], {}
        for name, (n_out, kt) in PRODUCTS.items():
            self.first_tile[name] = len(self.tiles)
            for j in range(n_out):
                for k0 in range(0, kt, SLOT_KT):
                    self.tiles.append((name, j, k0, min(SLOT_KT, kt - k0)))

    def sem(self, name):
        self.in_use.append(self.stage_sems.enter_context(self.nc.semaphore(name)))
        return self.in_use[-1]

    def clear_stage_semaphores(self):
        nc, used = self.nc, self.in_use
        with nc.Block() as block:
            @block.gpsimd
            def _(pool):
                for semaphore in used:
                    pool.sem_clear(semaphore)
        self.stage_sems.close()
        self.in_use = []

    def sb(self, name, shape, dtype=F32, ctx=None):
        return (ctx or self.ctx).enter_context(self.nc.sbuf_tensor(name, shape, dtype))

    def const(self, name):
        for table, where in self.tables:
            if name in where:
                a, b = where[name]
                return table[:, a:b]

    def vec(self, name):
        a, b = self.vec_at[name]
        return self.vecs[:, a:b]

    def chunks(self, name):
        return -(-PRODUCTS[name][1] // SLOT_KT)

    def load_weights(self, sp, first, last):
        for i in range(first, min(last, len(self.tiles))):
            name, j, k0, n = self.tiles[i]
            if i >= RING:
                sp.wait_ge(self.weights_used, i - RING + 1)
            sp.dma_start(self.ring[:, i % RING, 0:n, :], self.dram["w_" + name][j, :, k0:k0 + n, :]
                         ).then_inc(self.weights_landed[i % RING], 16)

    def load_ahead(self, sp, name):
        first = self.first_tile[name]
        self.load_weights(sp, first + RING, first + PRODUCTS[name][0] * self.chunks(name) + RING)

    def product_done(self, name, j):
        return self.first_tile[name] + (j + 1) * self.chunks(name)

    def product(self, pe, name, rhs, width, evacuated, between=None):
        n_out, kt = PRODUCTS[name]
        i = self.first_tile[name]
        for j in range(n_out):
            if j >= PRODUCT_BANKS:
                pe.wait_ge(evacuated, j - PRODUCT_BANKS + 1)
            for k0 in range(0, kt, SLOT_KT):
                pe.wait_ge(self.weights_landed[i % RING], 16 * (i // RING + 1))
                n = min(SLOT_KT, kt - k0)
                for k in range(n):
                    last = self.nc.tensor.matmul(
                        self.psum[:, j % PRODUCT_BANKS, 0:width], self.ring[:, i % RING, k, :],
                        rhs(k0 + k), start=(k0 + k == 0), stop=(k0 + k == kt - 1))
                last.then_inc(self.weights_used, 1)
                i += 1
            if between is not None:
                between(j)


def rms_norm(k, name, src, gain, dst, width=T, shift=None, add_to=None):
    nc = k.nc
    squared, summed = k.sem(name + "_squared"), k.sem(name + "_summed")
    var_ready, root_ready = k.sem(name + "_var"), k.sem(name + "_root")
    steps, written = k.sem(name + "_steps"), k.sem(name + "_written")
    rstd = k.rstd[:, 0:width]
    total = k.psum[:, 0, 0:width]

    with nc.Block() as block:
        @block.scalar
        def _(act):
            for j in range(KT):
                if j >= 2:
                    act.wait_ge(summed, j - 1)
                nc.scalar.activation(k.squares[:, j % 2, 0:width], src[:, j, :], ACT.Square
                                     ).then_inc(squared, 1)
            act.wait_ge(var_ready, 1)
            nc.scalar.activation(rstd, rstd, ACT.Sqrt).then_inc(root_ready, 1)

        @block.tensor
        def _(pe):
            for j in range(KT):
                pe.wait_ge(squared, j + 1)
                nc.tensor.matmul(total, k.const("ones"), k.squares[:, j % 2, 0:width],
                                 start=(j == 0), stop=(j == KT - 1)).then_inc(summed, 1)

        @block.vector
        def _(dve):
            link = Link(dve, steps)
            dve.wait_ge(summed, KT)
            nc.vector.tensor_scalar(rstd, total, 1.0 / D, EPS, ALU.mult, ALU.add).then_inc(var_ready, 1)
            dve.wait_ge(root_ready, 1)
            link(nc.vector.reciprocal(rstd, rstd))
            for j in range(KT):
                nc.vector.scalar_tensor_tensor(dst[:, j, :], src[:, j, :], gain[:, j:j + 1], rstd,
                                               ALU.mult, ALU.mult).then_inc(written, 1)
            for j in range(KT):
                if shift is not None:
                    dve.wait_ge(written, j + 1)
                    nc.vector.tensor_scalar(dst[:, j, :], dst[:, j, :], shift[:, j:j + 1], None, ALU.add)
                if add_to is not None:
                    dve.wait_ge(written, j + 1)
                    nc.vector.tensor_tensor(add_to[:, j, :], add_to[:, j, :], dst[:, j, :], ALU.add)


def load_inputs(k):
    nc = k.nc
    loaded = k.sem("inputs_loaded")
    with nc.Block() as block:
        @block.scalar
        def _(act):
            act.dma_start(k.tables[0][0][:], k.dram["consts_0"]).then_inc(loaded, 16)
            act.dma_start(k.tables[1][0][:], k.dram["consts_1"]).then_inc(loaded, 16)
            act.dma_start(k.masks[:], k.dram["masks"]).then_inc(loaded, 16)
            act.dma_start(k.vecs[:], k.dram["vecs"]).then_inc(loaded, 16)

        @block.sync
        def _(sp):
            sp.dma_start(k.h[:], k.dram["x_t"]).then_inc(loaded, 16)
            k.load_weights(sp, 0, RING)
            sp.wait_ge(loaded, 5 * 16)


def load(k, name, pairs):
    nc = k.nc
    loaded = k.sem(name + "_loaded")
    with nc.Block() as block:
        @block.sync
        def _(sp):
            for dst, src in pairs:
                sp.dma_start(dst, k.dram[src]).then_inc(loaded, 16)
            sp.wait_ge(loaded, 16 * len(pairs))


def memory_projections(k):
    nc = k.nc
    for name, dst in (("mem_k", k.mem_k), ("mem_v", k.mem_vt)):
        out = k.sem(name + "_out")
        with nc.Block() as block:
            @block.sync
            def _(sp):
                k.load_ahead(sp, name)

            @block.tensor
            def _(pe):
                k.product(pe, name, lambda kk: k.mem_n[:, kk, :], MEM, out)

            @block.scalar
            def _(act):
                for j in range(KT):
                    act.wait_ge(k.weights_used, k.product_done(name, j))
                    nc.scalar.copy(dst[:, j, :], k.psum[:, j % PRODUCT_BANKS, 0:MEM]).then_inc(out, 1)

    turn(k, "mem_v_turn", [([k.mem_vt[:, 4 * g + i, m * P:(m + 1) * P] for i in range(4)],
                            k.mem_v[:, m, g * T:(g + 1) * T]) for m in range(2) for g in range(2)])


def turn(k, name, groups):
    nc = k.nc
    turned, kept = k.sem(name + "_turned"), k.sem(name + "_kept")
    with nc.Block() as block:
        @block.tensor
        def _(pe):
            for g, (pieces, _) in enumerate(groups):
                if g >= 4:
                    pe.wait_ge(kept, g - 3)
                for i, piece in enumerate(pieces):
                    last = nc.tensor.transpose(k.psum[:, g % 4, i * P:(i + 1) * P], piece, k.const("ident"))
                last.then_inc(turned, 1)

        @block.scalar
        def _(act):
            for g, (pieces, dst) in enumerate(groups):
                act.wait_ge(turned, g + 1)
                nc.scalar.copy(dst, k.psum[:, g % 4, 0:len(pieces) * P]).then_inc(kept, 1)


def head_norm(k, name, items, mean):
    nc = k.nc
    squared, summed = k.sem(name + "_squared"), k.sem(name + "_summed")
    var_ready, root_ready, steps = k.sem(name + "_var"), k.sem(name + "_root"), k.sem(name + "_steps")
    with nc.Block() as block:
        @block.scalar
        def _(act):
            for i, (src, _, _, _) in enumerate(items):
                nc.scalar.activation(k.head_sq[:, i, :], src, ACT.Square).then_inc(squared, 1)
            for i in range(len(items)):
                act.wait_ge(var_ready, i + 1)
                nc.scalar.activation(k.head_sq[:, i, :], k.head_sq[:, i, :], ACT.Sqrt).then_inc(root_ready, 1)

        @block.tensor
        def _(pe):
            for i in range(len(items)):
                pe.wait_ge(squared, i + 1)
                nc.tensor.matmul(k.psum[:, i, :], k.const("head_ones"), k.head_sq[:, i, :],
                                 start=True, stop=True).then_inc(summed, 1)

        @block.vector
        def _(dve):
            link = Link(dve, steps)
            for i in range(len(items)):
                dve.wait_ge(summed, i + 1)
                nc.vector.tensor_scalar(k.head_sq[:, i, :], k.psum[:, i, :], mean, EPS,
                                        ALU.mult, ALU.add).then_inc(var_ready, 1)
            for i, (src, dst, scale, gate) in enumerate(items):
                dve.wait_ge(root_ready, i + 1)
                link(nc.vector.reciprocal(k.head_sq[:, i, :], k.head_sq[:, i, :]))
                if gate is not None:
                    link(nc.vector.tensor_tensor(k.head_sq[:, i, :], k.head_sq[:, i, :], gate, ALU.mult))
                link(nc.vector.scalar_tensor_tensor(dst, src, scale, k.head_sq[:, i, :], ALU.mult, ALU.mult))


def mixer_projection(k):
    nc = k.nc
    out, padded, steps, convolved = (k.sem("mix_in_out"), k.sem("mix_in_padded"), k.sem("mix_in_steps"),
                                     k.sem("mix_in_convolved"))
    conv_tiles = [BQ, BQ + 1, BK, BK + 1, BV, BV + 1]
    gates = [t + i for t in (RG, BG, CG, DG) for i in range(2)]
    with nc.Block() as block:
        @block.sync
        def _(sp):
            k.load_ahead(sp, "mix_in")

        @block.tensor
        def _(pe):
            k.product(pe, "mix_in", lambda kk: k.n[:, kk, :], T, out)

        @block.scalar
        def _(act):
            act.wait_ge(padded, 1)
            for j in range(PRODUCTS["mix_in"][0]):
                act.wait_ge(k.weights_used, k.product_done("mix_in", j))
                bank = k.psum[:, j % PRODUCT_BANKS, :]
                if j in conv_tiles:
                    nc.scalar.copy(k.conv_in[:, conv_tiles.index(j), 3:3 + T], bank).then_inc(out, 1)
                elif j in gates:
                    nc.scalar.activation(k.z[:, j, :], bank, ACT.Silu).then_inc(out, 1)
                elif j == CQ:
                    nc.scalar.mul(k.z[:, j, :], bank, (HD // 2) ** -0.5).then_inc(out, 1)
                else:
                    nc.scalar.copy(k.z[:, j, :], bank).then_inc(out, 1)
            for i, j in enumerate(conv_tiles):
                act.wait_ge(convolved, i + 1)
                nc.scalar.activation(k.z[:, j, :], k.z[:, j, :], ACT.Silu)

        @block.vector
        def _(dve):
            link = Link(dve, steps)
            nc.vector.memset(k.conv_in[:, :, 0:3], 0.0).then_inc(padded, 1)
            w = k.vec("gdn_conv")
            for i, j in enumerate(conv_tiles):
                dve.wait_ge(out, j + 1)
                link(nc.vector.tensor_scalar(k.z[:, j, :], k.conv_in[:, i, 0:T], w[:, i:i + 1], None, ALU.mult))
                for tap in range(1, 4):
                    step = nc.vector.scalar_tensor_tensor(
                        k.z[:, j, :], k.conv_in[:, i, tap:tap + T], w[:, 6 * tap + i:6 * tap + i + 1],
                        k.z[:, j, :], ALU.mult, ALU.add)
                    if tap < 3:
                        link(step)
                step.then_inc(convolved, 1)


def rotary(k):
    nc = k.nc
    C1 = 6.28125
    C2 = float(np.frombuffer((np.frombuffer(np.float32(TWO_PI - C1).tobytes(), np.uint32)
                              & np.uint32(0xFFFFF000)).tobytes(), np.float32)[0])
    C3 = float(TWO_PI - C1 - C2)
    ROUND = 1.5 * 2.0 ** 23
    steps, reduced, tables, turned = (k.sem("rotary_steps"), k.sem("rotary_reduced"), k.sem("rotary_tables"),
                                      k.sem("rotary_turned"))
    asteps = k.sem("rotary_asteps")
    ang, n, cos, sin, tmp = (k.scratch[:, i, :] for i in range(5))
    tiles = (RQ, RQ + 1, RK, RK + 1)
    with nc.Block() as block:
        @block.tensor
        def _(pe):
            for i, j in enumerate(tiles):
                nc.tensor.matmul(k.psum[:, i, :], k.const("rotate_half"), k.z[:, j, :],
                                 start=True, stop=True).then_inc(turned, 1)

        @block.scalar
        def _(act):
            link = Link(act, asteps)
            act.wait_ge(reduced, 1)
            nc.scalar.activation(sin, ang, ACT.Sin).then_inc(tables, 1)
            link(nc.scalar.activation(cos, ang, ACT.Abs))
            nc.scalar.activation(cos, cos, ACT.Sin, bias=k.half_pi[:, 0:1], scale=-1.0).then_inc(tables, 1)

        @block.vector
        def _(dve):
            link = Link(dve, steps)
            link(nc.vector.memset(k.half_pi[:], float(np.pi / 2)))
            link(nc.vector.tensor_copy(ang, k.positions[:]))
            link(nc.vector.tensor_scalar(ang, ang, k.const("freq"), None, ALU.mult))
            link(nc.vector.tensor_scalar(n, ang, 1.0 / TWO_PI, ROUND, ALU.mult, ALU.add))
            link(nc.vector.tensor_scalar(n, n, ROUND, None, ALU.subtract))
            for c in (C1, C2, C3):
                link(nc.vector.scalar_tensor_tensor(ang, n, -c, ang, ALU.mult, ALU.add))
            nc.vector.tensor_scalar(ang, ang, 3.141592, -3.141592, ALU.min, ALU.max).then_inc(reduced, 1)
            dve.wait_ge(tables, 2)
            for i, j in enumerate(tiles):
                dve.wait_ge(turned, i + 1)
                link(nc.vector.tensor_tensor(tmp, k.psum[:, i, :], sin, ALU.mult))
                link(nc.vector.tensor_tensor(k.z[:, j, :], k.z[:, j, :], cos, ALU.mult))
                link(nc.vector.tensor_tensor(k.z[:, j, :], k.z[:, j, :], tmp, ALU.add))


def head_rows(h):
    return slice(HD * (h % 2), HD * (h % 2) + HD)


def retention(k):
    nc = k.nc
    scored, weighted, mixed = k.sem("ret_scored"), k.sem("ret_weighted"), k.sem("ret_mixed")
    work = [(h, j) for h in range(HEADS) for j in range(TT)]
    with nc.Block() as block:
        @block.tensor
        def _(pe):
            def scores(i):
                h, j = work[i]
                rows = head_rows(h)
                if i >= 4:
                    pe.wait_ge(weighted, i - 3)
                nc.tensor.matmul(k.psum[:, i % 4, 0:T - j * P], k.z[rows, RK + h // 2, j * P:(j + 1) * P],
                                 k.z[rows, RQ + h // 2, j * P:T], start=True, stop=True).then_inc(scored, 1)

            scores(0)
            scores(1)
            for i, (h, j) in enumerate(work):
                if i + 2 < len(work):
                    scores(i + 2)
                pe.wait_ge(weighted, i + 1)
                nc.tensor.matmul(k.psum[head_rows(h), 4 + h // 2, j * P:T],
                                 k.v_tok[:, 0, j, h * HD:(h + 1) * HD], k.scratch[:, i % 4, 0:T - j * P],
                                 start=(j == 0), stop=(j == TT - 1)).then_inc(mixed, 1)

        @block.vector
        def _(dve):
            for i, (h, j) in enumerate(work):
                dve.wait_ge(scored, i + 1)
                if i >= 4:
                    dve.wait_ge(mixed, i - 3)
                nc.vector.tensor_tensor(k.scratch[:, i % 4, 0:T - j * P], k.psum[:, i % 4, 0:T - j * P],
                                        k.const(f"decay{h}")[:, 0:T - j * P], ALU.mult).then_inc(weighted, 1)

        @block.scalar
        def _(act):
            for m in range(2):
                act.wait_ge(mixed, 2 * TT * (m + 1))
                nc.scalar.copy(k.o[:, m, :], k.psum[:, 4 + m, :])


def log_decays(k):
    nc = k.nc
    up, x_ready, logs, negs, steps, asteps, cum = (
        k.sem("dec_up"), k.sem("dec_x"), k.sem("dec_logs"), k.sem("dec_negs"), k.sem("dec_steps"),
        k.sem("dec_asteps"), k.sem("dec_cum"))
    tmp = [k.scratch[:, i, :] for i in range(3)]
    low = [k.scratch[:, 3 + i, :] for i in range(3)]
    src = [low[0], k.z[:, DF, :], k.z[:, DF + 1, :]]
    with nc.Block() as block:
        @block.tensor
        def _(pe):
            nc.tensor.matmul(k.psum[:, 0, :], k.gla_up[64:96, :], k.z[64:96, MISC, :],
                             start=True, stop=True).then_inc(up, 1)

        @block.scalar
        def _(act):
            link = Link(act, asteps)
            act.wait_ge(x_ready, 1)
            for i in range(3):
                link(nc.scalar.activation(tmp[i], src[i], ACT.Abs))
            for i in range(3):
                link(nc.scalar.activation(tmp[i], tmp[i], ACT.Exp, scale=-1.0))
            for i in range(3):
                nc.scalar.activation(tmp[i], tmp[i], ACT.Ln, bias=1.0).then_inc(logs, 1)
            act.wait_ge(negs, 3)
            for i in (1, 2):
                nc.scalar.activation(k.z[:, DF + i - 1, :], src[i], ACT.Sigmoid, scale=-1.0)

        @block.vector
        def _(dve):
            link = Link(dve, steps)
            dve.wait_ge(up, 1)
            nc.vector.tensor_scalar(low[0], k.psum[:, 0, :], k.vec("gla_bias"), None, ALU.add).then_inc(x_ready, 1)
            dve.wait_ge(x_ready, 1)
            for i in range(3):
                dve.wait_ge(logs, i + 1)
                nc.vector.scalar_tensor_tensor(low[i], src[i], 0.0, tmp[i], ALU.min, ALU.subtract
                                               ).then_inc(negs, 1)
            dve.wait_ge(negs, 3)
            link(nc.vector.tensor_scalar(low[0], low[0], 1.0 / 16.0, None, ALU.mult))
            for i in range(3):
                nc.vector.tensor_tensor_scan(k.cum[:, i, :], k.const("scan_keep"), low[i], 0.0,
                                             ALU.mult, ALU.add).then_inc(cum, 1)


def gated_scores(k, name, cum, q, key, width, probs):
    nc = k.nc
    heads = P // width
    nl = len(LEVELS) + 1
    diffed, decayed, qs_ready, ks_ready, scored, picked, steps, asteps, zeroed = (
        k.sem(f"{name}_{s}") for s in ("diffed", "decayed", "qs", "ks", "scored", "picked", "steps",
                                       "asteps", "zeroed"))
    e = [k.scratch[:, i, :] for i in range(2)]
    qs = [k.scratch[:, 2 + i, :] for i in range(2)]
    ks = [k.scratch[:, 4 + i, :] for i in range(2)]

    def diagonal(h):
        return probs[h].rearrange("p (c x) -> p c x", x=T + P)[:, :, 0:P]

    with nc.Block() as block:
        @block.vector
        def _(dve):
            def difference(n):
                if n >= 2:
                    dve.wait_ge(qs_ready, n - 1)
                    dve.wait_ge(ks_ready, n - 1)
                b = LEVELS[n]
                g = cum.rearrange("p (c x) -> p c x", x=2 * b)
                nc.vector.tensor_tensor(e[n % 2].rearrange("p (c x) -> p c x", x=2 * b), g,
                                        g[:, :, b - 1:b].broadcast_to([P, T // (2 * b), 2 * b]),
                                        ALU.subtract).then_inc(diffed, 1)

            difference(0)
            for n in range(nl):
                if n < nl - 1:
                    if n < nl - 2:
                        difference(n + 1)
                    dve.wait_ge(decayed, n + 1)
                    if n >= 2:
                        dve.wait_ge(scored, heads * (n - 1))
                    nc.vector.tensor_tensor(qs[n % 2], q, e[n % 2], ALU.mult).then_inc(qs_ready, 1)
                if n == 0:
                    dve.wait_ge(zeroed, heads)
                for h in range(heads):
                    dve.wait_ge(scored, heads * n + h + 1)
                    if n:
                        dve.wait_ge(picked, heads * (n - 1) + h + 1)
                    nc.vector.copy_predicated(
                        diagonal(h), k.masks[:, n:n + 1, :].bitcast(U32).broadcast_to([P, TT, P]),
                        k.psum[:, (n % 2) * heads + h, :].rearrange("p (c x) -> p c x", x=P)).then_inc(picked, 1)

        @block.scalar
        def _(act):
            link = Link(act, asteps)
            for n in range(nl - 1):
                act.wait_ge(diffed, n + 1)
                link(nc.scalar.activation(e[n % 2], e[n % 2], ACT.Abs))
                nc.scalar.activation(e[n % 2], e[n % 2], ACT.Exp, scale=-1.0).then_inc(decayed, 1)

        @block.gpsimd
        def _(pool):
            for h in range(heads):
                nc.gpsimd.memset(probs[h], 0.0).then_inc(zeroed, 1)
            for n in range(nl - 1):
                pool.wait_ge(decayed, n + 1)
                if n >= 2:
                    pool.wait_ge(scored, heads * (n - 1))
                nc.gpsimd.tensor_tensor(ks[n % 2], key, e[n % 2], ALU.mult).then_inc(ks_ready, 1)

        @block.tensor
        def _(pe):
            for n in range(nl):
                if n < nl - 1:
                    pe.wait_ge(qs_ready, n + 1)
                    pe.wait_ge(ks_ready, n + 1)
                    a, b = ks[n % 2], qs[n % 2]
                else:
                    a, b = key, q
                for h in range(heads):
                    if n >= 2:
                        pe.wait_ge(picked, heads * (n - 2) + h + 1)
                    rows = slice(width * h, width * (h + 1))
                    for c in range(TT):
                        last = nc.tensor.matmul(k.psum[:, (n % 2) * heads + h, c * P:(c + 1) * P],
                                                a[rows, c * P:(c + 1) * P], b[rows, c * P:(c + 1) * P],
                                                start=True, stop=True)
                    last.then_inc(scored, 1)

    fwd, bwd, qg, kg, q_late = (k.scratch[:, i, :] for i in range(5))
    k_early = k.scratch[:, 5, 0:P]
    ends, factors, grown, crossed, kept = (k.sem(f"{name}_{s}") for s in
                                           ("ends", "factors", "grown", "crossed", "kept"))
    with nc.Block() as block:
        @block.vector
        def _(dve):
            g = cum.rearrange("p (c x) -> p c x", x=P)
            nc.vector.tensor_tensor(bwd.rearrange("p (c x) -> p c x", x=P),
                                    g[:, :, P - 1:P].broadcast_to([P, TT, P]), g, ALU.subtract
                                    ).then_inc(ends, 1)
            dve.wait_ge(factors, 2)
            nc.vector.tensor_tensor(qg, q, fwd, ALU.mult).then_inc(grown, 1)
            nc.vector.tensor_tensor(kg, key, bwd, ALU.mult).then_inc(grown, 1)
            dve.wait_ge(grown, 2)
            nc.vector.tensor_copy(q_late[:, 0:P], qg[:, 2 * P:3 * P]).then_inc(grown, 1)
            nc.vector.tensor_scalar(q_late[:, P:2 * P], qg[:, 3 * P:T], fwd[:, 3 * P - 1:3 * P], None,
                                    ALU.mult).then_inc(grown, 1)
            nc.vector.tensor_scalar(k_early, kg[:, 0:P], fwd[:, 2 * P - 1:2 * P], None,
                                    ALU.mult).then_inc(grown, 1)

        @block.scalar
        def _(act):
            nc.scalar.activation(fwd, cum, ACT.Exp).then_inc(factors, 1)
            act.wait_ge(ends, 1)
            nc.scalar.activation(bwd, bwd, ACT.Exp).then_inc(factors, 1)
            for h in range(heads):
                act.wait_ge(crossed, h + 1)
                a, b = k.psum[:, (2 * h) % 8, :], k.psum[:, (2 * h + 1) % 8, :]
                nc.scalar.copy(probs[h][:, P:2 * P], a[:, 0:P])
                nc.scalar.copy(probs[h][:, 2 * T + 3 * P:3 * T], a[:, P:2 * P])
                nc.scalar.copy(probs[h][:, 2 * P:T], a[:, 2 * P:T])
                nc.scalar.copy(probs[h][:, T + 2 * P:2 * T], b[:, 0:2 * P]).then_inc(kept, 1)

        @block.tensor
        def _(pe):
            pe.wait_ge(grown, 5)
            for h in range(heads):
                rows = slice(width * h, width * (h + 1))
                a, b = k.psum[:, 2 * h, :], k.psum[:, 2 * h + 1, :]
                nc.tensor.matmul(a[:, 0:P], kg[rows, 0:P], qg[rows, P:2 * P], start=True, stop=True)
                nc.tensor.matmul(a[:, P:2 * P], kg[rows, 2 * P:3 * P], qg[rows, 3 * P:T], start=True, stop=True)
                nc.tensor.matmul(a[:, 2 * P:T], k_early[rows, :], q_late[rows, 0:2 * P], start=True, stop=True)
                nc.tensor.matmul(b[:, 0:2 * P], kg[rows, P:2 * P], q_late[rows, 0:2 * P],
                                 start=True, stop=True).then_inc(crossed, 1)


def mix_values(k, name, mixer, probs):
    nc = k.nc
    mixed = k.sem(name + "_mixed")
    with nc.Block() as block:
        @block.tensor
        def _(pe):
            for h in range(HEADS):
                for j in range(TT):
                    last = nc.tensor.matmul(k.psum[head_rows(h), h // 2, j * P:T],
                                            k.v_tok[:, mixer, j, h * HD:(h + 1) * HD],
                                            probs[h][:, j * (T + P):(j + 1) * T],
                                            start=(j == 0), stop=(j == TT - 1))
                last.then_inc(mixed, 1)

        @block.scalar
        def _(act):
            for m in range(2):
                act.wait_ge(mixed, 2 * (m + 1))
                nc.scalar.copy(k.o[:, 2 * mixer + m, :], k.psum[:, m, :])


def delta_prepare(k):
    nc = k.nc
    aready, steps, asteps, gs, spread = (k.sem("dp_" + s) for s in ("a", "steps", "asteps", "g", "spread"))
    done = k.sem("dp_done")
    tok = k.misc_tok
    x, ex, pos = (k.small[:, i, :].rearrange("p (c h) -> p c h", h=HEADS) for i in range(3))
    g_tok = k.g_tok.rearrange("p (c h) -> p c h", h=HEADS)
    with nc.Block() as block:
        @block.vector
        def _(dve):
            link = Link(dve, steps)
            link(nc.vector.tensor_tensor(x, tok[:, :, 0:HEADS],
                                         k.vec("dt_bias").unsqueeze(1).broadcast_to([P, TT, HEADS]), ALU.add))
            nc.vector.tensor_scalar(pos, x, 0.0, None, ALU.max).then_inc(aready, 1)
            dve.wait_ge(asteps, 5)
            link(nc.vector.tensor_tensor(pos, pos, ex, ALU.add))
            link(nc.vector.tensor_tensor(pos, pos, k.small[:, 3, 0:HEADS].unsqueeze(1)
                                         .broadcast_to([P, TT, HEADS]), ALU.mult))
            nc.vector.tensor_scalar(g_tok, pos, -1.0, None, ALU.mult).then_inc(gs, 1)

        @block.scalar
        def _(act):
            link = Link(act, asteps)
            link(nc.scalar.activation(k.small[:, 3, 0:HEADS], k.vec("a_log"), ACT.Exp))
            act.wait_ge(aready, 1)
            link(nc.scalar.activation(ex, x, ACT.Abs))
            link(nc.scalar.activation(ex, ex, ACT.Exp, scale=-1.0))
            link(nc.scalar.activation(ex, ex, ACT.Ln, bias=1.0))
            link(nc.scalar.activation(k.beta.rearrange("p (c h) -> p c h", h=HEADS), tok[:, :, 32:32 + HEADS],
                                      ACT.Sigmoid))
            act.wait_ge(spread, 5)
            link(nc.scalar.copy(k.gc_tok[:], k.psum[:, 7, 0:16]))
            link(nc.scalar.activation(k.gamma_tok[:], k.psum[:, 7, 0:16], ACT.Exp))
            for h in range(HEADS):
                nc.scalar.activation(k.gamma[:, h, :], k.psum[:, h, :], ACT.Exp).then_inc(done, 1)

        @block.tensor
        def _(pe):
            pe.wait_ge(gs, 1)
            nc.tensor.matmul(k.psum[:, 7, 0:16], k.const("upto"), k.g_tok[:], start=True, stop=True
                             ).then_inc(spread, 1)
            for h in range(HEADS):
                for c in range(TT):
                    col = k.g_tok[:, c * HEADS + h:c * HEADS + h + 1]
                    last = nc.tensor.matmul(k.psum[:, h, c * P:(c + 1) * P], col.broadcast_to([P, P]),
                                            k.const("upto"), start=True, stop=True)
                last.then_inc(spread, 1)

    limited, risen, masked, dsteps = (k.sem("dr_" + s) for s in ("limited", "risen", "masked", "steps"))
    with nc.Block() as block:
        @block.vector
        def _(dve):
            link = Link(dve, dsteps)
            for h in range(HEADS):
                for c in range(TT):
                    i = c * HEADS + h
                    nc.vector.tensor_scalar(k.ratio[:, h, c * P:(c + 1) * P], k.psum[:, h, c * P:(c + 1) * P],
                                            k.gc_tok[:, i:i + 1], 0.0, ALU.subtract, ALU.min).then_inc(limited, 1)
            for h in range(HEADS):
                last = nc.vector.tensor_tensor(
                    k.tail.rearrange("p (c h) -> p c h", h=HEADS)[:, :, h:h + 1],
                    k.psum[:, h, :].rearrange("p (c x) -> p c x", x=P)[:, :, P - 1:P],
                    k.gc_tok.rearrange("p (c h) -> p c h", h=HEADS)[:, :, h:h + 1], ALU.subtract)
                last.then_inc(limited, 1)
            for h in range(HEADS):
                dve.wait_ge(risen, h + 2)
                tri = k.const("upto").unsqueeze(1).broadcast_to([P, TT, P])
                r = k.ratio[:, h, :].rearrange("p (c x) -> p c x", x=P)
                nc.vector.tensor_tensor(r, r, tri, ALU.mult).then_inc(masked, 1)
            kt = k.k_tok.rearrange("p c (h d) -> p (c h) d", d=HD)
            nc.vector.tensor_tensor(kt, kt, k.tail.unsqueeze(2).broadcast_to([P, 16, HD]), ALU.mult
                                    ).then_inc(masked, 1)
            for h in range(HEADS):
                rows = head_rows(h)
                nc.vector.tensor_tensor(k.qg[rows, h // 2, :], k.z[rows, BQ + h // 2, :], k.gamma[rows, h, :],
                                        ALU.mult).then_inc(masked, 1)
                nc.vector.tensor_copy(
                    k.whole[rows, h // 2, :].unsqueeze(2),
                    k.gamma[rows, h, :].rearrange("p (c x) -> p c x", x=P)[:, :, P - 1:P]).then_inc(masked, 1)

        @block.scalar
        def _(act):
            act.wait_ge(limited, 20)
            nc.scalar.activation(k.tail[:], k.tail[:], ACT.Exp).then_inc(risen, 1)
            for h in range(HEADS):
                nc.scalar.activation(k.ratio[:, h, :], k.ratio[:, h, :], ACT.Exp).then_inc(risen, 1)


def delta_inverse(k):
    nc = k.nc
    scored, weighted, beta_done = k.sem("di_scored"), k.sem("di_weighted"), k.sem("di_beta")
    with nc.Block() as block:
        @block.tensor
        def _(pe):
            for kind in range(2):
                for h in range(HEADS):
                    rows, tile = head_rows(h), h // 2
                    for c in range(TT):
                        cols = slice(c * P, (c + 1) * P)
                        last = nc.tensor.matmul(k.psum[:, kind * 4 + h, cols], k.z[rows, BK + tile, cols],
                                                k.z[rows, (BK if kind == 0 else BQ) + tile, cols],
                                                start=True, stop=True)
                    last.then_inc(scored, 1)

        @block.vector
        def _(dve):
            for h in range(HEADS):
                dve.wait_ge(scored, h + 1)
                nc.vector.tensor_tensor(k.nt[:, h, :], k.psum[:, h, :], k.ratio[:, h, :], ALU.mult
                                        ).then_inc(weighted, 1)
            for h in range(HEADS):
                dve.wait_ge(scored, HEADS + h + 1)
                dve.wait_ge(beta_done, h + 1)
                nc.vector.tensor_tensor(k.ratio[:, h, :], k.psum[:, 4 + h, :], k.ratio[:, h, :], ALU.mult
                                        ).then_inc(weighted, 1)

        @block.scalar
        def _(act):
            for h in range(HEADS):
                act.wait_ge(weighted, h + 1)
                for c in range(TT):
                    i = c * HEADS + h
                    cols = slice(c * P, (c + 1) * P)
                    last = nc.scalar.activation(k.nt[:, h, cols], k.nt[:, h, cols], ACT.Copy,
                                                scale=k.beta[:, i:i + 1])
                last.then_inc(beta_done, 1)

    picked, q_ready, q_kept, xs, x_new, xt_new, started = (
        k.sem("dx_" + s) for s in ("picked", "q", "q_kept", "xs", "x_new", "xt_new", "started"))

    def blocks(a):
        return a.rearrange("p (c x) -> p c x", x=P)

    with nc.Block() as block:
        @block.gpsimd
        def _(pool):
            for n in range(len(LEVELS)):
                for h in range(HEADS):
                    i = n * HEADS + h
                    if i >= 4:
                        pool.wait_ge(q_ready, i - 3)
                    nc.gpsimd.tensor_tensor(blocks(k.nb[:, h, :]), blocks(k.nt[:, h, :]),
                                            k.masks[:, n:n + 1, :].broadcast_to([P, TT, P]), ALU.mult
                                            ).then_inc(picked, 1)

        @block.tensor
        def _(pe):
            for n in range(len(LEVELS)):
                for h in range(HEADS):
                    i = n * HEADS + h
                    pe.wait_ge(picked, i + 1)
                    if n == 0:
                        pe.wait_ge(started, 1)
                    else:
                        pe.wait_ge(x_new, i - 3)
                    for c in range(TT):
                        cols = slice(c * P, (c + 1) * P)
                        last = nc.tensor.matmul(k.psum[:, h, cols], k.nb[:, h, cols], k.inv_n[:, h, cols],
                                                start=True, stop=True)
                    last.then_inc(q_ready, 1)
                for h in range(HEADS):
                    i = n * HEADS + h
                    pe.wait_ge(q_kept, i + 1)
                    if i >= 1:
                        pe.wait_ge(x_new, i)
                        pe.wait_ge(xt_new, i)
                    for c in range(TT):
                        cols = slice(c * P, (c + 1) * P)
                        nc.tensor.matmul(k.psum[:, 4 + h % 2, cols], k.inv_t[:, h, cols], k.q_sb[:, h % 2, cols],
                                         start=True, stop=True)
                    for c in range(TT):
                        cols = slice(c * P, (c + 1) * P)
                        last = nc.tensor.matmul(k.psum[:, 6 + h % 2, cols], k.q_sb[:, h % 2, cols],
                                                k.inv_t[:, h, cols], start=True, stop=True)
                    last.then_inc(xs, 1)

        @block.scalar
        def _(act):
            for n in range(len(LEVELS)):
                for h in range(HEADS):
                    i = n * HEADS + h
                    act.wait_ge(q_ready, i + 1)
                    if i >= 2:
                        act.wait_ge(xs, i - 1)
                    nc.scalar.copy(k.q_sb[:, h % 2, :], k.psum[:, h, :]).then_inc(q_kept, 1)

        @block.vector
        def _(dve):
            eye = k.const("ident").unsqueeze(1).broadcast_to([P, TT, P])
            for h in range(HEADS):
                nc.vector.tensor_copy(blocks(k.inv_n[:, h, :]), eye)
                last = nc.vector.tensor_copy(blocks(k.inv_t[:, h, :]), eye)
            last.then_inc(started, 1)
            dve.wait_ge(started, 1)
            for n in range(len(LEVELS)):
                for h in range(HEADS):
                    i = n * HEADS + h
                    dve.wait_ge(xs, i + 1)
                    if i >= 4:
                        dve.wait_ge(x_new, i - 3)
                        dve.wait_ge(xt_new, i - 3)
                    nc.vector.tensor_tensor(k.inv_n[:, h, :], k.inv_n[:, h, :], k.psum[:, 4 + h % 2, :],
                                            ALU.subtract).then_inc(x_new, 1)
                    nc.vector.tensor_tensor(k.inv_t[:, h, :], k.inv_t[:, h, :], k.psum[:, 6 + h % 2, :],
                                            ALU.subtract).then_inc(xt_new, 1)


def delta_scan(k):
    nc = k.nc
    ks, r_ready, solved, u_ready, out, grown, s_ready, steps = (
        k.sem("ds_" + s) for s in ("ks", "r", "solved", "u", "out", "grown", "s", "steps"))
    r = k.scratch[:, 0, 0:256]
    u = k.scratch[:, 1, 0:256]
    with nc.Block() as block:
        @block.tensor
        def _(pe):
            for c in range(TT):
                cols = slice(c * P, (c + 1) * P)
                pe.wait_ge(s_ready, c + 1)
                if c >= 1:
                    for h in range(HEADS):
                        last = nc.tensor.matmul(k.psum[:, h % 2, (h // 2) * HD:(h // 2 + 1) * HD],
                                                k.z[head_rows(h), BK + h // 2, cols],
                                                k.state[head_rows(h), h // 2, :], start=True, stop=True)
                    last.then_inc(ks, 1)
                pe.wait_ge(r_ready, c + 1)
                for h in range(HEADS):
                    last = nc.tensor.matmul(k.psum[:, 7, h * HD:(h + 1) * HD], k.inv_t[:, h, cols],
                                            r[:, h * HD:(h + 1) * HD], start=True, stop=True)
                last.then_inc(solved, 1)
                pe.wait_ge(u_ready, c + 1)
                if c < TT - 1:
                    for h in range(HEADS):
                        last = nc.tensor.matmul(k.psum[head_rows(h), 2 + h // 2, 0:HD],
                                                k.k_tok[:, c, h * HD:(h + 1) * HD], u[:, h * HD:(h + 1) * HD],
                                                start=True, stop=True)
                    last.then_inc(grown, 1)
                for h in range(HEADS):
                    if c >= 1:
                        nc.tensor.matmul(k.psum[head_rows(h), 4 + h // 2, cols], k.state[head_rows(h), h // 2, :],
                                         k.qg[head_rows(h), h // 2, cols], start=True, stop=False)
                    last = nc.tensor.matmul(k.psum[head_rows(h), 4 + h // 2, cols], u[:, h * HD:(h + 1) * HD],
                                            k.ratio[:, h, cols], start=(c == 0), stop=True)
                last.then_inc(out, 1)

        @block.vector
        def _(dve):
            link = Link(dve, steps)
            nc.vector.memset(k.state[:], 0.0).then_inc(s_ready, 1)
            for c in range(TT):
                v = k.v_tok[:, 1, c, :].rearrange("p (h d) -> p h d", d=HD)
                r4 = r.rearrange("p (h d) -> p h d", d=HD)
                if c >= 1:
                    dve.wait_ge(ks, c)
                    link(nc.vector.tensor_tensor(
                        r.rearrange("p (g o d) -> p o g d", g=2, o=2),
                        k.psum[:, 0:2, 0:2 * HD].rearrange("p o (g d) -> p o g d", g=2),
                        k.gamma_tok[:, c * HEADS:(c + 1) * HEADS].rearrange("p (g o) -> p o g", g=2)
                        .unsqueeze(3).broadcast_to([P, 2, 2, HD]), ALU.mult))
                    nc.vector.tensor_tensor(r4, v, r4, ALU.subtract).then_inc(r_ready, 1)
                else:
                    nc.vector.tensor_copy(r4, v).then_inc(r_ready, 1)
                dve.wait_ge(solved, c + 1)
                if c >= 1:
                    dve.wait_ge(out, c)
                nc.vector.tensor_tensor(
                    u.rearrange("p (h d) -> p h d", d=HD),
                    k.psum[:, 7, 0:256].rearrange("p (h d) -> p h d", d=HD),
                    k.beta[:, c * HEADS:(c + 1) * HEADS].unsqueeze(2).broadcast_to([P, HEADS, HD]),
                    ALU.mult).then_inc(u_ready, 1)
                if c < TT - 1:
                    dve.wait_ge(grown, c + 1)
                    dve.wait_ge(out, c + 1)
                    link(nc.vector.scalar_tensor_tensor(
                        k.state[:, 0, :], k.state[:, 0, :], k.whole[:, 0, c:c + 1], k.psum[:, 2, 0:HD],
                        ALU.mult, ALU.add))
                    nc.vector.scalar_tensor_tensor(
                        k.state[:, 1, :], k.state[:, 1, :], k.whole[:, 1, c:c + 1], k.psum[:, 3, 0:HD],
                        ALU.mult, ALU.add).then_inc(s_ready, 1)

        @block.scalar
        def _(act):
            for m in range(2):
                act.wait_ge(out, TT)
                nc.scalar.copy(k.o[:, 2 + m, :], k.psum[:, 4 + m, :])


def residual_product(k, name):
    nc = k.nc
    out = k.sem(name + "_out")
    with nc.Block() as block:
        @block.sync
        def _(sp):
            k.load_ahead(sp, name)

        @block.tensor
        def _(pe):
            k.product(pe, name, lambda kk: k.act_in[:, kk, :], T, out)

        @block.vector
        def _(dve):
            for j in range(KT):
                dve.wait_ge(k.weights_used, k.product_done(name, j))
                nc.vector.tensor_tensor(k.h[:, j, :], k.h[:, j, :], k.psum[:, j % PRODUCT_BANKS, :], ALU.add
                                        ).then_inc(out, 1)


def cross_attention(k):
    nc = k.nc
    out = k.sem("att_q_out")
    with nc.Block() as block:
        @block.sync
        def _(sp):
            k.load_ahead(sp, "att_q")

        @block.tensor
        def _(pe):
            k.product(pe, "att_q", lambda kk: k.n[:, kk, :], T, out)

        @block.scalar
        def _(act):
            for j in range(KT):
                act.wait_ge(k.weights_used, k.product_done("att_q", j))
                nc.scalar.copy(k.z[:, j, :], k.psum[:, j % PRODUCT_BANKS, :]).then_inc(out, 1)

    scale = 256 ** -0.5
    scored, maxed, risen, normed, turned, kept, steps = (
        k.sem("xa_" + s) for s in ("scored", "maxed", "risen", "normed", "turned", "kept", "steps"))
    units = [(hp, i) for hp in range(2) for i in range(TT)]
    with nc.Block() as block:
        @block.tensor
        def _(pe):
            def scores(u):
                hp, i = units[u]
                if u >= 3:
                    pe.wait_ge(risen, 2 * (u - 2))
                for h in range(2):
                    for kk in range(2):
                        f = 2 * (2 * hp + h) + kk
                        last = nc.tensor.matmul(k.psum[:, u % 3, h * MEM:(h + 1) * MEM],
                                                k.z[:, f, i * P:(i + 1) * P], k.mem_k[:, f, :],
                                                start=(kk == 0), stop=(kk == 1))
                last.then_inc(scored, 1)

            scores(0)
            for u in range(len(units)):
                if u + 1 < len(units):
                    scores(u + 1)
                pe.wait_ge(normed, 2 * (u + 1))
                if u >= 2:
                    pe.wait_ge(kept, u - 1)
                for b in range(4):
                    last = nc.tensor.transpose(k.psum[:, 4 + u % 2, b * P:(b + 1) * P],
                                               k.scratch[:, u % 4, b * P:(b + 1) * P], k.const("ident"))
                last.then_inc(turned, 1)

        @block.vector
        def _(dve):
            link = Link(dve, steps)
            for u in range(len(units)):
                dve.wait_ge(scored, u + 1)
                m = k.small[:, u % 4, 0:2]
                link(nc.vector.tensor_reduce(m, k.psum[:, u % 3, :].rearrange("p (h x) -> p h x", h=2),
                                             AX_X, ALU.max))
                nc.vector.tensor_scalar(m, m, -scale, None, ALU.mult).then_inc(maxed, 1)
                dve.wait_ge(risen, 2 * (u + 1))
                s = k.small[:, u % 4, 2:4]
                link(nc.vector.reciprocal(s, s))
                for h in range(2):
                    p = k.scratch[:, u % 4, h * MEM:(h + 1) * MEM]
                    nc.vector.tensor_scalar(p, p, s[:, h:h + 1], None, ALU.mult).then_inc(normed, 1)

        @block.scalar
        def _(act):
            def keep(u):
                hp, i = units[u]
                act.wait_ge(turned, u + 1)
                nc.scalar.copy(k.probs_t[:, 4 * hp:4 * hp + 4, i * P:(i + 1) * P],
                               k.psum[:, 4 + u % 2, :].rearrange("p (b x) -> p b x", b=4)).then_inc(kept, 1)

            for u in range(len(units)):
                act.wait_ge(maxed, u + 1)
                if u >= 4:
                    act.wait_ge(turned, u - 3)
                for h in range(2):
                    nc.scalar.activation(k.scratch[:, u % 4, h * MEM:(h + 1) * MEM],
                                         k.psum[:, u % 3, h * MEM:(h + 1) * MEM], ACT.Exp,
                                         bias=k.small[:, u % 4, h:h + 1], scale=scale,
                                         accum_out=k.small[:, u % 4, 2 + h:3 + h]).then_inc(risen, 1)
                if u >= 1:
                    keep(u - 1)
            keep(len(units) - 1)

    mixed, moved = k.sem("xa_mixed"), k.sem("xa_moved")
    with nc.Block() as block:
        @block.tensor
        def _(pe):
            for f in range(KT):
                if f >= 4:
                    pe.wait_ge(moved, f - 3)
                for m in range(2):
                    last = nc.tensor.matmul(k.psum[:, f % 4, :], k.mem_v[:, m, f * P:(f + 1) * P],
                                            k.probs_t[:, 2 * (f // 2) + m, :], start=(m == 0), stop=(m == 1))
                last.then_inc(mixed, 1)

        @block.scalar
        def _(act):
            for f in range(KT):
                act.wait_ge(mixed, f + 1)
                nc.scalar.copy(k.act_in[:, f, :], k.psum[:, f % 4, :]).then_inc(moved, 1)


MOD_CHUNKS = 32


def ffn_up(k, idx):
    nc = k.nc
    name = f"up_{idx}"
    both, mod = idx == 0, idx == 0
    out, padded, gate_done, risen, hid_done, steps = (
        k.sem(f"{name}_{s}") for s in ("out", "padded", "gate", "risen", "hid", "steps"))
    taps = k.vec(f"ffn_conv_{idx}")
    nt = 2 * FT if both else FT
    if mod:
        mod_loaded = [k.sem("mod_loaded0"), k.sem("mod_loaded1")]
        mod_ready, mod_summed, mod_steps = k.sem("mod_ready"), k.sem("mod_summed"), k.sem("mod_steps")
    with nc.Block() as block:
        @block.sync
        def _(sp):
            k.load_ahead(sp, name)

        if mod:
            @block.gpsimd
            def _(pool):
                for c in range(MOD_CHUNKS):
                    if c >= 2:
                        pool.wait_ge(mod_ready, c - 1)
                    pool.dma_start(k.mod_w[:, c % 2], k.dram["mod_w"][c]).then_inc(mod_loaded[c % 2], 16)

        @block.tensor
        def _(pe):
            def between(j):
                c = j - 4
                if mod and 0 <= c < MOD_CHUNKS:
                    pe.wait_ge(mod_ready, c + 1)
                    for b in range(3):
                        last = nc.tensor.matmul(k.psum[:, 7, 3 * c + b:3 * c + b + 1],
                                                k.mod_acc[:, c % 2, b * P:(b + 1) * P], k.const("ones")[:, 0:1],
                                                start=True, stop=True)
                    last.then_inc(mod_summed, 1)

            k.product(pe, name, lambda kk: k.n[:, kk, :], T, out, between=between)

        @block.scalar
        def _(act):
            def rise(p):
                act.wait_ge(gate_done, p + 1)
                bias = k.vec(f"ffn_conv_b_{idx}")[:, p:p + 1] if not both else 0.0
                nc.scalar.activation(k.conv_g[:, p % 2, :], k.conv_g[:, p % 2, :], ACT.Silu, bias=bias
                                     ).then_inc(risen, 1)

            act.wait_ge(padded, 1)
            for p in range(FT):
                if p >= 2:
                    act.wait_ge(hid_done, p - 1)
                for s in range(2):
                    act.wait_ge(k.weights_used, k.product_done(name, 2 * p + s))
                    nc.scalar.copy(k.up_in[:, p % 2, s, 2:2 + T], k.psum[:, (2 * p + s) % PRODUCT_BANKS, :]
                                   ).then_inc(out, 1)
                if p >= 1:
                    rise(p - 1)
            rise(FT - 1)

        @block.vector
        def _(dve):
            link = Link(dve, steps)

            def conv(dst, src, col, last_sem):
                link(nc.vector.tensor_scalar(dst, src[:, 0:T], taps[:, col:col + 1], None, ALU.mult))
                link(nc.vector.scalar_tensor_tensor(dst, src[:, 1:1 + T], taps[:, nt + col:nt + col + 1],
                                                    dst, ALU.mult, ALU.add))
                step = nc.vector.scalar_tensor_tensor(dst, src[:, 2:2 + T],
                                                      taps[:, 2 * nt + col:2 * nt + col + 1], dst,
                                                      ALU.mult, ALU.add)
                if last_sem is None:
                    link(step)
                else:
                    step.then_inc(last_sem, 1)

            def hidden(p):
                dve.wait_ge(risen, p + 1)
                value = k.conv_v[:, p % 2, :] if both else k.up_in[:, p % 2, 1, 2:2 + T]
                nc.vector.tensor_tensor(k.hidden[:, p, :], k.conv_g[:, p % 2, :], value, ALU.mult
                                        ).then_inc(hid_done, 1)

            def mod_chunk(c):
                dve.wait_ge(mod_loaded[c % 2], 16 * (c // 2 + 1))
                if c >= 2:
                    dve.wait_ge(mod_summed, c - 1)
                acc, cond = k.mod_acc[:, c % 2, :], k.cond[:]
                link(nc.vector.tensor_scalar(acc, k.mod_w[:, c % 2, 0, :], cond[:, 0:1], None, ALU.mult))
                for r in range(1, KT):
                    step = nc.vector.scalar_tensor_tensor(acc, k.mod_w[:, c % 2, r, :], cond[:, r:r + 1],
                                                          acc, ALU.mult, ALU.add)
                    if r < KT - 1:
                        link(step)
                step.then_inc(mod_ready, 1)

            nc.vector.memset(k.up_in[:, :, :, 0:2], 0.0).then_inc(padded, 1)
            for p in range(FT):
                dve.wait_ge(out, 2 * p + 1)
                if p >= 2:
                    dve.wait_ge(hid_done, p - 1)
                conv(k.conv_g[:, p % 2, :], k.up_in[:, p % 2, 0], p, gate_done)
                dve.wait_ge(out, 2 * p + 2)
                if both:
                    conv(k.conv_v[:, p % 2, :], k.up_in[:, p % 2, 1], FT + p, None)
                if mod and p < MOD_CHUNKS // 2:
                    mod_chunk(2 * p)
                if p >= 1:
                    hidden(p - 1)
                if mod and p < MOD_CHUNKS // 2:
                    mod_chunk(2 * p + 1)
            hidden(FT - 1)


def plain_product(k, name, src, dst):
    nc = k.nc
    out = k.sem(name + "_out")
    with nc.Block() as block:
        @block.sync
        def _(sp):
            k.load_ahead(sp, name)

        @block.tensor
        def _(pe):
            k.product(pe, name, src, T, out)

        @block.scalar
        def _(act):
            for j in range(PRODUCTS[name][0]):
                act.wait_ge(k.weights_used, k.product_done(name, j))
                nc.scalar.copy(dst[:, j, :], k.psum[:, j % PRODUCT_BANKS, :]).then_inc(out, 1)


def condition(k):
    nc = k.nc
    with nc.Block() as block:
        @block.scalar
        def _(act):
            nc.scalar.activation(k.cond[:], k.vec("cond"), ACT.Silu)


def modulation(k):
    nc = k.nc
    steps = k.sem("modulation_steps")
    with nc.Block() as block:
        @block.vector
        def _(dve):
            link = Link(dve, steps)
            for i in range(2):
                link(nc.vector.tensor_tensor(k.mod[:, i, :], k.psum[:, 7, 48 * i:48 * (i + 1)],
                                             k.vec(f"mod_b_{i}"), ALU.add))
                for part, norm in ((1, f"mix_pre_{i}"), (2, f"mix_post_{i}"), (4, f"ffn_pre_{i}"),
                                   (5, f"ffn_post_{i}")):
                    m = k.mod[:, i, part * KT:(part + 1) * KT]
                    link(nc.vector.scalar_tensor_tensor(m, m, 1.0, k.vec(norm), ALU.add, ALU.mult))


def mod_part(k, i, part):
    return k.mod[:, i, part * KT:(part + 1) * KT]


def ab_projection(k):
    nc = k.nc
    out, padded, steps, convolved = (k.sem("ab_in_" + s) for s in ("out", "padded", "steps", "conv"))
    with nc.Block() as block:
        @block.sync
        def _(sp):
            k.load_ahead(sp, "ab_in")

        @block.tensor
        def _(pe):
            k.product(pe, "ab_in", lambda kk: k.n[:, kk, :], T, out)

        @block.scalar
        def _(act):
            act.wait_ge(padded, 1)
            for j in range(PRODUCTS["ab_in"][0]):
                act.wait_ge(k.weights_used, k.product_done("ab_in", j))
                bank = k.psum[:, j % PRODUCT_BANKS, :]
                if j < GR:
                    if j >= 2:
                        act.wait_ge(convolved, j - 1)
                    nc.scalar.copy(k.conv_in[:, j % 2, 3:3 + T], bank).then_inc(out, 1)
                elif j < NQT:
                    nc.scalar.activation(k.z[:, j, :], bank, ACT.Gelu_apprx_tanh).then_inc(out, 1)
                elif j == GL:
                    nc.scalar.activation(k.z[:, j, :], bank, ACT.Sigmoid).then_inc(out, 1)
                else:
                    nc.scalar.copy(k.z[:, j, :], bank).then_inc(out, 1)

        @block.vector
        def _(dve):
            link = Link(dve, steps)
            nc.vector.memset(k.conv_in[:, 0:2, 0:3], 0.0).then_inc(padded, 1)
            w, b = k.vec("ab_conv"), k.vec("ab_conv_b")
            for j in range(KT):
                dve.wait_ge(out, j + 1)
                link(nc.vector.tensor_scalar(k.z[:, j, :], k.conv_in[:, j % 2, 0:T], w[:, j:j + 1],
                                             b[:, j:j + 1], ALU.mult, ALU.add))
                for tap in range(1, 4):
                    step = nc.vector.scalar_tensor_tensor(
                        k.z[:, j, :], k.conv_in[:, j % 2, tap:tap + T], w[:, KT * tap + j:KT * tap + j + 1],
                        k.z[:, j, :], ALU.mult, ALU.add)
                    if tap < 3:
                        link(step)
                step.then_inc(convolved, 1)


def recurrence(k):
    nc = k.nc
    rate_up, rate_done, projected, opened, ready_a, ready_t, sqrt_in, rooted, steps, asteps, scanned = (
        k.sem("lru_" + s) for s in ("rate_up", "rate", "projected", "opened", "a", "t", "sqrt_in", "rooted",
                                    "steps", "asteps", "scanned"))
    r, inp, th = k.lru_r, k.lru_i, k.lru_t
    rate, nrate, e = k.small[:, 0, 0:KT], k.small[:, 1, 0:KT], k.small[:, 2, 0:KT]
    with nc.Block() as block:
        @block.tensor
        def _(pe):
            for i in range(KT):
                for g in range(2):
                    if i >= 4:
                        pe.wait_ge(opened, 2 * (i - 4) + g + 1)
                    nc.tensor.matmul(k.psum[:, 2 * (i % 4) + g, :], k.lru_w[:, g, i, :], k.z[:, XR + i, :],
                                     start=True, stop=True).then_inc(projected, 1)

        @block.scalar
        def _(act):
            link = Link(act, asteps)
            link(nc.scalar.activation(e, k.vec("lru_lam"), ACT.Abs))
            link(nc.scalar.activation(e, e, ACT.Exp, scale=-1.0))
            nc.scalar.activation(e, e, ACT.Ln, bias=1.0).then_inc(rate_up, 1)
            for i in range(KT):
                for g, (dst, bias) in enumerate(((r, "lru_b_r"), (inp, "lru_b_i"))):
                    act.wait_ge(projected, 2 * i + g + 1)
                    nc.scalar.activation(dst[:, i, :], k.psum[:, 2 * (i % 4) + g, :], ACT.Sigmoid,
                                         bias=k.vec(bias)[:, i:i + 1]).then_inc(opened, 1)
            act.wait_ge(rate_done, 1)
            act.wait_ge(opened, 2 * KT)
            for i in range(KT):
                nc.scalar.activation(th[:, i, :], r[:, i, :], ACT.Tanh, scale=rate[:, i:i + 1]
                                     ).then_inc(ready_t, 1)
            for i in range(KT):
                act.wait_ge(ready_t, i + 1)
                nc.scalar.activation(r[:, i, :], r[:, i, :], ACT.Exp, scale=nrate[:, i:i + 1]
                                     ).then_inc(ready_a, 1)
            for i in range(KT):
                act.wait_ge(sqrt_in, i + 1)
                nc.scalar.activation(th[:, i, :], th[:, i, :], ACT.Sqrt, scale=2.0).then_inc(rooted, 1)

        @block.vector
        def _(dve):
            link = Link(dve, steps)
            dve.wait_ge(rate_up, 1)
            link(nc.vector.tensor_scalar(rate, k.vec("lru_lam"), -1.0, 0.0, ALU.mult, ALU.max))
            link(nc.vector.tensor_tensor(rate, rate, e, ALU.add))
            link(nc.vector.tensor_scalar(rate, rate, 8.0, None, ALU.mult))
            nc.vector.tensor_scalar(nrate, rate, -1.0, None, ALU.mult).then_inc(rate_done, 1)
            for i in range(KT):
                tmp = k.scratch[:, i % 2, :]
                dve.wait_ge(opened, 2 * i + 2)
                nc.vector.tensor_tensor(inp[:, i, :], inp[:, i, :], k.z[:, XR + i, :], ALU.mult)
                dve.wait_ge(ready_t, i + 1)
                link(nc.vector.tensor_scalar(tmp, th[:, i, :], 1.0, None, ALU.add))
                link(nc.vector.reciprocal(tmp, tmp))
                dve.wait_ge(ready_a, i + 1)
                link(nc.vector.tensor_tensor(th[:, i, :], th[:, i, :], tmp, ALU.mult))
                nc.vector.tensor_scalar(th[:, i, :], th[:, i, :], 1e-30, None, ALU.max).then_inc(sqrt_in, 1)
            for i in range(KT):
                dve.wait_ge(rooted, i + 1)
                link(nc.vector.tensor_tensor(inp[:, i, :], inp[:, i, :], th[:, i, :], ALU.mult))
                link(nc.vector.tensor_tensor_scan(th[:, i, :], r[:, i, :], inp[:, i, :], 0.0,
                                                  ALU.mult, ALU.add))
                nc.vector.tensor_tensor(k.act_in[:, i, :], th[:, i, :], k.z[:, GR + i, :], ALU.mult
                                        ).then_inc(scanned, 1)


def group_rows(g):
    return slice(HD * (g % 2), HD * (g % 2) + HD)


def compress(k):
    nc = k.nc
    loaded, spread, hid, acted, up, steps, moved, pe_kept = (
        k.sem("cmp_" + s) for s in ("loaded", "spread", "hid", "acted", "up", "steps", "moved", "pe_kept"))
    with nc.Block() as block:
        @block.sync
        def _(sp):
            sp.dma_start(k.cmp_w1[:], k.dram["cmp_w1"]).then_inc(loaded, 16)
            sp.dma_start(k.cmp_w2[:], k.dram["cmp_w2"]).then_inc(loaded, 16)

        @block.scalar
        def _(act):
            for kind, tile in enumerate((KC, VC)):
                for g in range(NG):
                    src = k.z[group_rows(g), tile + g // 2, :]
                    nc.scalar.copy(k.pairs[0:HD, kind, g, :], src)
                    nc.scalar.copy(k.pairs[HD:P, kind, g, 0:T - 1], src[:, 1:T]).then_inc(spread, 1)
            for kind in range(2):
                act.wait_ge(pe_kept, kind + 1)
                nc.scalar.activation(k.cmp_hid[:, kind, :, 0:NCMP],
                                     k.psum[:, kind, 0:NG * NCMP].rearrange("p (g n) -> p g n", g=NG),
                                     ACT.Gelu_apprx_tanh, bias=k.small[:, kind, 0:1]).then_inc(acted, 1)

        @block.vector
        def _(dve):
            nc.vector.memset(k.cmp_hid[:, :, :, NCMP:32], 0.0).then_inc(steps, 1)
            for kind in range(2):
                dve.wait_ge(hid, kind + 1)
                nc.vector.tensor_copy(k.small[:, kind, 0:1], k.psum[:, 2 + kind, 0:1]).then_inc(pe_kept, 1)
            dve.wait_ge(acted, 2)
            dve.wait_ge(steps, 1)
            nc.vector.tensor_copy(k.cmp_hid4, k.cmp_hid[:, 1].unsqueeze(2).broadcast_to([P, NG, 4, 32])
                                  ).then_inc(steps, 1)
            dve.wait_ge(up, 1)
            for g in range(NG):
                nc.vector.tensor_copy(k.cmp_k[group_rows(g), g // 2, :],
                                      k.psum[group_rows(g), 4, (g // 2) * 32:(g // 2) * 32 + 32])
            nc.vector.tensor_copy(k.cmp_v[:], k.psum[:, 5, 0:NG * HD].rearrange("p (g d) -> p g d", g=NG))

        @block.tensor
        def _(pe):
            pe.wait_ge(loaded, 32)
            for kind in range(2):
                pe.wait_ge(spread, NG * (kind + 1))
                for j in range(16):
                    nc.tensor.matmul(k.psum[:, kind, 0:NG * NCMP], k.cmp_w1[:, kind, j, :],
                                     k.pairs[:, kind, :, 2 * j:2 * j + 16 * (NCMP - 1) + 1:16],
                                     start=(j == 0), stop=(j == 15))
                pe_vec = k.vec("pe_k" if kind == 0 else "pe_v")
                for j in range(16):
                    last = nc.tensor.matmul(k.psum[:, 2 + kind, 0:1], k.cmp_w1[:, kind, j, :],
                                            pe_vec[:, j:j + 1], start=(j == 0), stop=(j == 15))
                last.then_inc(hid, 1)
            pe.wait_ge(acted, 2)
            pe.wait_ge(steps, 2)
            for g in range(NG):
                nc.tensor.matmul(k.psum[group_rows(g), 4, (g // 2) * 32:(g // 2) * 32 + 32],
                                 k.cmp_w2[:, 0, :], k.cmp_hid[:, 0, g, :], start=True, stop=True)
            for g in range(NG):
                last = nc.tensor.matmul(k.psum[:, 5, g * HD:(g + 1) * HD],
                                        k.cmp_hid4[:, g].rearrange("p r n -> p (r n)"),
                                        k.cmp_w2[:, 1, :], start=True, stop=True)
            last.then_inc(up, 1)


def compressed_attention(k):
    nc = k.nc
    scored, taken, steps, shifted, risen, gated, turned, kept = (
        k.sem("ca_" + s) for s in ("scored", "taken", "steps", "shifted", "risen", "gated", "turned", "kept"))
    scale = HD ** -0.5
    with nc.Block() as block:
        @block.tensor
        def _(pe):
            for i in range(TT):
                if i >= 2:
                    pe.wait_ge(taken, 2 * (i - 1))
                for h in range(NQ):
                    g, r = h // 4, h % 4
                    at = (4 * (g // 2) + r) * 32
                    last = nc.tensor.matmul(k.psum[:, 2 * (i % 2) + g % 2, at:at + 32],
                                            k.z[group_rows(g), NQT + 4 * (g // 2) + r, i * P:(i + 1) * P],
                                            k.cmp_k[group_rows(g), g // 2, :], start=True, stop=True)
                last.then_inc(scored, 1)
            for i in range(TT):
                pe.wait_ge(gated, i + 1)
                for g in range(NG):
                    last = nc.tensor.transpose(k.psum[:, 4 + i, g * P:(g + 1) * P],
                                               k.scratch[:, i, g * P:(g + 1) * P], k.const("ident"))
                last.then_inc(turned, 1)

        @block.scalar
        def _(act):
            for i in range(TT):
                act.wait_ge(shifted, i + 1)
                nc.scalar.activation(k.scratch[:, i, :], k.scratch[:, i, :], ACT.Exp, scale=scale
                                     ).then_inc(risen, 1)
            for i in range(TT):
                act.wait_ge(turned, i + 1)
                nc.scalar.copy(k.cmp_pt[:, :, i * P:(i + 1) * P],
                               k.psum[:, 4 + i, :].rearrange("p (g x) -> p g x", g=NG)).then_inc(kept, 1)

        @block.vector
        def _(dve):
            link = Link(dve, steps)
            m, den = k.small[:, 0, 0:NQ], k.small[:, 1, 0:NQ]
            by_n = k.scratch[:, 4, 0:P].rearrange("p (g n) -> p g n", g=NG)
            imp = k.scratch[:, 4, P:P + 32].rearrange("p (g j) -> p g j", g=NG)
            rank = k.scratch[:, 4, P + 32:P + 64].rearrange("p (g j) -> p g j", g=NG)
            above = k.scratch[:, 5, 0:256].rearrange("p (g j i) -> p g j i", g=NG, j=NBLK)
            tied = k.scratch[:, 5, 256:512].rearrange("p (g j i) -> p g j i", g=NG, j=NBLK)
            for i in range(TT):
                s = k.scratch[:, i, :].rearrange("p (h n) -> p h n", h=NQ)
                dve.wait_ge(scored, i + 1)
                for odd in range(2):
                    nc.vector.tensor_tensor(
                        k.scratch[:, i, :].rearrange("p (g o r n) -> p o g r n", g=2, o=2, r=4)[:, odd],
                        k.psum[:, 2 * (i % 2) + odd, 0:256].rearrange("p (g r n) -> p g r n", g=2, r=4),
                        k.const(f"cmp_bias{i}").unsqueeze(1).unsqueeze(1).broadcast_to([P, 2, 4, 32]),
                        ALU.add).then_inc(taken, 1)
                dve.wait_ge(taken, 2 * (i + 1))
                link(nc.vector.tensor_reduce(m, s, AX_X, ALU.max))
                nc.vector.tensor_tensor(s, s, m.unsqueeze(2).broadcast_to([P, NQ, 32]), ALU.subtract
                                        ).then_inc(shifted, 1)
                dve.wait_ge(risen, i + 1)
                link(nc.vector.tensor_tensor(s, s, k.const(f"cmp_seen{i}").unsqueeze(1)
                                             .broadcast_to([P, NQ, 32]), ALU.mult))
                link(nc.vector.tensor_reduce(den, s, AX_X, ALU.add))
                link(nc.vector.tensor_scalar(den, den, 1e-30, None, ALU.max))
                link(nc.vector.reciprocal(den, den))
                link(nc.vector.tensor_tensor(s, s, den.unsqueeze(2).broadcast_to([P, NQ, 32]), ALU.mult))
                link(nc.vector.tensor_reduce(by_n, k.scratch[:, i, :].rearrange("p (g r n) -> p g n r", g=NG, r=4),
                                             AX_X, ALU.add))
                link(nc.vector.tensor_reduce(imp, by_n.rearrange("p g (j x) -> p g j x", x=4), AX_X, ALU.add))
                link(nc.vector.tensor_tensor(imp[:, :, 1:NBLK], imp[:, :, 1:NBLK], by_n[:, :, 3:31:4], ALU.add))
                link(nc.vector.tensor_tensor(imp, imp, k.const(f"block_bias{i}").unsqueeze(1)
                                             .broadcast_to([P, NG, NBLK]), ALU.add))
                mine = imp.unsqueeze(3).broadcast_to([P, NG, NBLK, NBLK])
                other = imp.unsqueeze(2).broadcast_to([P, NG, NBLK, NBLK])
                link(nc.vector.tensor_tensor(above, other, mine, ALU.is_gt))
                link(nc.vector.tensor_tensor(tied, other, mine, ALU.is_equal))
                t3 = k.scratch[:, 5, 256:512].rearrange("p (g x) -> p g x", g=NG)
                link(nc.vector.tensor_tensor(t3, t3, k.const("earlier").unsqueeze(1).broadcast_to([P, NG, 64]),
                                             ALU.mult))
                link(nc.vector.tensor_tensor(k.scratch[:, 5, 0:256], k.scratch[:, 5, 0:256],
                                             k.scratch[:, 5, 256:512], ALU.add))
                link(nc.vector.tensor_reduce(rank, above, AX_X, ALU.add))
                link(nc.vector.tensor_scalar(k.block_bias[:, i, :, :], rank, 3.5, NEG, ALU.is_ge, ALU.mult))
                nc.vector.tensor_tensor(
                    s, s, k.gate_tok[:, i, 0:48].rearrange("p (h b) -> p h b", b=3)[:, :, 0:1]
                    .broadcast_to([P, NQ, 32]), ALU.mult).then_inc(gated, 1)
                dve.wait_ge(gated, i + 1)


def partial_rotary(k):
    nc = k.nc
    turned, taken, steps = (k.sem("pr_" + s) for s in ("turned", "taken", "steps"))
    tiles = list(range(NQT, NQT + 8)) + [KS, KS + 1, KW, KW + 1]
    with nc.Block() as block:
        @block.tensor
        def _(pe):
            for i, j in enumerate(tiles):
                if i >= 4:
                    pe.wait_ge(taken, i - 3)
                nc.tensor.matmul(k.psum[:, i % 4, :], k.const("rotate_part"), k.z[:, j, :],
                                 start=True, stop=True).then_inc(turned, 1)

        @block.vector
        def _(dve):
            link = Link(dve, steps)
            for i, j in enumerate(tiles):
                tmp = k.scratch[:, i % 2, :]
                dve.wait_ge(turned, i + 1)
                link(nc.vector.tensor_tensor(k.z[:, j, :], k.z[:, j, :], k.const("rope_cos"), ALU.mult))
                nc.vector.tensor_tensor(tmp, k.psum[:, i % 4, :], k.const("rope_sin"), ALU.mult).then_inc(taken, 1)
                dve.wait_ge(taken, i + 1)
                link(nc.vector.tensor_tensor(k.z[:, j, :], k.z[:, j, :], tmp, ALU.add))


def sparse_attention(k):
    nc = k.nc
    scored, biased, maxed, risen, normed, turned, kept, mixed, moved, steps = (
        k.sem("sa_" + s) for s in ("scored", "biased", "maxed", "risen", "normed", "turned", "kept",
                                   "mixed", "moved", "steps"))
    scale = HD ** -0.5
    items = [(h, i, b) for h in range(NQ) for i in range(TT) for b in range(2)]
    BUF = 4

    def keys(i, b):
        first = 0 if b == 0 else max(0, i - 2)
        return first, i + 1 - first

    with nc.Block() as block:
        @block.gpsimd
        def _(pool):
            for g in range(NG):
                if g >= 2:
                    pool.wait_ge(maxed, 8 * 4 * (g - 1))
                for i in range(TT):
                    w = (i + 1) * P
                    dst = k.sel_bias[:, g % 2, i, :]
                    nc.gpsimd.tensor_copy(
                        dst[:, 0:w].rearrange("p (j x) -> p j x", x=HD),
                        k.block_bias[:, i, g, 0:2 * (i + 1)].unsqueeze(2).broadcast_to([P, 2 * (i + 1), HD])
                    ).then_inc(biased, 1)
                    pool.wait_ge(biased, 2 * (g * TT + i) + 1)
                    nc.gpsimd.tensor_tensor(dst[:, w - P:w], dst[:, w - P:w], k.const("causal"), ALU.add
                                            ).then_inc(biased, 1)

        @block.tensor
        def _(pe):
            def scores(n):
                h, i, b = items[n]
                g, r = h // 4, h % 4
                first, nk = keys(i, b)
                if n >= 3:
                    pe.wait_ge(maxed, n - 2)
                tile = (KS if b == 0 else KW) + g // 2
                nc.tensor.matmul(k.psum[:, n % 3, 0:nk * P],
                                 k.z[group_rows(g), NQT + 4 * (g // 2) + r, i * P:(i + 1) * P],
                                 k.z[group_rows(g), tile, first * P:(first + nk) * P],
                                 start=True, stop=True).then_inc(scored, 1)

            def transposes(n):
                h, i, b = items[n]
                pe.wait_ge(normed, n + 1)
                if n >= 3:
                    pe.wait_ge(kept, n - 2)
                for j in range(keys(i, b)[1]):
                    last = nc.tensor.transpose(k.psum[:, 3 + n % 3, j * P:(j + 1) * P],
                                               k.rows[:, n % BUF, j * P:(j + 1) * P], k.const("ident"))
                last.then_inc(turned, 1)

            def values(h):
                g, r = h // 4, h % 4
                pe.wait_ge(kept, 8 * (h + 1))
                if h >= 2:
                    pe.wait_ge(moved, h - 1)
                dst = k.psum[group_rows(g), 6 + h % 2, :]
                rows = slice(32 * r, 32 * r + 32)
                nc.tensor.matmul(dst, k.cmp_v[rows, g, :], k.cmp_pt[rows, g, :], start=True, stop=False)
                for b, v in enumerate((k.vs_tok, k.vw_tok)):
                    for j in range(TT):
                        last_t = T if b == 0 else min(T, (j + 3) * P)
                        last = nc.tensor.matmul(dst[:, j * P:last_t], v[:, j, g * HD:(g + 1) * HD],
                                                k.pt[:, h % 2, b, j, j * P:last_t],
                                                start=False, stop=(b == 1 and j == TT - 1))
                last.then_inc(mixed, 1)

            scores(0)
            scores(1)
            for n in range(len(items)):
                if n + 2 < len(items):
                    scores(n + 2)
                transposes(n)
                if n % 8 == 2 and n > 8:
                    values(n // 8 - 1)
            values(NQ - 1)

        @block.vector
        def _(dve):
            link = Link(dve, steps)

            def norm(n):
                h, i, b = items[n]
                w = keys(i, b)[1] * P
                dve.wait_ge(risen, n + 1)
                s = k.stats[:, 1, n % BUF:n % BUF + 1]
                link(nc.vector.reciprocal(s, s))
                p = k.rows[:, n % BUF, 0:w]
                gate = k.gate_tok[:, i, 3 * h + 1 + b:3 * h + 2 + b]
                nc.vector.tensor_scalar(p, p, s, gate, ALU.mult, ALU.mult).then_inc(normed, 1)

            for n, (h, i, b) in enumerate(items):
                w = keys(i, b)[1] * P
                dve.wait_ge(scored, n + 1)
                if n >= BUF:
                    dve.wait_ge(turned, n - BUF + 1)
                if b == 0:
                    dve.wait_ge(biased, 2 * ((h // 4) * TT + i + 1))
                    bias = k.sel_bias[:, (h // 4) % 2, i, 0:w]
                else:
                    bias = k.const("window")[:, 384 - w:384]
                m = k.stats[:, 0, n % BUF:n % BUF + 1]
                link(nc.vector.tensor_tensor_reduce(
                    out=k.rows[:, n % BUF, 0:w], in0=k.psum[:, n % 3, 0:w], in1=bias, scale=scale,
                    scalar=-3e38, op0=ALU.add, op1=ALU.max, accum_out=m))
                nc.vector.tensor_scalar(m, m, -1.0, None, ALU.mult).then_inc(maxed, 1)
                if n >= 1:
                    norm(n - 1)
            norm(len(items) - 1)

        @block.scalar
        def _(act):
            def keep(n):
                h, i, b = items[n]
                first, nk = keys(i, b)
                act.wait_ge(turned, n + 1)
                if h >= 2:
                    act.wait_ge(mixed, h - 1)
                nc.scalar.copy(k.pt[:, h % 2, b, first:first + nk, i * P:(i + 1) * P],
                               k.psum[:, 3 + n % 3, 0:nk * P].rearrange("p (j x) -> p j x", x=P)
                               ).then_inc(kept, 1)

            def move(h):
                g, r = h // 4, h % 4
                act.wait_ge(mixed, h + 1)
                nc.scalar.copy(k.act_in[group_rows(g), KT + 4 * (g // 2) + r, :],
                               k.psum[group_rows(g), 6 + h % 2, :]).then_inc(moved, 1)

            for n, (h, i, b) in enumerate(items):
                w = keys(i, b)[1] * P
                act.wait_ge(maxed, n + 1)
                nc.scalar.activation(k.rows[:, n % BUF, 0:w], k.rows[:, n % BUF, 0:w], ACT.Exp,
                                     bias=k.stats[:, 0, n % BUF:n % BUF + 1],
                                     accum_out=k.stats[:, 1, n % BUF:n % BUF + 1]).then_inc(risen, 1)
                if n >= 2:
                    keep(n - 2)
                if n % 8 == 5 and n > 8:
                    move(n // 8 - 1)
            keep(len(items) - 2)
            keep(len(items) - 1)
            move(NQ - 1)


def short_conv_mixer(k):
    nc = k.nc
    out, padded, steps, done = (k.sem("sc_" + s) for s in ("out", "padded", "steps", "done"))
    with nc.Block() as block:
        @block.sync
        def _(sp):
            k.load_ahead(sp, "sc_in")

        @block.tensor
        def _(pe):
            k.product(pe, "sc_in", lambda kk: k.n[:, kk, :], T, out)

        @block.scalar
        def _(act):
            for j in range(3 * KT):
                act.wait_ge(k.weights_used, k.product_done("sc_in", j))
                if j >= 6:
                    act.wait_ge(done, j // 3 - 1)
                nc.scalar.copy(k.scratch[:, j % 6, :], k.psum[:, j % PRODUCT_BANKS, :]).then_inc(out, 1)

        @block.vector
        def _(dve):
            link = Link(dve, steps)
            link(nc.vector.memset(k.up_in[:, 0, 0, 0:2], 0.0))
            w, b = k.vec("sc_conv"), k.vec("sc_conv_b")
            src, dst = k.up_in[:, 0, 0], k.conv_g[:, 0, :]
            for i in range(KT):
                c, v, g = (k.scratch[:, (3 * i + x) % 6, :] for x in range(3))
                dve.wait_ge(out, 3 * i + 2)
                if i >= 1:
                    dve.wait_ge(done, i)
                link(nc.vector.tensor_tensor(src[:, 2:2 + T], c, v, ALU.mult))
                link(nc.vector.tensor_scalar(dst, src[:, 0:T], w[:, i:i + 1], b[:, i:i + 1],
                                             ALU.mult, ALU.add))
                for tap in (1, 2):
                    link(nc.vector.scalar_tensor_tensor(dst, src[:, tap:tap + T],
                                                        w[:, KT * tap + i:KT * tap + i + 1], dst,
                                                        ALU.mult, ALU.add))
                dve.wait_ge(out, 3 * i + 3)
                nc.vector.tensor_tensor(k.act_in[:, i, :], dst, g, ALU.mult).then_inc(done, 1)


def store_output(k):
    nc = k.nc
    stored = k.stored
    with nc.Block() as block:
        @block.sync
        def _(sp):
            sp.dma_start(k.dram["out"], k.h[:]).then_inc(stored, 16)
            sp.wait_ge(stored, 16)


def build(nc, dram, wheres, vec_at, last_stage=None):
    done = []

    def reached(name):
        done.append(name)
        return last_stage == name

    with ExitStack() as ctx:
        k = Kernel(nc, ctx, dram)
        k.vec_at = vec_at
        k.tables = [(k.sb("consts_0", [P, dram["consts_0"].shape[1]]), wheres[0])]
        k.vecs = k.sb("vecs", [P, dram["vecs"].shape[1]])
        k.h = k.sb("h", [P, KT, T])
        k.n = k.sb("n", [P, KT, T])
        k.small = k.sb("small", [P, 4, 16])
        k.scratch = k.sb("scratch", [P, 6, T])
        k.squares, k.rstd = k.scratch[:, 0:2, :], k.scratch[:, 2, :]
        k.cond = k.sb("cond", [P, KT])
        k.mod = k.sb("mod", [P, 2, 48])

        with ExitStack() as first:
            k.tables.append((k.sb("consts_1", [P, dram["consts_1"].shape[1]], ctx=first), wheres[1]))
            k.masks = k.sb("masks", [P, len(LEVELS) + 1, P], ctx=first)
            load_inputs(k)
            condition(k)
            rms_norm(k, "mix_norm", k.h, k.vec("mix_norm"), k.n)
            with ExitStack() as a:
                k.z = k.sb("z1", [P, 31, T], ctx=a)
                k.o = k.n
                with ExitStack() as b:
                    k.conv_in = k.sb("conv_in1", [P, 6, T + 3], ctx=b)
                    mixer_projection(k)
                k.v_tok = k.sb("v_tok", [P, 4, TT, 256], ctx=a)
                k.k_tok = k.sb("k_tok", [P, TT, 256], ctx=a)
                k.misc_tok = k.sb("misc_tok", [P, TT, P], ctx=a)
                with ExitStack() as b:
                    k.cum = k.sb("cum", [P, 3, T], ctx=b)
                    with ExitStack() as c:
                        k.gla_up = k.sb("gla_up", [P, P], ctx=c)
                        k.positions = k.sb("positions", [P, T], I32, ctx=c)
                        k.half_pi = k.sb("half_pi", [P, 1], ctx=c)
                        load(k, "mixer_inputs", [(k.gla_up[64:96, :], "gla_up"), (k.positions[:], "positions")])
                        rotary(k)
                        k.head_sq = k.scratch
                        head_norm(k, "delta_qk", [(k.z[:, j, :], k.z[:, j, :], (HD ** -0.5 if j < BK else 1.0),
                                                   None) for j in (BQ, BQ + 1, BK, BK + 1)], 1.0)
                        log_decays(k)
                    if reached("mix_inputs"):
                        return k
                    groups = [([k.z[:, t + i % 2, (2 * g + i // 2) * P:(2 * g + i // 2 + 1) * P]
                                for i in range(4)], dst[:, 2 * g:2 * g + 2, :])
                              for t, dst in ((RV, k.v_tok[:, 0]), (BV, k.v_tok[:, 1]), (CV, k.v_tok[:, 2]),
                                             (DI, k.v_tok[:, 3]), (BK, k.k_tok)) for g in range(2)]
                    groups.append(([k.z[:, MISC, c * P:(c + 1) * P] for c in range(TT)], k.misc_tok[:, :, :]))
                    turn(k, "mix_turn", groups)
                    retention(k)
                    if reached("retention"):
                        return k
                    room = k.sb("scores", [P, 2, TT * (T + P)], ctx=b)
                    used = k.z[:, 0:10, :].rearrange("p (h a) x -> p h (a x)", h=2)
                    scores = [used[:, 0, :], used[:, 1, :], room[:, 0, :], room[:, 1, :]]
                    gated_scores(k, "gla", k.cum[:, 0, :], k.z[:, CQ, :], k.z[:, CK, :], 32, scores)
                    mix_values(k, "gla", 2, scores)
                    for i in range(2):
                        gated_scores(k, f"hgrn{i}", k.cum[:, 1 + i, :], k.z[:, DQ + i, :], k.z[:, DF + i, :],
                                     HD, scores[2 * i:2 * i + 2])
                    mix_values(k, "hgrn", 3, scores)
                if reached("gated"):
                    return k
                with ExitStack() as b:
                    k.gamma, k.q_sb, k.qg = k.z[:, 0:4, :], k.z[:, 4:6, :], k.z[:, 6:8, :]
                    k.nt, k.inv_n = k.z[:, 8:12, :], k.z[:, DQ:DQ + 4, :]
                    k.ratio = k.sb("ratio", [P, HEADS, T], ctx=b)
                    k.nb = k.sb("nb", [P, HEADS, T], ctx=b)
                    k.inv_t = k.sb("inv_t", [P, HEADS, T], ctx=b)
                    k.g_tok, k.gc_tok, k.gamma_tok, k.beta, k.tail = (
                        k.sb(s, [P, 16], ctx=b)[:] for s in ("g_tok", "gc_tok", "gamma_tok", "beta", "tail"))
                    k.whole = k.sb("whole", [P, 2, TT], ctx=b)
                    k.state = k.sb("state", [P, 2, HD], ctx=b)
                    delta_prepare(k)
                    if reached("delta_prepare"):
                        return k
                    delta_inverse(k)
                    if reached("delta_inverse"):
                        return k
                    delta_scan(k)
                    if reached("delta"):
                        return k
                gates = [RG, RG + 1, BG, BG + 1, CG, CG + 1, DG, DG + 1]
                gains = [1.0, 1.0] + [k.vec(s) for s in ("gdn_norm", "gla_norm", "hgrn_norm") for _ in range(2)]
                with ExitStack() as b:
                    k.head_sq = k.sb("head_sq", [P, 8, T], ctx=b)
                    head_norm(k, "mix_out_norm", [(k.o[:, i, :], k.o[:, i, :], gains[i], k.z[:, gates[i], :])
                                                  for i in range(8)], 1.0 / HD)
                k.act_in = k.o
                k.clear_stage_semaphores()
                residual_product(k, "mix_out")
            if reached("mix"):
                return k
            with ExitStack() as a:
                k.mem_k = k.sb("mem_k", [P, KT, MEM], ctx=a)
                k.mem_v = k.sb("mem_v", [P, 2, D], ctx=a)
                with ExitStack() as b:
                    k.mem = k.sb("mem", [P, KT, MEM], ctx=b)
                    k.mem_n = k.sb("mem_n", [P, KT, MEM], ctx=b)
                    k.mem_vt = k.sb("mem_vt", [P, KT, MEM], ctx=b)
                    load(k, "mem", [(k.mem[:], "mem_t")])
                    rms_norm(k, "mem_norm", k.mem, k.vec("mem_norm"), k.mem_n, MEM)
                    memory_projections(k)
                rms_norm(k, "att_norm", k.h, k.vec("att_norm"), k.n)
                k.z = k.sb("z_att", [P, KT, T], ctx=a)
                k.probs_t = k.sb("probs_t", [P, 8, T], ctx=a)
                k.act_in = k.sb("att_out", [P, KT, T], ctx=a)
                cross_attention(k)
                residual_product(k, "att_o")
            if reached("att"):
                return k
        k.tables.pop()
        k.clear_stage_semaphores()
        rms_norm(k, "ffn_norm", k.h, k.vec("ffn_norm"), k.n)
        with ExitStack() as a:
            ffn_buffers(k, a, 0)
            k.mod_w = k.sb("mod_w", [P, 2, KT, 384], ctx=a)
            k.mod_acc = k.sb("mod_acc", [P, 2, 384], ctx=a)
            ffn_up(k, 0)
            modulation(k)
            k.act_in = k.hidden
            residual_product(k, "down_0")
        rms_norm(k, "final_norm", k.h, k.vec("final_norm"), k.h)
        if reached("block1"):
            return k

        second = ctx.enter_context(ExitStack())
        k.tables.append((k.sb("consts_2", [P, dram["consts_2"].shape[1]], ctx=second), wheres[2]))
        load(k, "consts_2", [(k.tables[1][0][:], "consts_2")])
        rms_norm(k, "ab_norm", k.h, mod_part(k, 0, 1), k.n, shift=mod_part(k, 0, 0))
        with ExitStack() as a:
            k.z = k.sb("z2", [P, 37, T], ctx=a)
            with ExitStack() as b:
                k.conv_in = k.sb("conv_in2", [P, 2, T + 3], ctx=b)
                ab_projection(k)
            k.act_in = k.sb("ab_mixed", [P, 2 * KT, T], ctx=a)
            with ExitStack() as b:
                k.lru_w = k.sb("lru_w", [P, 2, KT, P], ctx=b)
                k.lru_r, k.lru_i = k.act_in[:, 0:KT, :], k.act_in[:, KT:2 * KT, :]
                k.lru_t = k.n
                load(k, "lru", [(k.lru_w[:], "lru_w")])
                recurrence(k)
            if reached("lru"):
                return k
            k.cmp_pt = k.sb("cmp_pt", [P, NG, T], ctx=a)
            k.cmp_k = k.sb("cmp_k", [P, 2, 32], ctx=a)
            k.cmp_v = k.sb("cmp_v", [P, NG, HD], ctx=a)
            k.block_bias = k.sb("block_bias", [P, TT, NG, NBLK], ctx=a)
            k.gate_tok = k.sb("gate_tok", [P, TT, P], ctx=a)
            with ExitStack() as b:
                k.pairs = k.act_in[:, KT:2 * KT, :].rearrange("p (a g) x -> p a g x", a=2)
                k.cmp_w1 = k.z[:, XR:XR + KT, :].rearrange("p (a j) (i x) -> p a (j i) x", a=2, x=P)
                k.cmp_w2 = k.sb("cmp_w2", [P, 2, HD], ctx=b)
                k.cmp_hid = k.n[:, 0, 0:2 * NG * 32].rearrange("p (a g n) -> p a g n", a=2, g=NG)
                k.cmp_hid4 = k.n[:, 1, :].rearrange("p (g r n) -> p g r n", g=NG, r=4)
                compress(k)
            turn(k, "gate_turn", [([k.z[:, GL, c * P:(c + 1) * P] for c in range(TT)], k.gate_tok[:, :, :])])
            compressed_attention(k)
            if reached("cmp"):
                return k
            partial_rotary(k)
            k.vs_tok = k.z[:, KC:KC + 2, :].rearrange("p a (b x) -> p (a b) x", x=256)
            k.vw_tok = k.z[:, VC:VC + 2, :].rearrange("p a (b x) -> p (a b) x", x=256)
            turn(k, "nsa_turn", [([k.z[:, t + i % 2, (2 * g + i // 2) * P:(2 * g + i // 2 + 1) * P]
                                   for i in range(4)], dst[:, 2 * g:2 * g + 2, :])
                                 for t, dst in ((VS, k.vs_tok), (VW, k.vw_tok)) for g in range(2)])
            k.pt = k.z[:, 0:16, :].rearrange("p (a b j) x -> p a b j x", a=2, b=2)
            k.rows = k.scratch[:, 0:4, :]
            k.stats = k.sb("stats", [P, 2, 4], ctx=a)
            k.sel_bias = k.n[:, :, :].rearrange("p (a i) x -> p a i x", a=2)
            sparse_attention(k)
            if reached("nsa"):
                return k
            plain_product(k, "ab_out", lambda kk: k.act_in[:, kk, :], k.n)
        rms_norm(k, "ab_post", k.n, mod_part(k, 0, 2), k.n, add_to=k.h)
        if reached("ab"):
            return k
        k.clear_stage_semaphores()
        second_ffn(k, 0)
        if reached("ffn1"):
            return k

        rms_norm(k, "sc_norm", k.h, mod_part(k, 1, 1), k.n, shift=mod_part(k, 1, 0))
        with ExitStack() as a:
            ffn_buffers(k, a, 9)
            k.act_in = k.hidden
            short_conv_mixer(k)
            plain_product(k, "sc_out", lambda kk: k.act_in[:, kk, :], k.n)
        if reached("sc"):
            return k
        rms_norm(k, "sc_post", k.n, mod_part(k, 1, 2), k.n, add_to=k.h)
        if reached("sc2"):
            return k
        second_ffn(k, 1)
        store_output(k)
    return k


def ffn_buffers(k, ctx, idx):
    k.up_in = k.sb(f"up_in{idx}", [P, 2, 2, T + 2], ctx=ctx)
    k.conv_g = k.sb(f"conv_g{idx}", [P, 2, T], ctx=ctx)
    k.conv_v = k.sb(f"conv_v{idx}", [P, 2, T], ctx=ctx)
    k.hidden = k.sb(f"hidden{idx}", [P, FT, T], ctx=ctx)


def second_ffn(k, layer):
    rms_norm(k, f"ffn_pre_{layer}", k.h, mod_part(k, layer, 4), k.n, shift=mod_part(k, layer, 3))
    with ExitStack() as a:
        ffn_buffers(k, a, layer + 1)
        ffn_up(k, layer + 1)
        plain_product(k, f"down_{layer + 1}", lambda kk: k.hidden[:, kk, :], k.n)
    rms_norm(k, f"ffn_post_{layer}", k.n, mod_part(k, layer, 5), k.n, add_to=k.h)


def tiled(w):
    kk, n = w.shape
    if n % P:
        w = np.concatenate([w, np.zeros((kk, P - n % P), w.dtype)], axis=1)
    return np.ascontiguousarray(w.reshape(kk // P, P, -1, P).transpose(2, 1, 0, 3))


def columns(v):
    v = np.asarray(v)
    return np.ascontiguousarray(v.reshape(-1, P).T)


def laid_out(x, mem, positions, mix_norm_w, w_in, gdn_conv_w, gdn_a_log, gdn_dt_bias, gdn_norm_w,
             gla_gk_up, gla_gk_bias, gla_norm_w, hgrn_lb_logits, hgrn_norm_w, w_out, xattn_norm_w,
             mem_norm_w, xattn_wq, xattn_wk, xattn_wv, xattn_wo, ffn_norm_w, ffn_up, ffn_conv_w,
             ffn_down, final_norm_w, c_2, mod_w_2, mod_b_2, norm_mix_pre_2, norm_mix_post_2,
             norm_ffn_pre_2, norm_ffn_post_2, ab_w_in_2, ab_conv_w_2, ab_conv_b_2, lru_w_r_2, lru_b_r_2,
             lru_w_i_2, lru_b_i_2, lru_lam_2, cmp_pe_k_2, cmp_pe_v_2, cmp_wk1_2, cmp_wk2_2, cmp_wv1_2,
             cmp_wv2_2, ab_w_out_2, sc_w_in_2, sc_conv_w_2, sc_conv_b_2, sc_w_out_2, ffn_w_gate_2,
             ffn_w_up_2, ffn_conv_w_2, ffn_conv_b_2, ffn_w_down_2):
    a = {}
    tables = constants()
    for i, (table, _) in enumerate(tables):
        a[f"consts_{i}"] = table
    wheres = [where for _, where in tables]
    a["masks"] = level_masks()

    def feature_major(v):
        return np.ascontiguousarray(v[0].T.reshape(KT, P, -1).transpose(1, 0, 2))

    a["x_t"], a["mem_t"] = feature_major(x), feature_major(mem)
    a["positions"] = np.ascontiguousarray(np.broadcast_to(positions, (P, T)))

    sizes = [256] * 7 + [4, 4, 256, 128, 128, 256, 16, 256] + [256] * 4
    parts = np.split(w_in[0], np.cumsum(sizes)[:-1], axis=1)
    (rq, rk, rv, rg, bq, bk, bv, ba, bb, bg, cq, ck, cv, c_lr, cg, dq, df, di, dg) = parts
    misc = np.zeros((D, P), np.float32)
    misc[:, 0:4], misc[:, 32:36], misc[:, 64:80] = ba, bb, c_lr
    a["w_mix_in"] = tiled(np.concatenate([rq, rk, rv, bv, cv, di, rg, bq, bk, bg, cg, dq, df, dg,
                                          cq, ck, misc], axis=1))
    a["w_mem_k"], a["w_mem_v"] = tiled(xattn_wk[0]), tiled(xattn_wv[0])
    a["w_mix_out"], a["w_att_q"], a["w_att_o"] = tiled(w_out[0]), tiled(xattn_wq[0]), tiled(xattn_wo[0])
    gate, val = tiled(ffn_up[0][:, :FF]), tiled(ffn_up[0][:, FF:])
    a["w_up_0"] = np.stack([gate, val], axis=1).reshape(2 * FT, P, KT, P)
    a["w_down_0"] = tiled(ffn_down[0])
    up = np.zeros((32, P), np.float32)
    up[0:16] = gla_gk_up[0]
    a["gla_up"] = up

    a["mod_w"] = np.ascontiguousarray(
        mod_w_2.reshape(2, KT, P, 16, 384).transpose(0, 3, 2, 1, 4).reshape(32, P, KT, 384))

    heads = [4 * (2 * gp + odd) + r for gp in range(2) for r in range(4) for odd in range(2)]
    order = np.concatenate([np.arange(HD) + HD * h for h in heads])
    sizes = [1024, 1024, 1024] + [256] * 6 + [48]
    parts = np.split(ab_w_in_2[0], np.cumsum(sizes)[:-1], axis=1)
    parts[2] = parts[2][:, order]
    a["w_ab_in"] = tiled(np.concatenate(parts, axis=1))
    wo = ab_w_out_2[0]
    a["w_ab_out"] = tiled(np.concatenate([wo[:1024], wo[1024:][order]], axis=0))
    for i in range(2):
        gate, val = tiled(ffn_w_gate_2[i]), tiled(ffn_w_up_2[i])
        a[f"w_up_{i + 1}"] = np.stack([gate, val], axis=1).reshape(2 * FT, P, KT, P)
        a[f"w_down_{i + 1}"] = tiled(ffn_w_down_2[i])
    b_part, c_part, v_part = (tiled(sc_w_in_2[0][:, i * D:(i + 1) * D]) for i in range(3))
    a["w_sc_in"] = np.stack([c_part, v_part, b_part], axis=1).reshape(3 * KT, P, KT, P)
    a["w_sc_out"] = tiled(sc_w_out_2[0])

    lru = np.zeros((P, 2, KT, P), np.float32)
    for g, w in enumerate((lru_w_r_2[0], lru_w_i_2[0])):
        for n in range(16):
            s = slice(64 * (n % 2), 64 * (n % 2) + 64)
            lru[s, g, n // 2, s] = w[n]
    a["lru_w"] = lru
    a["cmp_w1"] = np.ascontiguousarray(
        np.stack([w[0].reshape(16, P, P) for w in (cmp_wk1_2, cmp_wv1_2)]).transpose(2, 0, 1, 3))
    a["cmp_w2"] = np.ascontiguousarray(np.stack([cmp_wk2_2[0], cmp_wv2_2[0]], axis=1))

    v = {
        "mix_norm": columns(mix_norm_w), "att_norm": columns(xattn_norm_w), "mem_norm": columns(mem_norm_w),
        "ffn_norm": columns(ffn_norm_w), "final_norm": columns(final_norm_w),
        "gdn_conv": columns(gdn_conv_w[0]), "ffn_conv_0": columns(ffn_conv_w[0]),
        "gla_bias": columns(gla_gk_bias[0]),
        "gdn_norm": columns(np.tile(gdn_norm_w[0], 2)), "gla_norm": columns(np.tile(gla_norm_w[0], 2)),
        "hgrn_norm": columns(np.tile(hgrn_norm_w[0], 2)),
        "a_log": np.broadcast_to(gdn_a_log, (P, HEADS)), "dt_bias": np.broadcast_to(gdn_dt_bias, (P, HEADS)),
        "ab_conv": columns(ab_conv_w_2[0]), "ab_conv_b": columns(ab_conv_b_2),
        "lru_b_r": columns(lru_b_r_2), "lru_b_i": columns(lru_b_i_2), "lru_lam": columns(lru_lam_2),
        "sc_conv": columns(sc_conv_w_2[0]), "sc_conv_b": columns(sc_conv_b_2), "cond": columns(c_2),
        "pe_k": columns(cmp_pe_k_2), "pe_v": columns(cmp_pe_v_2),
    }
    for i in range(2):
        v[f"mix_pre_{i}"], v[f"mix_post_{i}"] = columns(norm_mix_pre_2[i]), columns(norm_mix_post_2[i])
        v[f"ffn_pre_{i}"], v[f"ffn_post_{i}"] = columns(norm_ffn_pre_2[i]), columns(norm_ffn_post_2[i])
        v[f"mod_b_{i}"] = columns(mod_b_2[i])
        v[f"ffn_conv_{i + 1}"] = columns(ffn_conv_w_2[i])
        v[f"ffn_conv_b_{i + 1}"] = columns(ffn_conv_b_2[i])
    at, vec_at = 0, {}
    for name, n in VECTORS.items():
        assert v[name].shape == (P, n), name
        vec_at[name] = (at, at + n)
        at += n
    a["vecs"] = np.ascontiguousarray(np.concatenate([v[name] for name in VECTORS], axis=1))
    return a, wheres, vec_at


def program(nc, arrays, wheres, vec_at, last_stage=None):
    dram = {name: nc.dram_tensor("in_" + name, v.shape, mybir.dt.from_np(v.dtype), kind="ExternalInput").ap()
            for name, v in arrays.items()}
    dram["out"] = nc.dram_tensor("out_t", (P, KT, T), F32, kind="ExternalOutput").ap()
    return build(nc, dram, wheres, vec_at, last_stage)


def kernel(**inputs):
    import concourse.bacc as bacc
    from concourse.bass_utils import run_bass_kernel_spmd

    arrays, wheres, vec_at = laid_out(**{name: np.asarray(v) for name, v in inputs.items()})
    nc = bacc.Bacc("TRN2", target_bir_lowering=False, num_devices=1)
    program(nc, arrays, wheres, vec_at)
    result = run_bass_kernel_spmd(nc, [{"in_" + name: v for name, v in arrays.items()}], core_ids=[0])
    out = result.results[0]["out_t"]
    return np.ascontiguousarray(out.transpose(2, 1, 0)).reshape(1, T, D)
```

```python
from contextlib import ExitStack

import numpy as np

import concourse.bass as bass
from concourse import mybir

ALU = mybir.AluOpType
ACT = mybir.ActivationFunctionType
F32 = mybir.dt.float32
F32R = mybir.dt.float32r
U32 = mybir.dt.uint32
I32 = mybir.dt.int32
AX_X = mybir.AxisListType.X

P = 128
T = 512
D = 1024
KT = D // P
MEM = 256
TT = T // P
FF = 2816
FT = FF // P
HEADS = 4
HD = 64
NQ = 16
NG = 4
NCMP = 31
NBLK = 8
EPS = 1e-6
NEG = -1e30
TWO_PI = 2.0 * np.pi

RING = 6
HIGH = 3
SLOT_KT = 8
BANKS = 8
PRODUCT_BANKS = 4

PRODUCTS = {
    "mix_in": (31, 8), "mix_out": (8, 8),
    "mem_k": (8, 8), "mem_v": (8, 8),
    "att_q": (8, 8), "att_o": (8, 8),
    "up_0": (2 * FT, 8), "down_0": (8, FT),
    "ab_in": (37, 8), "ab_out": (8, 16),
    "up_1": (2 * FT, 8), "down_1": (8, FT),
    "sc_in": (24, 8), "sc_out": (8, 8),
    "up_2": (2 * FT, 8), "down_2": (8, FT),
}

RQ, RK, RV, BV, CV, DI, RG, BQ, BK, BG, CG, DQ, DF, DG = range(0, 28, 2)
CQ, CK, MISC = 28, 29, 30
XR, GR, NQT, KC, VC, KS, VS, KW, VW, GL = 0, 8, 16, 24, 26, 28, 30, 32, 34, 36


def packed(tables):
    tables = {k: np.ascontiguousarray(v, dtype=np.float32) for k, v in tables.items()}
    at, where = 0, {}
    for k, v in tables.items():
        where[k] = (at, at + v.shape[1])
        at += v.shape[1]
    return np.concatenate(list(tables.values()), axis=1), where


def constants():
    part = np.arange(P)
    tok = np.arange(T)
    c = both = {}
    c["ident"] = np.eye(P)
    c["ones"] = np.ones((P, P))
    c["head_ones"] = (part[:, None] // HD == part[None, :] // HD) * 1.0
    c = first = {}
    rot = np.zeros((P, P))
    for d in range(P):
        if d % HD < HD // 2:
            rot[d + HD // 2, d] = -1.0
        else:
            rot[d - HD // 2, d] = 1.0
    c["rotate_half"] = rot
    c["upto"] = (part[:, None] <= part[None, :]) * 1.0
    c["scan_keep"] = np.broadcast_to((tok % P != 0) * 1.0, (P, T))
    freqs = (np.float32(10000.0) ** (-np.arange(0, HD, 2, dtype=np.float32) / HD)).astype(np.float32)
    c["freq"] = freqs[part % (HD // 2)][:, None]
    log_gamma = np.log(1.0 - np.exp2(-5.0 - np.arange(HEADS)))
    rel = tok[None, :] - part[:, None]
    for h in range(HEADS):
        c[f"decay{h}"] = np.where(rel >= 0, np.exp(log_gamma[h] * np.maximum(rel, 0)), 0.0) * HD ** -0.5
    c = second = {}
    rot = np.zeros((P, P))
    for d in range(P):
        if d % HD < 8:
            rot[d + 8, d] = -1.0
        elif d % HD < 16:
            rot[d - 8, d] = 1.0
    c["rotate_part"] = rot
    inv = (np.float32(500000.0) ** (-np.arange(8, dtype=np.float32) / 8)).astype(np.float32)
    ang = (tok[None, :].astype(np.float32) * inv[part % 8][:, None]).astype(np.float32).astype(np.float64)
    turned = (part % HD < 16)[:, None]
    c["rope_cos"] = np.where(turned, np.cos(ang), 1.0)
    c["rope_sin"] = np.where(turned, np.sin(ang), 0.0)
    c["causal"] = np.where(part[None, :] <= part[:, None], 0.0, NEG)
    near = part[:, None] + 256 - np.arange(384)[None, :]
    c["window"] = np.where((near >= 0) & (near < 256), 0.0, NEG)
    for i in range(TT):
        t = i * P + part[:, None]
        n = np.arange(32)[None, :]
        seen = (16 * n + 31 <= t) & (n < NCMP)
        c[f"cmp_bias{i}"] = np.where(seen, 0.0, NEG)
        c[f"cmp_seen{i}"] = seen * 1.0
        j = np.arange(NBLK)[None, :]
        forced = (j == 0) | (j == t // HD)
        c[f"block_bias{i}"] = np.where(64 * j <= t, np.where(forced, 1.0e4, 0.0), NEG)
    j, i = np.meshgrid(np.arange(NBLK), np.arange(NBLK), indexing="ij")
    c["earlier"] = np.broadcast_to((i < j).reshape(1, 64) * 1.0, (P, 64))
    return packed(both), packed(first), packed(second)


def level_masks():
    s, t = np.arange(P)[:, None], np.arange(P)[None, :]
    out = [((s // (2 * b) == t // (2 * b)) & (s % (2 * b) < b) & (t % (2 * b) >= b)) for b in LEVELS]
    out.append(s == t)
    return np.stack(out, axis=1).astype(np.float32)


LEVELS = (1, 2, 4, 8, 16, 32, 64)

VECTORS = {
    "mix_norm": KT, "att_norm": KT, "mem_norm": KT, "ffn_norm": KT, "final_norm": KT,
    "gdn_conv": 4 * 6, "gdn_norm": 1, "gla_norm": 1, "hgrn_norm": 1, "gla_bias": 1,
    "a_log": HEADS, "dt_bias": HEADS, "ffn_conv_0": 3 * 2 * FT,
    "mix_pre_0": KT, "mix_post_0": KT, "ffn_pre_0": KT, "ffn_post_0": KT,
    "mix_pre_1": KT, "mix_post_1": KT, "ffn_pre_1": KT, "ffn_post_1": KT,
    "ab_conv": 4 * KT, "ab_conv_b": KT, "lru_b_r": KT, "lru_b_i": KT, "lru_lam": KT,
    "sc_conv": 3 * KT, "sc_conv_b": KT,
    "ffn_conv_1": 3 * FT, "ffn_conv_b_1": FT, "ffn_conv_2": 3 * FT, "ffn_conv_b_2": FT,
    "mod_b": 96, "cond": KT, "pe_k": 16, "pe_v": 16,
}


class Link:

    def __init__(self, engine, semaphore):
        self.engine, self.semaphore, self.count = engine, semaphore, 0

    def __call__(self, instruction):
        self.count += 1
        instruction.then_inc(self.semaphore, 1)
        self.engine.wait_ge(self.semaphore, self.count)


class Kernel:

    def __init__(self, nc, ctx, dram):
        self.nc, self.ctx, self.dram = nc, ctx, dram
        self.place, self.aliases = {}, {}
        self.psum = ctx.enter_context(nc.psum_tensor("psum", [P, BANKS, T], F32))
        self.ring = self.sb("ring", [P, RING, SLOT_KT, P])
        self.high = self.sb("high", [P, HIGH, SLOT_KT, P])
        self.weights_landed = [ctx.enter_context(nc.semaphore(f"weights_landed{s}")) for s in range(RING)]
        self.weights_used = ctx.enter_context(nc.semaphore("weights_used"))
        self.weights_rounded = ctx.enter_context(nc.semaphore("weights_rounded"))
        self.weights_split = ctx.enter_context(nc.semaphore("weights_split"))
        self.next_split = 0
        self.stored = ctx.enter_context(nc.semaphore("stored"))
        self.stage_sems, self.in_use = ctx.enter_context(ExitStack()), []
        self.tiles, self.first_tile = [], {}
        for name, (n_out, kt) in PRODUCTS.items():
            self.first_tile[name] = len(self.tiles)
            for j in range(n_out):
                for k0 in range(0, kt, SLOT_KT):
                    self.tiles.append((name, j, k0, min(SLOT_KT, kt - k0)))

    def sem(self, name):
        self.in_use.append(self.stage_sems.enter_context(self.nc.semaphore(name)))
        return self.in_use[-1]

    def clear_stage_semaphores(self):
        nc, used = self.nc, self.in_use
        with nc.Block() as block:
            @block.gpsimd
            def _(pool):
                for semaphore in used:
                    pool.sem_clear(semaphore)
        self.stage_sems.close()
        self.in_use = []

    def sb(self, name, shape, dtype=F32, ctx=None):
        tensor = (ctx or self.ctx).enter_context(self.nc.sbuf_tensor(name, shape, dtype))
        self.place[tensor.name] = self.nc.sbuf_base - 4 * int(np.prod(shape[1:]))
        return tensor

    def rounded(self, ap):
        tensor = ap.tensor
        if tensor.name not in self.aliases:
            self.aliases[tensor.name] = self.nc.alloc_sbuf_tensor_at(
                f"rounded_{tensor.name}", list(tensor.shape), F32R, offset=self.place[tensor.name])
        return bass.AP(tensor=self.aliases[tensor.name], offset=ap.offset, ap=ap.ap)

    def const(self, name):
        for table, where in self.tables:
            if name in where:
                a, b = where[name]
                return table[:, a:b]

    def vec(self, name):
        a, b = self.vec_at[name]
        return self.vecs[:, a:b]

    def chunks(self, name):
        return -(-PRODUCTS[name][1] // SLOT_KT)

    def load_weights(self, sp, first, last):
        for i in range(first, min(last, len(self.tiles))):
            name, j, k0, n = self.tiles[i]
            if i >= RING:
                sp.wait_ge(self.weights_used, i - RING + 1)
            sp.dma_start(self.ring[:, i % RING, 0:n, :], self.dram["w_" + name][j, :, k0:k0 + n, :]
                         ).then_inc(self.weights_landed[i % RING], 16)

    def load_ahead(self, sp, name):
        first = self.first_tile[name]
        self.load_weights(sp, first + RING, first + PRODUCTS[name][0] * self.chunks(name) + RING)

    def product_done(self, name, j):
        return self.first_tile[name] + (j + 1) * self.chunks(name)

    def split_weights(self, dve, name, j):
        nc = self.nc
        last = min(self.first_tile[name] + (j + 1) * self.chunks(name) + 2,
                   self.first_tile[{"mix_in": "mix_out", "ab_in": "ab_out"}[name]]
                   if name in ("mix_in", "ab_in") else len(self.tiles))
        for i in range(self.next_split, last):
            n = self.tiles[i][3]
            raw, high = self.ring[:, i % RING, 0:n, :], self.high[:, i % HIGH, 0:n, :]
            dve.wait_ge(self.weights_landed[i % RING], 16 * (i // RING + 1))
            if i >= HIGH:
                dve.wait_ge(self.weights_used, i - HIGH + 1)
            nc.vector.tensor_copy(self.rounded(high), raw).then_inc(self.weights_rounded, 1)
            dve.wait_ge(self.weights_rounded, i + 1)
            nc.vector.tensor_tensor(self.rounded(raw), raw, self.rounded(high), ALU.subtract).then_inc(self.weights_split, 1)
        self.next_split = max(last, self.next_split)

    def product(self, pe, name, rhs, width, evacuated, between=None, inputs_ready=None):
        n_out, kt = PRODUCTS[name]
        i = self.first_tile[name]
        for j in range(n_out):
            if j >= PRODUCT_BANKS:
                pe.wait_ge(evacuated, j - PRODUCT_BANKS + 1)
            out = self.psum[:, j % PRODUCT_BANKS, 0:width]
            for k0 in range(0, kt, SLOT_KT):
                pe.wait_ge(self.weights_split, i + 1)
                n = min(SLOT_KT, kt - k0)
                for k in range(n):
                    if j == 0 and inputs_ready is not None:
                        pe.wait_ge(inputs_ready, k0 + k + 1)
                    w_high = self.rounded(self.high[:, i % HIGH, k, :])
                    w_low = self.rounded(self.ring[:, i % RING, k, :])
                    x_high, x_low = (self.rounded(x) for x in rhs(k0 + k))
                    self.nc.tensor.matmul(out, w_high, x_high, start=(k0 + k == 0), stop=False)
                    self.nc.tensor.matmul(out, w_high, x_low, start=False, stop=False)
                    last = self.nc.tensor.matmul(out, w_low, x_high, start=False, stop=(k0 + k == kt - 1))
                last.then_inc(self.weights_used, 1)
                i += 1
            if between is not None:
                between(j)

    def normed(self, kk):
        return self.n[:, kk, :], self.n_low[:, kk, :]




def split(k, link, high, value):
    link(k.nc.vector.tensor_copy(k.rounded(high), value))
    return k.nc.vector.tensor_tensor(k.rounded(value), value, k.rounded(high), ALU.subtract)


def prepare(k, name, src, gain, high, low, width=T, loads=()):
    nc = k.nc
    squared, added, steps, done = (k.sem(f"{name}_{s}") for s in ("squared", "added", "steps", "done"))
    with nc.Block() as block:
        @block.scalar
        def _(act):
            for j in range(KT):
                if j >= 2:
                    act.wait_ge(added, j - 1)
                nc.scalar.activation(k.squares[:, j % 2, 0:width], src[:, j, :], ACT.Square).then_inc(squared, 1)

        @block.gpsimd
        def _(pool):
            add_squares(k, pool, squared, added, width)

        @block.vector
        def _(dve):
            link = Link(dve, steps)
            for j in range(KT):
                link(nc.vector.tensor_scalar(low[:, j, :], src[:, j, :], gain[:, j:j + 1], None, ALU.mult))
                split(k, link, high[:, j, :], low[:, j, :]).then_inc(done, 1)


def add_squares(k, pool, squared, added, width=T):
    nc = k.nc
    for j in range(KT):
        pool.wait_ge(squared, j + 1)
        sq, total = k.squares[:, j % 2, 0:width], k.sum_sq[:, 0:width]
        if j == 0:
            nc.gpsimd.tensor_copy(total, sq).then_inc(added, 1)
        else:
            pool.wait_ge(added, j)
            nc.gpsimd.tensor_tensor(total, total, sq, ALU.add).then_inc(added, 1)


class Root:

    def __init__(self, k, name, width=T):
        self.k, self.width = k, width
        self.summed, self.var, self.root, self.done = (
            k.sem(f"{name}_{s}") for s in ("summed", "var", "root", "rstd"))
        self.bank, self.rstd = k.psum[:, BANKS - 1, 0:width], k.rstd[:, 0:width]

    def tensor(self):
        self.k.nc.tensor.matmul(self.bank, self.k.const("ones"), self.k.sum_sq[:, 0:self.width],
                                start=True, stop=True).then_inc(self.summed, 1)

    def vector(self, dve):
        dve.wait_ge(self.summed, 1)
        self.k.nc.vector.tensor_scalar(self.rstd, self.bank, 1.0 / D, EPS, ALU.mult, ALU.add
                                       ).then_inc(self.var, 1)
        dve.wait_ge(self.root, 1)
        self.k.nc.vector.reciprocal(self.rstd, self.rstd).then_inc(self.done, 1)
        dve.wait_ge(self.done, 1)

    def scalar(self, act):
        act.wait_ge(self.var, 1)
        self.k.nc.scalar.activation(self.rstd, self.rstd, ACT.Sqrt).then_inc(self.root, 1)


def boundary(k, name, first_gain, add, gain=None, shift=None, y=None):
    nc = k.nc
    first = Root(k, name + "_a")
    y = k.n if y is None else y
    renewed, squared, summed, var, root, scaled, shifted, steps, done = (
        k.sem(f"{name}_{s}") for s in ("renewed", "squared", "summed", "var", "root", "scaled", "shifted",
                                       "steps", "done"))
    total = k.psum[:, BANKS - 2, :]
    with nc.Block() as block:
        @block.tensor
        def _(pe):
            first.tensor()
            for j in range(KT if gain is not None else 0):
                pe.wait_ge(squared, j + 1)
                nc.tensor.matmul(total, k.const("ones"), k.squares[:, j % 2, :], start=(j == 0),
                                 stop=(j == KT - 1)).then_inc(summed, 1)

        @block.scalar
        def _(act):
            first.scalar(act)
            if gain is None:
                return
            for j in range(KT):
                act.wait_ge(renewed, j + 1)
                if j >= 2:
                    act.wait_ge(summed, j - 1)
                nc.scalar.activation(k.squares[:, j % 2, :], k.h[:, j, :], ACT.Square).then_inc(squared, 1)
            act.wait_ge(var, 1)
            nc.scalar.activation(k.rstd, k.rstd, ACT.Sqrt).then_inc(root, 1)
            for j in range(KT):
                act.wait_ge(scaled, j + 1)
                nc.scalar.activation(k.n_low[:, j, :], k.n_low[:, j, :], ACT.Identity,
                                     bias=shift[:, j:j + 1]).then_inc(shifted, 1)

        @block.vector
        def _(dve):
            link = Link(dve, steps)
            first.vector(dve)
            for j in range(KT):
                dst = y if add else k.h
                step = nc.vector.scalar_tensor_tensor(dst[:, j, :], dst[:, j, :], first_gain[:, j:j + 1],
                                                      k.rstd, ALU.mult, ALU.mult)
                if add:
                    link(step)
                    step = nc.vector.tensor_tensor(k.h[:, j, :], k.h[:, j, :], y[:, j, :], ALU.add)
                step.then_inc(renewed, 1)
            if gain is None:
                return
            dve.wait_ge(summed, KT)
            dve.wait_ge(renewed, KT)
            nc.vector.tensor_scalar(k.rstd, total, 1.0 / D, EPS, ALU.mult, ALU.add).then_inc(var, 1)
            dve.wait_ge(root, 1)
            link(nc.vector.reciprocal(k.rstd, k.rstd))
            for j in range(KT + 1):
                if j < KT:
                    nc.vector.scalar_tensor_tensor(k.n_low[:, j, :], k.h[:, j, :], gain[:, j:j + 1], k.rstd,
                                                   ALU.mult, ALU.mult).then_inc(scaled, 1)
                if j >= 1:
                    dve.wait_ge(shifted, j)
                    split(k, link, k.n[:, j - 1, :], k.n_low[:, j - 1, :]).then_inc(done, 1)


def load_inputs(k):
    nc = k.nc
    loaded = k.sem("inputs_loaded")
    with nc.Block() as block:
        @block.scalar
        def _(act):
            act.dma_start(k.tables[0][0][:], k.dram["consts_0"]).then_inc(loaded, 16)
            act.dma_start(k.tables[1][0][:], k.dram["consts_1"]).then_inc(loaded, 16)
            act.dma_start(k.masks[:], k.dram["masks"]).then_inc(loaded, 16)
            act.dma_start(k.vecs[:], k.dram["vecs"]).then_inc(loaded, 16)

        @block.sync
        def _(sp):
            sp.dma_start(k.h[:], k.dram["x_t"]).then_inc(loaded, 16)
            k.load_weights(sp, 0, RING)
            sp.wait_ge(loaded, 5 * 16)


def load(k, name, pairs):
    nc = k.nc
    loaded = k.sem(name + "_loaded")
    with nc.Block() as block:
        @block.sync
        def _(sp):
            for dst, src in pairs:
                sp.dma_start(dst, k.dram[src]).then_inc(loaded, 16)
            sp.wait_ge(loaded, 16 * len(pairs))


def memory_projections(k):
    nc = k.nc
    root = Root(k, "mem_root", MEM)
    for name, dst in (("mem_k", k.mem_k), ("mem_v", k.mem_vt)):
        out = k.sem(name + "_out")
        with nc.Block() as block:
            @block.sync
            def _(sp):
                k.load_ahead(sp, name)

            @block.tensor
            def _(pe):
                if name == "mem_k":
                    root.tensor()
                k.product(pe, name, lambda kk: (k.mem_high[:, kk, :], k.mem_low[:, kk, :]), MEM, out)

            @block.scalar
            def _(act):
                if name == "mem_k":
                    root.scalar(act)

            @block.vector
            def _(dve):
                k.split_weights(dve, name, -1)
                if name == "mem_k":
                    root.vector(dve)
                for j in range(KT):
                    k.split_weights(dve, name, j)
                    dve.wait_ge(k.weights_used, k.product_done(name, j))
                    nc.vector.tensor_tensor(dst[:, j, :], k.psum[:, j % PRODUCT_BANKS, 0:MEM],
                                            k.rstd[:, 0:MEM], ALU.mult).then_inc(out, 1)

    turn(k, "mem_v_turn", [([k.mem_vt[:, 4 * g + i, m * P:(m + 1) * P] for i in range(4)],
                            k.mem_v[:, m, g * T:(g + 1) * T]) for m in range(2) for g in range(2)])


def turn(k, name, groups):
    nc = k.nc
    turned, kept = k.sem(name + "_turned"), k.sem(name + "_kept")
    with nc.Block() as block:
        @block.tensor
        def _(pe):
            for g, (pieces, _) in enumerate(groups):
                if g >= 4:
                    pe.wait_ge(kept, g - 3)
                for i, piece in enumerate(pieces):
                    last = nc.tensor.transpose(k.psum[:, g % 4, i * P:(i + 1) * P], piece, k.const("ident"))
                last.then_inc(turned, 1)

        @block.scalar
        def _(act):
            for g, (pieces, dst) in enumerate(groups):
                act.wait_ge(turned, g + 1)
                nc.scalar.copy(dst, k.psum[:, g % 4, 0:len(pieces) * P]).then_inc(kept, 1)


def head_norm(k, name, items, mean, highs=None):
    nc = k.nc
    squared, summed = k.sem(name + "_squared"), k.sem(name + "_summed")
    var_ready, root_ready, steps = k.sem(name + "_var"), k.sem(name + "_root"), k.sem(name + "_steps")
    with nc.Block() as block:
        @block.scalar
        def _(act):
            for i, (src, _, _, _) in enumerate(items):
                nc.scalar.activation(k.head_sq[:, i, :], src, ACT.Square).then_inc(squared, 1)
            for i in range(len(items)):
                act.wait_ge(var_ready, i + 1)
                nc.scalar.activation(k.head_sq[:, i, :], k.head_sq[:, i, :], ACT.Sqrt).then_inc(root_ready, 1)

        @block.tensor
        def _(pe):
            for i in range(len(items)):
                pe.wait_ge(squared, i + 1)
                nc.tensor.matmul(k.psum[:, i, :], k.const("head_ones"), k.head_sq[:, i, :],
                                 start=True, stop=True).then_inc(summed, 1)

        @block.vector
        def _(dve):
            link = Link(dve, steps)
            for i in range(len(items)):
                dve.wait_ge(summed, i + 1)
                nc.vector.tensor_scalar(k.head_sq[:, i, :], k.psum[:, i, :], mean, EPS,
                                        ALU.mult, ALU.add).then_inc(var_ready, 1)
            for i, (src, dst, scale, gate) in enumerate(items):
                dve.wait_ge(root_ready, i + 1)
                link(nc.vector.reciprocal(k.head_sq[:, i, :], k.head_sq[:, i, :]))
                if gate is not None:
                    link(nc.vector.tensor_tensor(k.head_sq[:, i, :], k.head_sq[:, i, :], gate, ALU.mult))
                link(nc.vector.scalar_tensor_tensor(dst, src, scale, k.head_sq[:, i, :], ALU.mult, ALU.mult))
                if highs is not None:
                    link(split(k, link, highs[i], dst))


class Modulation:

    def __init__(self, k, name, first, n):
        self.k, self.first, self.n = k, first, n
        self.ready, self.summed, self.steps = (k.sem(f"{name}_{s}") for s in ("mod_ready", "mod_summed",
                                                                              "mod_steps"))

    def load(self, sp, c):
        if c < self.n:
            if c >= 2:
                sp.wait_ge(self.ready, c - 1)
            i = self.first + c
            sp.dma_start(self.k.mod_w[:, i % 2], self.k.dram["mod_w"][i]).then_inc(self.k.mod_loaded[i % 2], 16)

    def vector(self, dve, link, c):
        if c >= self.n:
            return
        nc, i = self.k.nc, self.first + c
        dve.wait_ge(self.k.mod_loaded[i % 2], 16 * (i // 2 + 1))
        if c >= 2:
            dve.wait_ge(self.summed, c - 1)
        acc, w, cond = self.k.mod_acc[:, i % 2, :], self.k.mod_w[:, i % 2], self.k.cond
        link(nc.vector.tensor_scalar(acc, w[:, 0, :], cond[:, 0:1], None, ALU.mult))
        for r in range(1, KT):
            step = nc.vector.scalar_tensor_tensor(acc, w[:, r, :], cond[:, r:r + 1], acc, ALU.mult, ALU.add)
            if r < KT - 1:
                link(step)
        step.then_inc(self.ready, 1)

    def tensor(self, pe, c):
        if not 0 <= c < self.n:
            return
        pe.wait_ge(self.ready, c + 1)
        for b in range(2):
            col = 2 * c + b
            last = self.k.nc.tensor.matmul(self.k.psum[:, BANKS - 2, col:col + 1],
                                           self.k.mod_acc[:, (self.first + c) % 2, b * P:(b + 1) * P],
                                           self.k.const("ones")[:, 0:1], start=True, stop=True)
        last.then_inc(self.summed, 1)

    def keep(self, dve):
        dve.wait_ge(self.summed, self.n)
        a, b = 2 * self.first, 2 * (self.first + self.n)
        self.k.nc.vector.tensor_tensor(self.k.mod_cols[:, a:b], self.k.psum[:, BANKS - 2, 0:b - a],
                                       self.k.vec("mod_b")[:, a:b], ALU.add)


def mixer_projection(k):
    nc = k.nc
    name, n_out = "mix_in", PRODUCTS["mix_in"][0]
    root = Root(k, "mix_in_root")
    mod = Modulation(k, "mix_in", 0, 24)
    out, gated, padded, steps, convolved = (k.sem("mix_in_" + s) for s in ("out", "gated", "padded", "steps",
                                                                           "convolved"))
    conv_tiles = [BQ, BQ + 1, BK, BK + 1, BV, BV + 1]
    gates = [t + i for t in (RG, BG, CG, DG) for i in range(2)]
    with nc.Block() as block:
        @block.sync
        def _(sp):
            first = k.first_tile[name] + RING
            for j in range(n_out):
                k.load_weights(sp, first + j, first + j + 1)
                mod.load(sp, j)

        @block.tensor
        def _(pe):
            root.tensor()
            k.product(pe, name, k.normed, T, out, between=lambda j: mod.tensor(pe, j - 2))

        @block.scalar
        def _(act):
            root.scalar(act)
            for j in range(n_out):
                act.wait_ge(out, j + 1)
                if j in gates:
                    nc.scalar.activation(k.z[:, j, :], k.z[:, j, :], ACT.Silu)
            for i, j in enumerate(conv_tiles):
                act.wait_ge(convolved, i + 1)
                nc.scalar.activation(k.z[:, j, :], k.z[:, j, :], ACT.Silu)

        @block.vector
        def _(dve):
            link = Link(dve, steps)
            link(nc.vector.memset(k.conv_in[:, :, 0:3], 0.0))
            w = k.vec("gdn_conv")
            k.split_weights(dve, name, -1)
            root.vector(dve)
            for j in range(n_out):
                k.split_weights(dve, name, j)
                dve.wait_ge(k.weights_used, k.product_done(name, j))
                bank = k.psum[:, j % PRODUCT_BANKS, :]
                if j in conv_tiles:
                    nc.vector.tensor_tensor(k.conv_in[:, conv_tiles.index(j), 3:3 + T], bank, k.rstd, ALU.mult
                                            ).then_inc(out, 1)
                else:
                    scale = (HD // 2) ** -0.5 if j == CQ else 1.0
                    nc.vector.scalar_tensor_tensor(k.z[:, j, :], bank, scale, k.rstd, ALU.mult, ALU.mult
                                                   ).then_inc(out, 1)
                mod.vector(dve, link, j)
            for i, j in enumerate(conv_tiles):
                dve.wait_ge(out, j + 1)
                link(nc.vector.tensor_scalar(k.z[:, j, :], k.conv_in[:, i, 0:T], w[:, i:i + 1], None, ALU.mult))
                for tap in range(1, 4):
                    step = nc.vector.scalar_tensor_tensor(
                        k.z[:, j, :], k.conv_in[:, i, tap:tap + T], w[:, 6 * tap + i:6 * tap + i + 1],
                        k.z[:, j, :], ALU.mult, ALU.add)
                    if tap < 3:
                        link(step)
                step.then_inc(convolved, 1)
            mod.keep(dve)


def rotary(k):
    nc = k.nc
    C1 = 6.28125
    C2 = float(np.frombuffer((np.frombuffer(np.float32(TWO_PI - C1).tobytes(), np.uint32)
                              & np.uint32(0xFFFFF000)).tobytes(), np.float32)[0])
    C3 = float(TWO_PI - C1 - C2)
    ROUND = 1.5 * 2.0 ** 23
    steps, reduced, tables, turned = (k.sem("rotary_steps"), k.sem("rotary_reduced"), k.sem("rotary_tables"),
                                      k.sem("rotary_turned"))
    asteps = k.sem("rotary_asteps")
    ang, n, cos, sin, tmp = (k.scratch[:, i, :] for i in range(5))
    tiles = (RQ, RQ + 1, RK, RK + 1)
    with nc.Block() as block:
        @block.tensor
        def _(pe):
            for i, j in enumerate(tiles):
                nc.tensor.matmul(k.psum[:, i, :], k.const("rotate_half"), k.z[:, j, :],
                                 start=True, stop=True).then_inc(turned, 1)

        @block.scalar
        def _(act):
            link = Link(act, asteps)
            act.wait_ge(reduced, 1)
            nc.scalar.activation(sin, ang, ACT.Sin).then_inc(tables, 1)
            link(nc.scalar.activation(cos, ang, ACT.Abs))
            nc.scalar.activation(cos, cos, ACT.Sin, bias=k.half_pi[:, 0:1], scale=-1.0).then_inc(tables, 1)

        @block.vector
        def _(dve):
            link = Link(dve, steps)
            link(nc.vector.memset(k.half_pi[:], float(np.pi / 2)))
            link(nc.vector.tensor_copy(ang, k.positions[:]))
            link(nc.vector.tensor_scalar(ang, ang, k.const("freq"), None, ALU.mult))
            link(nc.vector.tensor_scalar(n, ang, 1.0 / TWO_PI, ROUND, ALU.mult, ALU.add))
            link(nc.vector.tensor_scalar(n, n, ROUND, None, ALU.subtract))
            for c in (C1, C2, C3):
                link(nc.vector.scalar_tensor_tensor(ang, n, -c, ang, ALU.mult, ALU.add))
            nc.vector.tensor_scalar(ang, ang, 3.141592, -3.141592, ALU.min, ALU.max).then_inc(reduced, 1)
            dve.wait_ge(tables, 2)
            for i, j in enumerate(tiles):
                dve.wait_ge(turned, i + 1)
                link(nc.vector.tensor_tensor(tmp, k.psum[:, i, :], sin, ALU.mult))
                link(nc.vector.tensor_tensor(k.z[:, j, :], k.z[:, j, :], cos, ALU.mult))
                link(nc.vector.tensor_tensor(k.z[:, j, :], k.z[:, j, :], tmp, ALU.add))


def head_rows(h):
    return slice(HD * (h % 2), HD * (h % 2) + HD)


def retention(k):
    nc = k.nc
    scored, weighted, mixed = k.sem("ret_scored"), k.sem("ret_weighted"), k.sem("ret_mixed")
    work = [(h, j) for h in range(HEADS) for j in range(TT)]
    with nc.Block() as block:
        @block.tensor
        def _(pe):
            def scores(i):
                h, j = work[i]
                rows = head_rows(h)
                if i >= 4:
                    pe.wait_ge(weighted, i - 3)
                nc.tensor.matmul(k.psum[:, i % 4, 0:T - j * P], k.z[rows, RK + h // 2, j * P:(j + 1) * P],
                                 k.z[rows, RQ + h // 2, j * P:T], start=True, stop=True).then_inc(scored, 1)

            scores(0)
            scores(1)
            for i, (h, j) in enumerate(work):
                if i + 2 < len(work):
                    scores(i + 2)
                pe.wait_ge(weighted, i + 1)
                nc.tensor.matmul(k.psum[head_rows(h), 4 + h // 2, j * P:T],
                                 k.v_tok[:, 0, j, h * HD:(h + 1) * HD], k.scratch[:, i % 4, 0:T - j * P],
                                 start=(j == 0), stop=(j == TT - 1)).then_inc(mixed, 1)

        @block.vector
        def _(dve):
            for i, (h, j) in enumerate(work):
                dve.wait_ge(scored, i + 1)
                if i >= 4:
                    dve.wait_ge(mixed, i - 3)
                nc.vector.tensor_tensor(k.scratch[:, i % 4, 0:T - j * P], k.psum[:, i % 4, 0:T - j * P],
                                        k.const(f"decay{h}")[:, 0:T - j * P], ALU.mult).then_inc(weighted, 1)

        @block.scalar
        def _(act):
            for m in range(2):
                act.wait_ge(mixed, 2 * TT * (m + 1))
                nc.scalar.copy(k.o[:, m, :], k.psum[:, 4 + m, :])


def log_decays(k):
    nc = k.nc
    up, x_ready, logs, negs, steps, asteps, cum = (
        k.sem("dec_up"), k.sem("dec_x"), k.sem("dec_logs"), k.sem("dec_negs"), k.sem("dec_steps"),
        k.sem("dec_asteps"), k.sem("dec_cum"))
    tmp = [k.scratch[:, i, :] for i in range(3)]
    low = [k.scratch[:, 3 + i, :] for i in range(3)]
    src = [low[0], k.z[:, DF, :], k.z[:, DF + 1, :]]
    with nc.Block() as block:
        @block.tensor
        def _(pe):
            nc.tensor.matmul(k.psum[:, 0, :], k.gla_up[64:96, :], k.z[64:96, MISC, :],
                             start=True, stop=True).then_inc(up, 1)

        @block.scalar
        def _(act):
            link = Link(act, asteps)
            act.wait_ge(x_ready, 1)
            for i in range(3):
                link(nc.scalar.activation(tmp[i], src[i], ACT.Abs))
            for i in range(3):
                link(nc.scalar.activation(tmp[i], tmp[i], ACT.Exp, scale=-1.0))
            for i in range(3):
                nc.scalar.activation(tmp[i], tmp[i], ACT.Ln, bias=1.0).then_inc(logs, 1)
            act.wait_ge(negs, 3)
            for i in (1, 2):
                nc.scalar.activation(k.z[:, DF + i - 1, :], src[i], ACT.Sigmoid, scale=-1.0)

        @block.vector
        def _(dve):
            link = Link(dve, steps)
            dve.wait_ge(up, 1)
            nc.vector.tensor_scalar(low[0], k.psum[:, 0, :], k.vec("gla_bias"), None, ALU.add).then_inc(x_ready, 1)
            dve.wait_ge(x_ready, 1)
            for i in range(3):
                dve.wait_ge(logs, i + 1)
                nc.vector.scalar_tensor_tensor(low[i], src[i], 0.0, tmp[i], ALU.min, ALU.subtract
                                               ).then_inc(negs, 1)
            dve.wait_ge(negs, 3)
            link(nc.vector.tensor_scalar(low[0], low[0], 1.0 / 16.0, None, ALU.mult))
            for i in range(3):
                nc.vector.tensor_tensor_scan(k.cum[:, i, :], k.const("scan_keep"), low[i], 0.0,
                                             ALU.mult, ALU.add).then_inc(cum, 1)


def gated_scores(k, name, cum, q, key, width, probs):
    nc = k.nc
    heads = P // width
    nl = len(LEVELS) + 1
    diffed, decayed, qs_ready, ks_ready, scored, picked, steps, asteps, zeroed = (
        k.sem(f"{name}_{s}") for s in ("diffed", "decayed", "qs", "ks", "scored", "picked", "steps",
                                       "asteps", "zeroed"))
    e = [k.scratch[:, i, :] for i in range(2)]
    qs = [k.scratch[:, 2 + i, :] for i in range(2)]
    ks = [k.scratch[:, 4 + i, :] for i in range(2)]

    def diagonal(h):
        return probs[h].rearrange("p (c x) -> p c x", x=T + P)[:, :, 0:P]

    with nc.Block() as block:
        @block.vector
        def _(dve):
            def difference(n):
                if n >= 2:
                    dve.wait_ge(qs_ready, n - 1)
                    dve.wait_ge(ks_ready, n - 1)
                b = LEVELS[n]
                g = cum.rearrange("p (c x) -> p c x", x=2 * b)
                nc.vector.tensor_tensor(e[n % 2].rearrange("p (c x) -> p c x", x=2 * b), g,
                                        g[:, :, b - 1:b].broadcast_to([P, T // (2 * b), 2 * b]),
                                        ALU.subtract).then_inc(diffed, 1)

            difference(0)
            for n in range(nl):
                if n < nl - 1:
                    if n < nl - 2:
                        difference(n + 1)
                    dve.wait_ge(decayed, n + 1)
                    if n >= 2:
                        dve.wait_ge(scored, heads * (n - 1))
                    nc.vector.tensor_tensor(qs[n % 2], q, e[n % 2], ALU.mult).then_inc(qs_ready, 1)
                if n == 0:
                    dve.wait_ge(zeroed, heads)
                for h in range(heads):
                    dve.wait_ge(scored, heads * n + h + 1)
                    if n:
                        dve.wait_ge(picked, heads * (n - 1) + h + 1)
                    nc.vector.copy_predicated(
                        diagonal(h), k.masks[:, n:n + 1, :].bitcast(U32).broadcast_to([P, TT, P]),
                        k.psum[:, (n % 2) * heads + h, :].rearrange("p (c x) -> p c x", x=P)).then_inc(picked, 1)

        @block.scalar
        def _(act):
            link = Link(act, asteps)
            for n in range(nl - 1):
                act.wait_ge(diffed, n + 1)
                link(nc.scalar.activation(e[n % 2], e[n % 2], ACT.Abs))
                nc.scalar.activation(e[n % 2], e[n % 2], ACT.Exp, scale=-1.0).then_inc(decayed, 1)

        @block.gpsimd
        def _(pool):
            for h in range(heads):
                nc.gpsimd.memset(probs[h], 0.0).then_inc(zeroed, 1)
            for n in range(nl - 1):
                pool.wait_ge(decayed, n + 1)
                if n >= 2:
                    pool.wait_ge(scored, heads * (n - 1))
                nc.gpsimd.tensor_tensor(ks[n % 2], key, e[n % 2], ALU.mult).then_inc(ks_ready, 1)

        @block.tensor
        def _(pe):
            for n in range(nl):
                if n < nl - 1:
                    pe.wait_ge(qs_ready, n + 1)
                    pe.wait_ge(ks_ready, n + 1)
                    a, b = ks[n % 2], qs[n % 2]
                else:
                    a, b = key, q
                if n >= 2:
                    pe.wait_ge(picked, heads * (n - 1))
                for c in range(TT):
                    for h in range(heads):
                        rows = slice(width * h, width * (h + 1))
                        last = nc.tensor.matmul(k.psum[:, (n % 2) * heads + h, c * P:(c + 1) * P],
                                                a[rows, c * P:(c + 1) * P], b[rows, c * P:(c + 1) * P],
                                                start=True, stop=True)
                        if c == TT - 1:
                            last.then_inc(scored, 1)

    fwd, bwd, qg, kg, q_late = (k.scratch[:, i, :] for i in range(5))
    k_early = k.scratch[:, 5, 0:P]
    ends, factors, grown, crossed, kept = (k.sem(f"{name}_{s}") for s in
                                           ("ends", "factors", "grown", "crossed", "kept"))
    with nc.Block() as block:
        @block.vector
        def _(dve):
            g = cum.rearrange("p (c x) -> p c x", x=P)
            nc.vector.tensor_tensor(bwd.rearrange("p (c x) -> p c x", x=P),
                                    g[:, :, P - 1:P].broadcast_to([P, TT, P]), g, ALU.subtract
                                    ).then_inc(ends, 1)
            dve.wait_ge(factors, 2)
            nc.vector.tensor_tensor(qg, q, fwd, ALU.mult).then_inc(grown, 1)
            nc.vector.tensor_tensor(kg, key, bwd, ALU.mult).then_inc(grown, 1)
            dve.wait_ge(grown, 2)
            nc.vector.tensor_copy(q_late[:, 0:P], qg[:, 2 * P:3 * P]).then_inc(grown, 1)
            nc.vector.tensor_scalar(q_late[:, P:2 * P], qg[:, 3 * P:T], fwd[:, 3 * P - 1:3 * P], None,
                                    ALU.mult).then_inc(grown, 1)
            nc.vector.tensor_scalar(k_early, kg[:, 0:P], fwd[:, 2 * P - 1:2 * P], None,
                                    ALU.mult).then_inc(grown, 1)

        @block.scalar
        def _(act):
            nc.scalar.activation(fwd, cum, ACT.Exp).then_inc(factors, 1)
            act.wait_ge(ends, 1)
            nc.scalar.activation(bwd, bwd, ACT.Exp).then_inc(factors, 1)
            for h in range(heads):
                act.wait_ge(crossed, h + 1)
                a, b = k.psum[:, (2 * h) % 8, :], k.psum[:, (2 * h + 1) % 8, :]
                nc.scalar.copy(probs[h][:, P:2 * P], a[:, 0:P])
                nc.scalar.copy(probs[h][:, 2 * T + 3 * P:3 * T], a[:, P:2 * P])
                nc.scalar.copy(probs[h][:, 2 * P:T], a[:, 2 * P:T])
                nc.scalar.copy(probs[h][:, T + 2 * P:2 * T], b[:, 0:2 * P]).then_inc(kept, 1)

        @block.tensor
        def _(pe):
            pe.wait_ge(grown, 5)
            for h in range(heads):
                rows = slice(width * h, width * (h + 1))
                a, b = k.psum[:, 2 * h, :], k.psum[:, 2 * h + 1, :]
                nc.tensor.matmul(a[:, 0:P], kg[rows, 0:P], qg[rows, P:2 * P], start=True, stop=True)
                nc.tensor.matmul(a[:, P:2 * P], kg[rows, 2 * P:3 * P], qg[rows, 3 * P:T], start=True, stop=True)
                nc.tensor.matmul(a[:, 2 * P:T], k_early[rows, :], q_late[rows, 0:2 * P], start=True, stop=True)
                nc.tensor.matmul(b[:, 0:2 * P], kg[rows, P:2 * P], q_late[rows, 0:2 * P],
                                 start=True, stop=True).then_inc(crossed, 1)


def mix_values(k, name, mixer, probs):
    nc = k.nc
    mixed = k.sem(name + "_mixed")
    with nc.Block() as block:
        @block.tensor
        def _(pe):
            for h in range(HEADS):
                for j in range(TT):
                    last = nc.tensor.matmul(k.psum[head_rows(h), h // 2, j * P:T],
                                            k.v_tok[:, mixer, j, h * HD:(h + 1) * HD],
                                            probs[h][:, j * (T + P):(j + 1) * T],
                                            start=(j == 0), stop=(j == TT - 1))
                last.then_inc(mixed, 1)

        @block.scalar
        def _(act):
            for m in range(2):
                act.wait_ge(mixed, 2 * (m + 1))
                nc.scalar.copy(k.o[:, 2 * mixer + m, :], k.psum[:, m, :])


def delta_prepare(k):
    nc = k.nc
    aready, steps, asteps, gs, spread = (k.sem("dp_" + s) for s in ("a", "steps", "asteps", "g", "spread"))
    done = k.sem("dp_done")
    tok = k.misc_tok
    x, ex, pos = (k.small[:, i, :].rearrange("p (c h) -> p c h", h=HEADS) for i in range(3))
    g_tok = k.g_tok.rearrange("p (c h) -> p c h", h=HEADS)
    with nc.Block() as block:
        @block.vector
        def _(dve):
            link = Link(dve, steps)
            link(nc.vector.tensor_tensor(x, tok[:, :, 0:HEADS],
                                         k.vec("dt_bias").unsqueeze(1).broadcast_to([P, TT, HEADS]), ALU.add))
            nc.vector.tensor_scalar(pos, x, 0.0, None, ALU.max).then_inc(aready, 1)
            dve.wait_ge(asteps, 5)
            link(nc.vector.tensor_tensor(pos, pos, ex, ALU.add))
            link(nc.vector.tensor_tensor(pos, pos, k.small[:, 3, 0:HEADS].unsqueeze(1)
                                         .broadcast_to([P, TT, HEADS]), ALU.mult))
            nc.vector.tensor_scalar(g_tok, pos, -1.0, None, ALU.mult).then_inc(gs, 1)

        @block.scalar
        def _(act):
            link = Link(act, asteps)
            link(nc.scalar.activation(k.small[:, 3, 0:HEADS], k.vec("a_log"), ACT.Exp))
            act.wait_ge(aready, 1)
            link(nc.scalar.activation(ex, x, ACT.Abs))
            link(nc.scalar.activation(ex, ex, ACT.Exp, scale=-1.0))
            link(nc.scalar.activation(ex, ex, ACT.Ln, bias=1.0))
            link(nc.scalar.activation(k.beta.rearrange("p (c h) -> p c h", h=HEADS), tok[:, :, 32:32 + HEADS],
                                      ACT.Sigmoid))
            act.wait_ge(spread, 5)
            link(nc.scalar.copy(k.gc_tok[:], k.psum[:, 7, 0:16]))
            link(nc.scalar.activation(k.gamma_tok[:], k.psum[:, 7, 0:16], ACT.Exp))
            for h in range(HEADS):
                nc.scalar.activation(k.gamma[:, h, :], k.psum[:, h, :], ACT.Exp).then_inc(done, 1)

        @block.tensor
        def _(pe):
            pe.wait_ge(gs, 1)
            nc.tensor.matmul(k.psum[:, 7, 0:16], k.const("upto"), k.g_tok[:], start=True, stop=True
                             ).then_inc(spread, 1)
            for h in range(HEADS):
                for c in range(TT):
                    col = k.g_tok[:, c * HEADS + h:c * HEADS + h + 1]
                    last = nc.tensor.matmul(k.psum[:, h, c * P:(c + 1) * P], col.broadcast_to([P, P]),
                                            k.const("upto"), start=True, stop=True)
                last.then_inc(spread, 1)

    limited, risen, masked, dsteps = (k.sem("dr_" + s) for s in ("limited", "risen", "masked", "steps"))
    with nc.Block() as block:
        @block.vector
        def _(dve):
            link = Link(dve, dsteps)
            for h in range(HEADS):
                for c in range(TT):
                    i = c * HEADS + h
                    nc.vector.tensor_scalar(k.ratio[:, h, c * P:(c + 1) * P], k.psum[:, h, c * P:(c + 1) * P],
                                            k.gc_tok[:, i:i + 1], 0.0, ALU.subtract, ALU.min).then_inc(limited, 1)
            for h in range(HEADS):
                last = nc.vector.tensor_tensor(
                    k.tail.rearrange("p (c h) -> p c h", h=HEADS)[:, :, h:h + 1],
                    k.psum[:, h, :].rearrange("p (c x) -> p c x", x=P)[:, :, P - 1:P],
                    k.gc_tok.rearrange("p (c h) -> p c h", h=HEADS)[:, :, h:h + 1], ALU.subtract)
                last.then_inc(limited, 1)
            for h in range(HEADS):
                dve.wait_ge(risen, h + 2)
                tri = k.const("upto").unsqueeze(1).broadcast_to([P, TT, P])
                r = k.ratio[:, h, :].rearrange("p (c x) -> p c x", x=P)
                nc.vector.tensor_tensor(r, r, tri, ALU.mult).then_inc(masked, 1)
            kt = k.k_tok.rearrange("p c (h d) -> p (c h) d", d=HD)
            nc.vector.tensor_tensor(kt, kt, k.tail.unsqueeze(2).broadcast_to([P, 16, HD]), ALU.mult
                                    ).then_inc(masked, 1)
            for h in range(HEADS):
                rows = head_rows(h)
                nc.vector.tensor_tensor(k.qg[rows, h // 2, :], k.z[rows, BQ + h // 2, :], k.gamma[rows, h, :],
                                        ALU.mult).then_inc(masked, 1)
                nc.vector.tensor_copy(
                    k.whole[rows, h // 2, :].unsqueeze(2),
                    k.gamma[rows, h, :].rearrange("p (c x) -> p c x", x=P)[:, :, P - 1:P]).then_inc(masked, 1)

        @block.scalar
        def _(act):
            act.wait_ge(limited, 20)
            nc.scalar.activation(k.tail[:], k.tail[:], ACT.Exp).then_inc(risen, 1)
            for h in range(HEADS):
                nc.scalar.activation(k.ratio[:, h, :], k.ratio[:, h, :], ACT.Exp).then_inc(risen, 1)


def delta_inverse(k):
    nc = k.nc
    scored, weighted, beta_done = k.sem("di_scored"), k.sem("di_weighted"), k.sem("di_beta")
    with nc.Block() as block:
        @block.tensor
        def _(pe):
            for kind in range(2):
                for h in range(HEADS):
                    rows, tile = head_rows(h), h // 2
                    for c in range(TT):
                        cols = slice(c * P, (c + 1) * P)
                        last = nc.tensor.matmul(k.psum[:, kind * 4 + h, cols], k.z[rows, BK + tile, cols],
                                                k.z[rows, (BK if kind == 0 else BQ) + tile, cols],
                                                start=True, stop=True)
                    last.then_inc(scored, 1)

        @block.vector
        def _(dve):
            for h in range(HEADS):
                dve.wait_ge(scored, h + 1)
                nc.vector.tensor_tensor(k.nt[:, h, :], k.psum[:, h, :], k.ratio[:, h, :], ALU.mult
                                        ).then_inc(weighted, 1)
            for h in range(HEADS):
                dve.wait_ge(scored, HEADS + h + 1)
                dve.wait_ge(beta_done, h + 1)
                nc.vector.tensor_tensor(k.ratio[:, h, :], k.psum[:, 4 + h, :], k.ratio[:, h, :], ALU.mult
                                        ).then_inc(weighted, 1)

        @block.scalar
        def _(act):
            for h in range(HEADS):
                act.wait_ge(weighted, h + 1)
                for c in range(TT):
                    i = c * HEADS + h
                    cols = slice(c * P, (c + 1) * P)
                    last = nc.scalar.activation(k.nt[:, h, cols], k.nt[:, h, cols], ACT.Copy,
                                                scale=k.beta[:, i:i + 1])
                last.then_inc(beta_done, 1)

    picked, q_ready, q_kept, xs, x_new, xt_new, started = (
        k.sem("dx_" + s) for s in ("picked", "q", "q_kept", "xs", "x_new", "xt_new", "started"))

    def blocks(a):
        return a.rearrange("p (c x) -> p c x", x=P)

    with nc.Block() as block:
        @block.gpsimd
        def _(pool):
            for n in range(len(LEVELS)):
                for h in range(HEADS):
                    i = n * HEADS + h
                    if i >= 4:
                        pool.wait_ge(q_ready, i - 3)
                    nc.gpsimd.tensor_tensor(blocks(k.nb[:, h, :]), blocks(k.nt[:, h, :]),
                                            k.masks[:, n:n + 1, :].broadcast_to([P, TT, P]), ALU.mult
                                            ).then_inc(picked, 1)

        @block.tensor
        def _(pe):
            for n in range(len(LEVELS)):
                for h in range(HEADS):
                    i = n * HEADS + h
                    pe.wait_ge(picked, i + 1)
                    if n == 0:
                        pe.wait_ge(started, 1)
                    else:
                        pe.wait_ge(x_new, i - 3)
                    for c in range(TT):
                        cols = slice(c * P, (c + 1) * P)
                        last = nc.tensor.matmul(k.psum[:, h, cols], k.nb[:, h, cols], k.inv_n[:, h, cols],
                                                start=True, stop=True)
                    last.then_inc(q_ready, 1)
                for h in range(HEADS):
                    i = n * HEADS + h
                    pe.wait_ge(q_kept, i + 1)
                    if i >= 1:
                        pe.wait_ge(x_new, i)
                        pe.wait_ge(xt_new, i)
                    for c in range(TT):
                        cols = slice(c * P, (c + 1) * P)
                        nc.tensor.matmul(k.psum[:, 4 + h % 2, cols], k.inv_t[:, h, cols], k.q_sb[:, h % 2, cols],
                                         start=True, stop=True)
                    for c in range(TT):
                        cols = slice(c * P, (c + 1) * P)
                        last = nc.tensor.matmul(k.psum[:, 6 + h % 2, cols], k.q_sb[:, h % 2, cols],
                                                k.inv_t[:, h, cols], start=True, stop=True)
                    last.then_inc(xs, 1)

        @block.scalar
        def _(act):
            for n in range(len(LEVELS)):
                for h in range(HEADS):
                    i = n * HEADS + h
                    act.wait_ge(q_ready, i + 1)
                    if i >= 2:
                        act.wait_ge(xs, i - 1)
                    nc.scalar.copy(k.q_sb[:, h % 2, :], k.psum[:, h, :]).then_inc(q_kept, 1)

        @block.vector
        def _(dve):
            eye = k.const("ident").unsqueeze(1).broadcast_to([P, TT, P])
            for h in range(HEADS):
                nc.vector.tensor_copy(blocks(k.inv_n[:, h, :]), eye)
                last = nc.vector.tensor_copy(blocks(k.inv_t[:, h, :]), eye)
            last.then_inc(started, 1)
            dve.wait_ge(started, 1)
            for n in range(len(LEVELS)):
                for h in range(HEADS):
                    i = n * HEADS + h
                    dve.wait_ge(xs, i + 1)
                    if i >= 4:
                        dve.wait_ge(x_new, i - 3)
                        dve.wait_ge(xt_new, i - 3)
                    nc.vector.tensor_tensor(k.inv_n[:, h, :], k.inv_n[:, h, :], k.psum[:, 4 + h % 2, :],
                                            ALU.subtract).then_inc(x_new, 1)
                    nc.vector.tensor_tensor(k.inv_t[:, h, :], k.inv_t[:, h, :], k.psum[:, 6 + h % 2, :],
                                            ALU.subtract).then_inc(xt_new, 1)


def delta_scan(k):
    nc = k.nc
    ks, r_ready, solved, u_ready, out, grown, s_ready, steps = (
        k.sem("ds_" + s) for s in ("ks", "r", "solved", "u", "out", "grown", "s", "steps"))
    r = k.scratch[:, 0, 0:256]
    u = k.scratch[:, 1, 0:256]
    with nc.Block() as block:
        @block.tensor
        def _(pe):
            for c in range(TT):
                cols = slice(c * P, (c + 1) * P)
                pe.wait_ge(s_ready, c + 1)
                if c >= 1:
                    for h in range(HEADS):
                        last = nc.tensor.matmul(k.psum[:, h % 2, (h // 2) * HD:(h // 2 + 1) * HD],
                                                k.z[head_rows(h), BK + h // 2, cols],
                                                k.state[head_rows(h), h // 2, :], start=True, stop=True)
                    last.then_inc(ks, 1)
                pe.wait_ge(r_ready, c + 1)
                for h in range(HEADS):
                    last = nc.tensor.matmul(k.psum[:, 7, h * HD:(h + 1) * HD], k.inv_t[:, h, cols],
                                            r[:, h * HD:(h + 1) * HD], start=True, stop=True)
                last.then_inc(solved, 1)
                pe.wait_ge(u_ready, c + 1)
                if c < TT - 1:
                    for h in range(HEADS):
                        last = nc.tensor.matmul(k.psum[head_rows(h), 2 + h // 2, 0:HD],
                                                k.k_tok[:, c, h * HD:(h + 1) * HD], u[:, h * HD:(h + 1) * HD],
                                                start=True, stop=True)
                    last.then_inc(grown, 1)
                for h in range(HEADS):
                    if c >= 1:
                        nc.tensor.matmul(k.psum[head_rows(h), 4 + h // 2, cols], k.state[head_rows(h), h // 2, :],
                                         k.qg[head_rows(h), h // 2, cols], start=True, stop=False)
                    last = nc.tensor.matmul(k.psum[head_rows(h), 4 + h // 2, cols], u[:, h * HD:(h + 1) * HD],
                                            k.ratio[:, h, cols], start=(c == 0), stop=True)
                last.then_inc(out, 1)

        @block.vector
        def _(dve):
            link = Link(dve, steps)
            nc.vector.memset(k.state[:], 0.0).then_inc(s_ready, 1)
            for c in range(TT):
                v = k.v_tok[:, 1, c, :].rearrange("p (h d) -> p h d", d=HD)
                r4 = r.rearrange("p (h d) -> p h d", d=HD)
                if c >= 1:
                    dve.wait_ge(ks, c)
                    link(nc.vector.tensor_tensor(
                        r.rearrange("p (g o d) -> p o g d", g=2, o=2),
                        k.psum[:, 0:2, 0:2 * HD].rearrange("p o (g d) -> p o g d", g=2),
                        k.gamma_tok[:, c * HEADS:(c + 1) * HEADS].rearrange("p (g o) -> p o g", g=2)
                        .unsqueeze(3).broadcast_to([P, 2, 2, HD]), ALU.mult))
                    nc.vector.tensor_tensor(r4, v, r4, ALU.subtract).then_inc(r_ready, 1)
                else:
                    nc.vector.tensor_copy(r4, v).then_inc(r_ready, 1)
                dve.wait_ge(solved, c + 1)
                if c >= 1:
                    dve.wait_ge(out, c)
                nc.vector.tensor_tensor(
                    u.rearrange("p (h d) -> p h d", d=HD),
                    k.psum[:, 7, 0:256].rearrange("p (h d) -> p h d", d=HD),
                    k.beta[:, c * HEADS:(c + 1) * HEADS].unsqueeze(2).broadcast_to([P, HEADS, HD]),
                    ALU.mult).then_inc(u_ready, 1)
                if c < TT - 1:
                    dve.wait_ge(grown, c + 1)
                    dve.wait_ge(out, c + 1)
                    link(nc.vector.scalar_tensor_tensor(
                        k.state[:, 0, :], k.state[:, 0, :], k.whole[:, 0, c:c + 1], k.psum[:, 2, 0:HD],
                        ALU.mult, ALU.add))
                    nc.vector.scalar_tensor_tensor(
                        k.state[:, 1, :], k.state[:, 1, :], k.whole[:, 1, c:c + 1], k.psum[:, 3, 0:HD],
                        ALU.mult, ALU.add).then_inc(s_ready, 1)

        @block.scalar
        def _(act):
            for m in range(2):
                act.wait_ge(out, TT)
                nc.scalar.copy(k.o[:, 2 + m, :], k.psum[:, 4 + m, :])


def residual_product(k, name, rhs, gain=None, mod=None):
    nc = k.nc
    out, squared, added, steps, done = (k.sem(f"{name}_{s}") for s in ("out", "squared", "added", "steps",
                                                                       "done"))
    with nc.Block() as block:
        @block.sync
        def _(sp):
            first = k.first_tile[name] + RING
            per = k.chunks(name)
            for j in range(KT):
                k.load_weights(sp, first + j * per, first + (j + 1) * per)
                if mod is not None:
                    mod.load(sp, j)

        @block.tensor
        def _(pe):
            k.product(pe, name, rhs, T, out,
                      between=(lambda j: mod.tensor(pe, j - 1)) if mod is not None else None)
            if mod is not None:
                mod.tensor(pe, KT - 1)

        @block.scalar
        def _(act):
            for j in range(KT):
                act.wait_ge(out, j + 1)
                if j >= 2:
                    act.wait_ge(added, j - 1)
                nc.scalar.activation(k.squares[:, j % 2, :], k.h[:, j, :], ACT.Square).then_inc(squared, 1)

        @block.gpsimd
        def _(pool):
            add_squares(k, pool, squared, added)

        @block.vector
        def _(dve):
            link = Link(dve, steps)
            k.split_weights(dve, name, -1)
            for j in range(KT):
                k.split_weights(dve, name, j)
                dve.wait_ge(k.weights_used, k.product_done(name, j))
                nc.vector.tensor_tensor(k.h[:, j, :], k.h[:, j, :], k.psum[:, j % PRODUCT_BANKS, :], ALU.add
                                        ).then_inc(out, 1)
                if gain is not None:
                    dve.wait_ge(out, j + 1)
                    link(nc.vector.tensor_scalar(k.n_low[:, j, :], k.h[:, j, :], gain[:, j:j + 1], None,
                                                 ALU.mult))
                    split(k, link, k.n[:, j, :], k.n_low[:, j, :]).then_inc(done, 1)
                if mod is not None:
                    mod.vector(dve, link, j)
            if mod is not None:
                mod.keep(dve)


def cross_attention(k):
    nc = k.nc
    name = "att_q"
    root = Root(k, "att_root")
    mod = Modulation(k, "att_q", 32, 8)
    out, msteps = k.sem("att_q_out"), k.sem("att_q_steps")
    with nc.Block() as block:
        @block.sync
        def _(sp):
            first = k.first_tile[name] + RING
            for j in range(KT):
                k.load_weights(sp, first + j, first + j + 1)
                mod.load(sp, j)

        @block.tensor
        def _(pe):
            root.tensor()
            k.product(pe, name, k.normed, T, out, between=lambda j: mod.tensor(pe, j - 1))
            mod.tensor(pe, KT - 1)

        @block.scalar
        def _(act):
            root.scalar(act)

        @block.vector
        def _(dve):
            link = Link(dve, msteps)
            k.split_weights(dve, name, -1)
            root.vector(dve)
            for j in range(KT):
                k.split_weights(dve, name, j)
                dve.wait_ge(k.weights_used, k.product_done(name, j))
                nc.vector.tensor_tensor(k.z[:, j, :], k.psum[:, j % PRODUCT_BANKS, :], k.rstd, ALU.mult
                                        ).then_inc(out, 1)
                mod.vector(dve, link, j)
            mod.keep(dve)

    scale = 256 ** -0.5
    scored, maxed, risen, normed, turned, kept, steps = (
        k.sem("xa_" + s) for s in ("scored", "maxed", "risen", "normed", "turned", "kept", "steps"))
    units = [(hp, i) for hp in range(2) for i in range(TT)]
    with nc.Block() as block:
        @block.tensor
        def _(pe):
            def scores(u):
                hp, i = units[u]
                if u >= 3:
                    pe.wait_ge(risen, 2 * (u - 2))
                for h in range(2):
                    for kk in range(2):
                        f = 2 * (2 * hp + h) + kk
                        last = nc.tensor.matmul(k.psum[:, u % 3, h * MEM:(h + 1) * MEM],
                                                k.z[:, f, i * P:(i + 1) * P], k.mem_k[:, f, :],
                                                start=(kk == 0), stop=(kk == 1))
                last.then_inc(scored, 1)

            scores(0)
            for u in range(len(units)):
                if u + 1 < len(units):
                    scores(u + 1)
                pe.wait_ge(normed, 2 * (u + 1))
                if u >= 2:
                    pe.wait_ge(kept, u - 1)
                for b in range(4):
                    last = nc.tensor.transpose(k.psum[:, 4 + u % 2, b * P:(b + 1) * P],
                                               k.scratch[:, u % 4, b * P:(b + 1) * P], k.const("ident"))
                last.then_inc(turned, 1)

        @block.vector
        def _(dve):
            link = Link(dve, steps)
            for u in range(len(units)):
                dve.wait_ge(scored, u + 1)
                m = k.small[:, u % 4, 0:2]
                link(nc.vector.tensor_reduce(m, k.psum[:, u % 3, :].rearrange("p (h x) -> p h x", h=2),
                                             AX_X, ALU.max))
                nc.vector.tensor_scalar(m, m, -scale, None, ALU.mult).then_inc(maxed, 1)
                dve.wait_ge(risen, 2 * (u + 1))
                s = k.small[:, u % 4, 2:4]
                link(nc.vector.reciprocal(s, s))
                for h in range(2):
                    p = k.scratch[:, u % 4, h * MEM:(h + 1) * MEM]
                    nc.vector.tensor_scalar(p, p, s[:, h:h + 1], None, ALU.mult).then_inc(normed, 1)

        @block.scalar
        def _(act):
            def keep(u):
                hp, i = units[u]
                act.wait_ge(turned, u + 1)
                nc.scalar.copy(k.probs_t[:, 4 * hp:4 * hp + 4, i * P:(i + 1) * P],
                               k.psum[:, 4 + u % 2, :].rearrange("p (b x) -> p b x", b=4)).then_inc(kept, 1)

            for u in range(len(units)):
                act.wait_ge(maxed, u + 1)
                if u >= 4:
                    act.wait_ge(turned, u - 3)
                for h in range(2):
                    nc.scalar.activation(k.scratch[:, u % 4, h * MEM:(h + 1) * MEM],
                                         k.psum[:, u % 3, h * MEM:(h + 1) * MEM], ACT.Exp,
                                         bias=k.small[:, u % 4, h:h + 1], scale=scale,
                                         accum_out=k.small[:, u % 4, 2 + h:3 + h]).then_inc(risen, 1)
                if u >= 1:
                    keep(u - 1)
            keep(len(units) - 1)

    mixed, moved, xsteps = k.sem("xa_mixed"), k.sem("xa_moved"), k.sem("xa_steps2")
    with nc.Block() as block:
        @block.tensor
        def _(pe):
            for f in range(KT):
                if f >= 4:
                    pe.wait_ge(moved, f - 3)
                for m in range(2):
                    last = nc.tensor.matmul(k.psum[:, f % 4, :], k.mem_v[:, m, f * P:(f + 1) * P],
                                            k.probs_t[:, 2 * (f // 2) + m, :], start=(m == 0), stop=(m == 1))
                last.then_inc(mixed, 1)

        @block.scalar
        def _(act):
            for f in range(KT):
                act.wait_ge(mixed, f + 1)
                nc.scalar.copy(k.att_low[:, f, :], k.psum[:, f % 4, :]).then_inc(moved, 1)

        @block.vector
        def _(dve):
            link = Link(dve, xsteps)
            for f in range(KT):
                dve.wait_ge(moved, f + 1)
                link(split(k, link, k.att_high[:, f, :], k.att_low[:, f, :]))


def ffn_up(k, idx):
    nc = k.nc
    name = f"up_{idx}"
    both = idx == 0
    out, padded, tapped, gate_done, risen, hid_done, steps = (
        k.sem(f"{name}_{s}") for s in ("out", "padded", "tapped", "gate", "risen", "hid", "steps"))
    taps = k.vec(f"ffn_conv_{idx}")
    nt = 2 * FT if both else FT
    root = Root(k, name + "_root") if both else None
    with nc.Block() as block:
        @block.sync
        def _(sp):
            k.load_ahead(sp, name)

        @block.tensor
        def _(pe):
            if both:
                root.tensor()
            k.product(pe, name, k.normed, T, out)

        @block.scalar
        def _(act):
            def rise(p):
                act.wait_ge(gate_done, p + 1)
                bias = k.vec(f"ffn_conv_b_{idx}")[:, p:p + 1] if not both else 0.0
                nc.scalar.activation(k.conv_g[:, p % 2, :], k.conv_g[:, p % 2, :], ACT.Silu, bias=bias
                                     ).then_inc(risen, 1)

            if both:
                root.scalar(act)
            act.wait_ge(padded, 1)
            for p in range(FT):
                if p >= 2:
                    act.wait_ge(hid_done, p - 1)
                for s in range(2):
                    j = 2 * p + s
                    x = k.up_in[:, p % 2, s, 2:2 + T]
                    if both:
                        act.wait_ge(out, j + 1)
                    else:
                        act.wait_ge(k.weights_used, k.product_done(name, j))
                        nc.scalar.copy(x, k.psum[:, j % PRODUCT_BANKS, :]).then_inc(out, 1)
                        act.wait_ge(out, j + 1)
                    if both or s == 0:
                        col = 2 * nt + s * FT + p
                        dst = (k.conv_g, k.conv_v)[s][:, p % 2, :]
                        nc.scalar.activation(dst, x, ACT.Copy, scale=taps[:, col:col + 1]).then_inc(tapped, 1)
                    if s == 0 and p >= 1:
                        rise(p - 1)
            rise(FT - 1)

        @block.vector
        def _(dve):
            link = Link(dve, steps)
            convs = 2 if both else 1

            def conv(p, s):
                dst, src = (k.conv_g, k.conv_v)[s][:, p % 2, :], k.up_in[:, p % 2, s]
                col = s * FT + p
                dve.wait_ge(tapped, convs * p + s + 1)
                link(nc.vector.scalar_tensor_tensor(dst, src[:, 0:T], taps[:, col:col + 1], dst,
                                                    ALU.mult, ALU.add))
                step = nc.vector.scalar_tensor_tensor(dst, src[:, 1:1 + T],
                                                      taps[:, nt + col:nt + col + 1], dst,
                                                      ALU.mult, ALU.add)
                if s == 0:
                    step.then_inc(gate_done, 1)
                else:
                    link(step)

            def hidden(p):
                dve.wait_ge(risen, p + 1)
                value = k.conv_v[:, p % 2, :] if both else k.up_in[:, p % 2, 1, 2:2 + T]
                link(nc.vector.tensor_tensor(k.hid_low[:, p, :], k.conv_g[:, p % 2, :], value, ALU.mult))
                split(k, link, k.hid_high[:, p, :], k.hid_low[:, p, :]).then_inc(hid_done, 1)

            def scaled(j):
                dve.wait_ge(k.weights_used, k.product_done(name, j))
                if j % 2 == 0 and j >= 4:
                    dve.wait_ge(hid_done, j // 2 - 1)
                nc.vector.tensor_tensor(k.up_in[:, (j // 2) % 2, j % 2, 2:2 + T],
                                        k.psum[:, j % PRODUCT_BANKS, :], k.rstd, ALU.mult).then_inc(out, 1)

            nc.vector.memset(k.up_in[:, :, :, 0:2], 0.0).then_inc(padded, 1)
            k.split_weights(dve, name, -1)
            if both:
                root.vector(dve)
            for p in range(FT):
                k.split_weights(dve, name, 2 * p)
                if both:
                    scaled(2 * p)
                if p >= 1 and both:
                    conv(p - 1, 1)
                    hidden(p - 1)
                conv(p, 0)
                k.split_weights(dve, name, 2 * p + 1)
                if both:
                    scaled(2 * p + 1)
                elif p >= 1:
                    hidden(p - 1)
            if both:
                conv(FT - 1, 1)
            hidden(FT - 1)


def plain_product(k, name, rhs, y):
    nc = k.nc
    out, squared, added = (k.sem(f"{name}_{s}") for s in ("out", "squared", "added"))
    with nc.Block() as block:
        @block.sync
        def _(sp):
            k.load_ahead(sp, name)

        @block.tensor
        def _(pe):
            k.product(pe, name, rhs, T, out)

        @block.scalar
        def _(act):
            for j in range(KT):
                act.wait_ge(k.weights_used, k.product_done(name, j))
                nc.scalar.copy(y[:, j, :], k.psum[:, j % PRODUCT_BANKS, :]).then_inc(out, 1)
                act.wait_ge(out, j + 1)
                if j >= 2:
                    act.wait_ge(added, j - 1)
                nc.scalar.activation(k.squares[:, j % 2, :], y[:, j, :], ACT.Square).then_inc(squared, 1)

        @block.gpsimd
        def _(pool):
            add_squares(k, pool, squared, added)

        @block.vector
        def _(dve):
            for j in range(-1, KT):
                k.split_weights(dve, name, j)


def condition(k):
    nc = k.nc
    with nc.Block() as block:
        @block.scalar
        def _(act):
            nc.scalar.activation(k.cond[:], k.vec("cond"), ACT.Silu)


def modulation(k):
    nc = k.nc
    steps = k.sem("modulation_steps")
    with nc.Block() as block:
        @block.vector
        def _(dve):
            link = Link(dve, steps)
            for i in range(2):
                for part, norm in ((1, f"mix_pre_{i}"), (2, f"mix_post_{i}"), (4, f"ffn_pre_{i}"),
                                   (5, f"ffn_post_{i}")):
                    m = mod_part(k, i, part)
                    link(nc.vector.scalar_tensor_tensor(m, m, 1.0, k.vec(norm), ALU.add, ALU.mult))


def mod_part(k, i, part):
    return k.mod_cols[:, (6 * i + part) * KT:(6 * i + part + 1) * KT]


def ab_projection(k):
    nc = k.nc
    out, padded, steps, convolved = (k.sem("ab_in_" + s) for s in ("out", "padded", "steps", "conv"))
    with nc.Block() as block:
        @block.sync
        def _(sp):
            k.load_ahead(sp, "ab_in")

        @block.tensor
        def _(pe):
            k.product(pe, "ab_in", k.normed, T, out)

        @block.scalar
        def _(act):
            act.wait_ge(padded, 1)
            for j in range(PRODUCTS["ab_in"][0]):
                act.wait_ge(k.weights_used, k.product_done("ab_in", j))
                bank = k.psum[:, j % PRODUCT_BANKS, :]
                if j < GR:
                    if j >= 2:
                        act.wait_ge(convolved, j - 1)
                    nc.scalar.copy(k.conv_in[:, j % 2, 3:3 + T], bank).then_inc(out, 1)
                elif j < NQT:
                    nc.scalar.activation(k.z[:, j, :], bank, ACT.Gelu_apprx_tanh).then_inc(out, 1)
                elif j == GL:
                    nc.scalar.activation(k.z[:, j, :], bank, ACT.Sigmoid).then_inc(out, 1)
                else:
                    nc.scalar.copy(k.z[:, j, :], bank).then_inc(out, 1)

        @block.vector
        def _(dve):
            link = Link(dve, steps)
            nc.vector.memset(k.conv_in[:, 0:2, 0:3], 0.0).then_inc(padded, 1)
            w, b = k.vec("ab_conv"), k.vec("ab_conv_b")
            k.split_weights(dve, "ab_in", -1)
            for j in range(PRODUCTS["ab_in"][0]):
                k.split_weights(dve, "ab_in", j)
                if j >= KT:
                    continue
                dve.wait_ge(out, j + 1)
                link(nc.vector.tensor_scalar(k.z[:, j, :], k.conv_in[:, j % 2, 0:T], w[:, j:j + 1],
                                             b[:, j:j + 1], ALU.mult, ALU.add))
                for tap in range(1, 4):
                    step = nc.vector.scalar_tensor_tensor(
                        k.z[:, j, :], k.conv_in[:, j % 2, tap:tap + T], w[:, KT * tap + j:KT * tap + j + 1],
                        k.z[:, j, :], ALU.mult, ALU.add)
                    if tap < 3:
                        link(step)
                step.then_inc(convolved, 1)


def recurrence(k):
    nc = k.nc
    rate_up, rate_done, projected, opened, ready_a, ready_t, sqrt_in, rooted, steps, asteps, scanned = (
        k.sem("lru_" + s) for s in ("rate_up", "rate", "projected", "opened", "a", "t", "sqrt_in", "rooted",
                                    "steps", "asteps", "scanned"))
    r, inp, th = k.lru_r, k.lru_i, k.lru_t
    rate, nrate, e = k.small[:, 0, 0:KT], k.small[:, 1, 0:KT], k.small[:, 2, 0:KT]
    with nc.Block() as block:
        @block.tensor
        def _(pe):
            for i in range(KT):
                for g in range(2):
                    if i >= 4:
                        pe.wait_ge(opened, 2 * (i - 4) + g + 1)
                    nc.tensor.matmul(k.psum[:, 2 * (i % 4) + g, :], k.lru_w[:, g, i, :], k.z[:, XR + i, :],
                                     start=True, stop=True).then_inc(projected, 1)

        @block.scalar
        def _(act):
            link = Link(act, asteps)
            link(nc.scalar.activation(e, k.vec("lru_lam"), ACT.Abs))
            link(nc.scalar.activation(e, e, ACT.Exp, scale=-1.0))
            nc.scalar.activation(e, e, ACT.Ln, bias=1.0).then_inc(rate_up, 1)
            for i in range(KT):
                for g, (dst, bias) in enumerate(((r, "lru_b_r"), (inp, "lru_b_i"))):
                    act.wait_ge(projected, 2 * i + g + 1)
                    nc.scalar.activation(dst[:, i, :], k.psum[:, 2 * (i % 4) + g, :], ACT.Sigmoid,
                                         bias=k.vec(bias)[:, i:i + 1]).then_inc(opened, 1)
            act.wait_ge(rate_done, 1)
            act.wait_ge(opened, 2 * KT)
            for i in range(KT):
                nc.scalar.activation(th[:, i, :], r[:, i, :], ACT.Tanh, scale=rate[:, i:i + 1]
                                     ).then_inc(ready_t, 1)
            for i in range(KT):
                act.wait_ge(ready_t, i + 1)
                nc.scalar.activation(r[:, i, :], r[:, i, :], ACT.Exp, scale=nrate[:, i:i + 1]
                                     ).then_inc(ready_a, 1)
            for i in range(KT):
                act.wait_ge(sqrt_in, i + 1)
                nc.scalar.activation(th[:, i, :], th[:, i, :], ACT.Sqrt, scale=2.0).then_inc(rooted, 1)

        @block.vector
        def _(dve):
            link = Link(dve, steps)
            dve.wait_ge(rate_up, 1)
            link(nc.vector.tensor_scalar(rate, k.vec("lru_lam"), -1.0, 0.0, ALU.mult, ALU.max))
            link(nc.vector.tensor_tensor(rate, rate, e, ALU.add))
            link(nc.vector.tensor_scalar(rate, rate, 8.0, None, ALU.mult))
            nc.vector.tensor_scalar(nrate, rate, -1.0, None, ALU.mult).then_inc(rate_done, 1)
            for i in range(KT):
                tmp = k.scratch[:, i % 2, :]
                dve.wait_ge(opened, 2 * i + 2)
                nc.vector.tensor_tensor(inp[:, i, :], inp[:, i, :], k.z[:, XR + i, :], ALU.mult)
                dve.wait_ge(ready_t, i + 1)
                link(nc.vector.tensor_scalar(tmp, th[:, i, :], 1.0, None, ALU.add))
                link(nc.vector.reciprocal(tmp, tmp))
                dve.wait_ge(ready_a, i + 1)
                link(nc.vector.tensor_tensor(th[:, i, :], th[:, i, :], tmp, ALU.mult))
                nc.vector.tensor_scalar(th[:, i, :], th[:, i, :], 1e-30, None, ALU.max).then_inc(sqrt_in, 1)
            for i in range(KT):
                dve.wait_ge(rooted, i + 1)
                link(nc.vector.tensor_tensor(inp[:, i, :], inp[:, i, :], th[:, i, :], ALU.mult))
                link(nc.vector.tensor_tensor_scan(th[:, i, :], r[:, i, :], inp[:, i, :], 0.0,
                                                  ALU.mult, ALU.add))
                link(nc.vector.tensor_tensor(th[:, i, :], th[:, i, :], k.z[:, GR + i, :], ALU.mult))
                split(k, link, inp[:, i, :], th[:, i, :]).then_inc(scanned, 1)


def group_rows(g):
    return slice(HD * (g % 2), HD * (g % 2) + HD)


def compress(k):
    nc = k.nc
    loaded, spread, hid, acted, up, steps, moved, pe_kept = (
        k.sem("cmp_" + s) for s in ("loaded", "spread", "hid", "acted", "up", "steps", "moved", "pe_kept"))
    with nc.Block() as block:
        @block.sync
        def _(sp):
            sp.dma_start(k.cmp_w1[:], k.dram["cmp_w1"]).then_inc(loaded, 16)
            sp.dma_start(k.cmp_w2[:], k.dram["cmp_w2"]).then_inc(loaded, 16)

        @block.scalar
        def _(act):
            for kind, tile in enumerate((KC, VC)):
                for g in range(NG):
                    src = k.z[group_rows(g), tile + g // 2, :]
                    nc.scalar.copy(k.pairs[0:HD, kind, g, :], src)
                    nc.scalar.copy(k.pairs[HD:P, kind, g, 0:T - 1], src[:, 1:T]).then_inc(spread, 1)
            for kind in range(2):
                act.wait_ge(pe_kept, kind + 1)
                nc.scalar.activation(k.cmp_hid[:, kind, :, 0:NCMP],
                                     k.psum[:, kind, 0:NG * NCMP].rearrange("p (g n) -> p g n", g=NG),
                                     ACT.Gelu_apprx_tanh, bias=k.small[:, kind, 0:1]).then_inc(acted, 1)

        @block.vector
        def _(dve):
            nc.vector.memset(k.cmp_hid[:, :, :, NCMP:32], 0.0).then_inc(steps, 1)
            for kind in range(2):
                dve.wait_ge(hid, kind + 1)
                nc.vector.tensor_copy(k.small[:, kind, 0:1], k.psum[:, 2 + kind, 0:1]).then_inc(pe_kept, 1)
            dve.wait_ge(acted, 2)
            dve.wait_ge(steps, 1)
            nc.vector.tensor_copy(k.cmp_hid4, k.cmp_hid[:, 1].unsqueeze(2).broadcast_to([P, NG, 4, 32])
                                  ).then_inc(steps, 1)
            dve.wait_ge(up, 1)
            for g in range(NG):
                nc.vector.tensor_copy(k.cmp_k[group_rows(g), g // 2, :],
                                      k.psum[group_rows(g), 4, (g // 2) * 32:(g // 2) * 32 + 32])
            nc.vector.tensor_copy(k.cmp_v[:], k.psum[:, 5, 0:NG * HD].rearrange("p (g d) -> p g d", g=NG))

        @block.tensor
        def _(pe):
            pe.wait_ge(loaded, 32)
            for kind in range(2):
                pe.wait_ge(spread, NG * (kind + 1))
                for j in range(16):
                    nc.tensor.matmul(k.psum[:, kind, 0:NG * NCMP], k.cmp_w1[:, kind, j, :],
                                     k.pairs[:, kind, :, 2 * j:2 * j + 16 * (NCMP - 1) + 1:16],
                                     start=(j == 0), stop=(j == 15))
                pe_vec = k.vec("pe_k" if kind == 0 else "pe_v")
                for j in range(16):
                    last = nc.tensor.matmul(k.psum[:, 2 + kind, 0:1], k.cmp_w1[:, kind, j, :],
                                            pe_vec[:, j:j + 1], start=(j == 0), stop=(j == 15))
                last.then_inc(hid, 1)
            pe.wait_ge(acted, 2)
            pe.wait_ge(steps, 2)
            for g in range(NG):
                nc.tensor.matmul(k.psum[group_rows(g), 4, (g // 2) * 32:(g // 2) * 32 + 32],
                                 k.cmp_w2[:, 0, :], k.cmp_hid[:, 0, g, :], start=True, stop=True)
            for g in range(NG):
                last = nc.tensor.matmul(k.psum[:, 5, g * HD:(g + 1) * HD],
                                        k.cmp_hid4[:, g].rearrange("p r n -> p (r n)"),
                                        k.cmp_w2[:, 1, :], start=True, stop=True)
            last.then_inc(up, 1)


def compressed_attention(k):
    nc = k.nc
    scored, taken, steps, shifted, risen, gated, turned, kept = (
        k.sem("ca_" + s) for s in ("scored", "taken", "steps", "shifted", "risen", "gated", "turned", "kept"))
    scale = HD ** -0.5
    with nc.Block() as block:
        @block.tensor
        def _(pe):
            for i in range(TT):
                if i >= 2:
                    pe.wait_ge(taken, 2 * (i - 1))
                for h in range(NQ):
                    g, r = h // 4, h % 4
                    at = (4 * (g // 2) + r) * 32
                    last = nc.tensor.matmul(k.psum[:, 2 * (i % 2) + g % 2, at:at + 32],
                                            k.z[group_rows(g), NQT + 4 * (g // 2) + r, i * P:(i + 1) * P],
                                            k.cmp_k[group_rows(g), g // 2, :], start=True, stop=True)
                last.then_inc(scored, 1)
            for i in range(TT):
                pe.wait_ge(gated, i + 1)
                for g in range(NG):
                    last = nc.tensor.transpose(k.psum[:, 4 + i, g * P:(g + 1) * P],
                                               k.scratch[:, i, g * P:(g + 1) * P], k.const("ident"))
                last.then_inc(turned, 1)

        @block.scalar
        def _(act):
            for i in range(TT):
                act.wait_ge(shifted, i + 1)
                nc.scalar.activation(k.scratch[:, i, :], k.scratch[:, i, :], ACT.Exp, scale=scale
                                     ).then_inc(risen, 1)
            for i in range(TT):
                act.wait_ge(turned, i + 1)
                for g in range(NG):
                    nc.scalar.copy(k.cmp_pt[g][:, i * P:(i + 1) * P], k.psum[:, 4 + i, g * P:(g + 1) * P]
                                   ).then_inc(kept, 1)

        @block.vector
        def _(dve):
            link = Link(dve, steps)
            m, den = k.small[:, 0, 0:NQ], k.small[:, 1, 0:NQ]
            by_n = k.scratch[:, 4, 0:P].rearrange("p (g n) -> p g n", g=NG)
            imp = k.scratch[:, 4, P:P + 32].rearrange("p (g j) -> p g j", g=NG)
            rank = k.scratch[:, 4, P + 32:P + 64].rearrange("p (g j) -> p g j", g=NG)
            above = k.scratch[:, 5, 0:256].rearrange("p (g j i) -> p g j i", g=NG, j=NBLK)
            tied = k.scratch[:, 5, 256:512].rearrange("p (g j i) -> p g j i", g=NG, j=NBLK)
            for i in range(TT):
                s = k.scratch[:, i, :].rearrange("p (h n) -> p h n", h=NQ)
                dve.wait_ge(scored, i + 1)
                for odd in range(2):
                    nc.vector.tensor_tensor(
                        k.scratch[:, i, :].rearrange("p (g o r n) -> p o g r n", g=2, o=2, r=4)[:, odd],
                        k.psum[:, 2 * (i % 2) + odd, 0:256].rearrange("p (g r n) -> p g r n", g=2, r=4),
                        k.const(f"cmp_bias{i}").unsqueeze(1).unsqueeze(1).broadcast_to([P, 2, 4, 32]),
                        ALU.add).then_inc(taken, 1)
                dve.wait_ge(taken, 2 * (i + 1))
                link(nc.vector.tensor_reduce(m, s, AX_X, ALU.max))
                nc.vector.tensor_tensor(s, s, m.unsqueeze(2).broadcast_to([P, NQ, 32]), ALU.subtract
                                        ).then_inc(shifted, 1)
                dve.wait_ge(risen, i + 1)
                link(nc.vector.tensor_tensor(s, s, k.const(f"cmp_seen{i}").unsqueeze(1)
                                             .broadcast_to([P, NQ, 32]), ALU.mult))
                link(nc.vector.tensor_reduce(den, s, AX_X, ALU.add))
                link(nc.vector.tensor_scalar(den, den, 1e-30, None, ALU.max))
                link(nc.vector.reciprocal(den, den))
                link(nc.vector.tensor_tensor(s, s, den.unsqueeze(2).broadcast_to([P, NQ, 32]), ALU.mult))
                link(nc.vector.tensor_reduce(by_n, k.scratch[:, i, :].rearrange("p (g r n) -> p g n r", g=NG, r=4),
                                             AX_X, ALU.add))
                link(nc.vector.tensor_reduce(imp, by_n.rearrange("p g (j x) -> p g j x", x=4), AX_X, ALU.add))
                link(nc.vector.tensor_tensor(imp[:, :, 1:NBLK], imp[:, :, 1:NBLK], by_n[:, :, 3:31:4], ALU.add))
                link(nc.vector.tensor_tensor(imp, imp, k.const(f"block_bias{i}").unsqueeze(1)
                                             .broadcast_to([P, NG, NBLK]), ALU.add))
                mine = imp.unsqueeze(3).broadcast_to([P, NG, NBLK, NBLK])
                other = imp.unsqueeze(2).broadcast_to([P, NG, NBLK, NBLK])
                link(nc.vector.tensor_tensor(above, other, mine, ALU.is_gt))
                link(nc.vector.tensor_tensor(tied, other, mine, ALU.is_equal))
                t3 = k.scratch[:, 5, 256:512].rearrange("p (g x) -> p g x", g=NG)
                link(nc.vector.tensor_tensor(t3, t3, k.const("earlier").unsqueeze(1).broadcast_to([P, NG, 64]),
                                             ALU.mult))
                link(nc.vector.tensor_tensor(k.scratch[:, 5, 0:256], k.scratch[:, 5, 0:256],
                                             k.scratch[:, 5, 256:512], ALU.add))
                link(nc.vector.tensor_reduce(rank, above, AX_X, ALU.add))
                link(nc.vector.tensor_scalar(k.block_bias[:, i, :, :], rank, 3.5, NEG, ALU.is_ge, ALU.mult))
                nc.vector.tensor_tensor(
                    s, s, k.gate_tok[:, i, 0:48].rearrange("p (h b) -> p h b", b=3)[:, :, 0:1]
                    .broadcast_to([P, NQ, 32]), ALU.mult).then_inc(gated, 1)
                dve.wait_ge(gated, i + 1)


def partial_rotary(k):
    nc = k.nc
    turned, taken, steps = (k.sem("pr_" + s) for s in ("turned", "taken", "steps"))
    tiles = list(range(NQT, NQT + 8)) + [KS, KS + 1, KW, KW + 1]
    with nc.Block() as block:
        @block.tensor
        def _(pe):
            for i, j in enumerate(tiles):
                if i >= 4:
                    pe.wait_ge(taken, i - 3)
                nc.tensor.matmul(k.psum[:, i % 4, :], k.const("rotate_part"), k.z[:, j, :],
                                 start=True, stop=True).then_inc(turned, 1)

        @block.vector
        def _(dve):
            link = Link(dve, steps)
            for i, j in enumerate(tiles):
                tmp = k.scratch[:, i % 2, :]
                dve.wait_ge(turned, i + 1)
                link(nc.vector.tensor_tensor(k.z[:, j, :], k.z[:, j, :], k.const("rope_cos"), ALU.mult))
                nc.vector.tensor_tensor(tmp, k.psum[:, i % 4, :], k.const("rope_sin"), ALU.mult).then_inc(taken, 1)
                dve.wait_ge(taken, i + 1)
                link(nc.vector.tensor_tensor(k.z[:, j, :], k.z[:, j, :], tmp, ALU.add))


def sparse_attention(k):
    nc = k.nc
    scored, biased, maxed, risen, normed, turned, kept, mixed, moved, steps = (
        k.sem("sa_" + s) for s in ("scored", "biased", "maxed", "risen", "normed", "turned", "kept",
                                   "mixed", "moved", "steps"))
    scale = HD ** -0.5
    items = [(h, i, b) for h in range(NQ) for i in range(TT) for b in range(2)]
    BUF = 4

    def keys(i, b):
        first = 0 if b == 0 else max(0, i - 2)
        return first, i + 1 - first

    with nc.Block() as block:
        @block.gpsimd
        def _(pool):
            for g in range(NG):
                if g >= 2:
                    pool.wait_ge(maxed, 8 * 4 * (g - 1))
                for i in range(TT):
                    w = (i + 1) * P
                    dst = k.sel_bias[g % 2][i]
                    nc.gpsimd.tensor_copy(
                        dst[:, 0:w].rearrange("p (j x) -> p j x", x=HD),
                        k.block_bias[:, i, g, 0:2 * (i + 1)].unsqueeze(2).broadcast_to([P, 2 * (i + 1), HD])
                    ).then_inc(biased, 1)
                    pool.wait_ge(biased, 2 * (g * TT + i) + 1)
                    nc.gpsimd.tensor_tensor(dst[:, w - P:w], dst[:, w - P:w], k.const("causal"), ALU.add
                                            ).then_inc(biased, 1)

        @block.tensor
        def _(pe):
            def scores(n):
                h, i, b = items[n]
                g, r = h // 4, h % 4
                first, nk = keys(i, b)
                if n >= 3:
                    pe.wait_ge(maxed, n - 2)
                tile = (KS if b == 0 else KW) + g // 2
                nc.tensor.matmul(k.psum[:, n % 3, 0:nk * P],
                                 k.z[group_rows(g), NQT + 4 * (g // 2) + r, i * P:(i + 1) * P],
                                 k.z[group_rows(g), tile, first * P:(first + nk) * P],
                                 start=True, stop=True).then_inc(scored, 1)

            def transposes(n):
                h, i, b = items[n]
                pe.wait_ge(normed, n + 1)
                if n >= 3:
                    pe.wait_ge(kept, n - 2)
                for j in range(keys(i, b)[1]):
                    last = nc.tensor.transpose(k.psum[:, 3 + n % 3, j * P:(j + 1) * P],
                                               k.rows[:, n % BUF, j * P:(j + 1) * P], k.const("ident"))
                last.then_inc(turned, 1)

            def values(h):
                g, r = h // 4, h % 4
                pe.wait_ge(kept, 8 * (h + 1))
                if h >= 2:
                    pe.wait_ge(moved, h - 1)
                dst = k.psum[group_rows(g), 6 + h % 2, :]
                rows = slice(32 * r, 32 * r + 32)
                nc.tensor.matmul(dst, k.cmp_v[rows, g, :], k.cmp_pt[g][rows, :], start=True, stop=False)
                for b, v in enumerate((k.vs_tok, k.vw_tok)):
                    for j in range(TT):
                        last_t = T if b == 0 else min(T, (j + 3) * P)
                        last = nc.tensor.matmul(dst[:, j * P:last_t], v[:, j, g * HD:(g + 1) * HD],
                                                k.pt[:, h % 2, b, j, j * P:last_t],
                                                start=False, stop=(b == 1 and j == TT - 1))
                last.then_inc(mixed, 1)

            scores(0)
            scores(1)
            for n in range(len(items)):
                if n + 2 < len(items):
                    scores(n + 2)
                transposes(n)
                if n % 8 == 2 and n > 8:
                    values(n // 8 - 1)
            values(NQ - 1)

        @block.vector
        def _(dve):
            link = Link(dve, steps)

            def norm(n):
                h, i, b = items[n]
                w = keys(i, b)[1] * P
                dve.wait_ge(risen, n + 1)
                s = k.stats[:, 1, n % BUF:n % BUF + 1]
                link(nc.vector.reciprocal(s, s))
                p = k.rows[:, n % BUF, 0:w]
                gate = k.gate_tok[:, i, 3 * h + 1 + b:3 * h + 2 + b]
                nc.vector.tensor_scalar(p, p, s, gate, ALU.mult, ALU.mult).then_inc(normed, 1)

            def divide(h):
                g, r = h // 4, h % 4
                if g % 2:
                    dve.wait_ge(moved, h + 1)
                    tile = 4 * (g // 2) + r
                    link(split(k, link, k.z[:, NQT + tile, :], k.ab_low[:, tile, :]))

            for n, (h, i, b) in enumerate(items):
                w = keys(i, b)[1] * P
                dve.wait_ge(scored, n + 1)
                if n >= BUF:
                    dve.wait_ge(turned, n - BUF + 1)
                if b == 0:
                    dve.wait_ge(biased, 2 * ((h // 4) * TT + i + 1))
                    bias = k.sel_bias[(h // 4) % 2][i]
                else:
                    bias = k.const("window")[:, 384 - w:384]
                m = k.stats[:, 0, n % BUF:n % BUF + 1]
                link(nc.vector.tensor_tensor_reduce(
                    out=k.rows[:, n % BUF, 0:w], in0=k.psum[:, n % 3, 0:w], in1=bias, scale=scale,
                    scalar=-3e38, op0=ALU.add, op1=ALU.max, accum_out=m))
                nc.vector.tensor_scalar(m, m, -1.0, None, ALU.mult).then_inc(maxed, 1)
                if n >= 1:
                    norm(n - 1)
                if n % 8 == 7 and n > 8:
                    divide(n // 8 - 1)
            norm(len(items) - 1)
            divide(NQ - 1)

        @block.scalar
        def _(act):
            def keep(n):
                h, i, b = items[n]
                first, nk = keys(i, b)
                act.wait_ge(turned, n + 1)
                if h >= 2:
                    act.wait_ge(mixed, h - 1)
                nc.scalar.copy(k.pt[:, h % 2, b, first:first + nk, i * P:(i + 1) * P],
                               k.psum[:, 3 + n % 3, 0:nk * P].rearrange("p (j x) -> p j x", x=P)
                               ).then_inc(kept, 1)

            def move(h):
                g, r = h // 4, h % 4
                act.wait_ge(mixed, h + 1)
                nc.scalar.copy(k.ab_low[group_rows(g), 4 * (g // 2) + r, :],
                               k.psum[group_rows(g), 6 + h % 2, :]).then_inc(moved, 1)

            for n, (h, i, b) in enumerate(items):
                w = keys(i, b)[1] * P
                act.wait_ge(maxed, n + 1)
                nc.scalar.activation(k.rows[:, n % BUF, 0:w], k.rows[:, n % BUF, 0:w], ACT.Exp,
                                     bias=k.stats[:, 0, n % BUF:n % BUF + 1],
                                     accum_out=k.stats[:, 1, n % BUF:n % BUF + 1]).then_inc(risen, 1)
                if n >= 2:
                    keep(n - 2)
                if n % 8 == 5 and n > 8:
                    move(n // 8 - 1)
            keep(len(items) - 2)
            keep(len(items) - 1)
            move(NQ - 1)


def short_conv_mixer(k):
    nc = k.nc
    out, padded, steps, done = (k.sem("sc_" + s) for s in ("out", "padded", "steps", "done"))
    with nc.Block() as block:
        @block.sync
        def _(sp):
            k.load_ahead(sp, "sc_in")

        @block.tensor
        def _(pe):
            k.product(pe, "sc_in", k.normed, T, out)

        @block.scalar
        def _(act):
            for j in range(3 * KT):
                act.wait_ge(k.weights_used, k.product_done("sc_in", j))
                if j >= 6:
                    act.wait_ge(done, j // 3 - 1)
                nc.scalar.copy(k.scratch[:, j % 6, :], k.psum[:, j % PRODUCT_BANKS, :]).then_inc(out, 1)

        @block.vector
        def _(dve):
            link = Link(dve, steps)
            link(nc.vector.memset(k.up_in[:, 0, 0, 0:2], 0.0))
            w, b = k.vec("sc_conv"), k.vec("sc_conv_b")
            src, dst = k.up_in[:, 0, 0], k.conv_g[:, 0, :]
            k.split_weights(dve, "sc_in", -1)
            for i in range(KT):
                c, v, g = (k.scratch[:, (3 * i + x) % 6, :] for x in range(3))
                k.split_weights(dve, "sc_in", 3 * i)
                k.split_weights(dve, "sc_in", 3 * i + 1)
                dve.wait_ge(out, 3 * i + 2)
                if i >= 1:
                    dve.wait_ge(done, i)
                link(nc.vector.tensor_tensor(src[:, 2:2 + T], c, v, ALU.mult))
                link(nc.vector.tensor_scalar(dst, src[:, 0:T], w[:, i:i + 1], b[:, i:i + 1],
                                             ALU.mult, ALU.add))
                for tap in (1, 2):
                    link(nc.vector.scalar_tensor_tensor(dst, src[:, tap:tap + T],
                                                        w[:, KT * tap + i:KT * tap + i + 1], dst,
                                                        ALU.mult, ALU.add))
                k.split_weights(dve, "sc_in", 3 * i + 2)
                dve.wait_ge(out, 3 * i + 3)
                nc.vector.tensor_tensor(k.hid_low[:, i, :], dst, g, ALU.mult).then_inc(done, 1)
                dve.wait_ge(done, i + 1)
                link(split(k, link, k.hid_high[:, i, :], k.hid_low[:, i, :]))


def store_output(k):
    nc = k.nc
    stored = k.stored
    with nc.Block() as block:
        @block.sync
        def _(sp):
            sp.dma_start(k.dram["out"], k.h[:]).then_inc(stored, 16)
            sp.wait_ge(stored, 16)


def build(nc, dram, wheres, vec_at, last_stage=None):
    done = []

    def reached(name):
        done.append(name)
        return last_stage == name

    with ExitStack() as ctx:
        k = Kernel(nc, ctx, dram)
        k.vec_at = vec_at
        k.tables = [(k.sb("consts_0", [P, dram["consts_0"].shape[1]]), wheres[0])]
        k.vecs = k.sb("vecs", [P, dram["vecs"].shape[1]])
        k.h = k.sb("h", [P, KT, T])
        k.n = k.sb("n", [P, KT, T])
        k.n_low = k.sb("n_low", [P, KT, T])
        k.sum_sq = k.sb("sum_sq", [P, T])
        k.rstd = k.sb("rstd", [P, T])[:]
        k.small = k.sb("small", [P, 4, 16])
        room = k.sb("scratch", [P, 6 * (T + 3)])
        k.scratch = room[:, 0:6 * T].rearrange("p (a x) -> p a x", x=T)
        k.squares = k.scratch[:, 0:2, :]
        k.cond = k.sb("cond", [P, KT])
        k.mod_cols = k.sb("mod_cols", [P, 96])
        k.mod_loaded = [ctx.enter_context(nc.semaphore(f"mod_loaded{i}")) for i in range(2)]

        with ExitStack() as first:
            k.tables.append((k.sb("consts_1", [P, dram["consts_1"].shape[1]], ctx=first), wheres[1]))
            k.masks = k.sb("masks", [P, len(LEVELS) + 1, P], ctx=first)
            load_inputs(k)
            condition(k)
            prepare(k, "mix_norm", k.h, k.vec("mix_norm"), k.n, k.n_low)
            with ExitStack() as a:
                k.z = k.sb("z1", [P, 31, T], ctx=a)
                with ExitStack() as b:
                    modulation_buffers(k, b, "a")
                    k.conv_in = room[:, :].rearrange("p (a x) -> p a x", x=T + 3)
                    mixer_projection(k)
                k.o = k.n
                k.v_tok = k.n_low[:, :, :].rearrange("p (m a) (b x) -> p m (a b) x", m=4, x=256)
                k.k_tok = k.sb("k_tok", [P, TT, 256], ctx=a)
                k.misc_tok = k.sb("misc_tok", [P, TT, P], ctx=a)
                with ExitStack() as b:
                    k.cum = k.sb("cum", [P, 3, T], ctx=b)
                    with ExitStack() as c:
                        k.gla_up = k.sb("gla_up", [P, P], ctx=c)
                        k.positions = k.sb("positions", [P, T], I32, ctx=c)
                        k.half_pi = k.sb("half_pi", [P, 1], ctx=c)
                        load(k, "mixer_inputs", [(k.gla_up[64:96, :], "gla_up"), (k.positions[:], "positions")])
                        rotary(k)
                        k.head_sq = k.scratch
                        head_norm(k, "delta_qk", [(k.z[:, j, :], k.z[:, j, :], (HD ** -0.5 if j < BK else 1.0),
                                                   None) for j in (BQ, BQ + 1, BK, BK + 1)], 1.0)
                        log_decays(k)
                    if reached("mix_inputs"):
                        return k
                    groups = [([k.z[:, t + i % 2, (2 * g + i // 2) * P:(2 * g + i // 2 + 1) * P]
                                for i in range(4)], dst[:, 2 * g:2 * g + 2, :])
                              for t, dst in ((RV, k.v_tok[:, 0]), (BV, k.v_tok[:, 1]), (CV, k.v_tok[:, 2]),
                                             (DI, k.v_tok[:, 3]), (BK, k.k_tok)) for g in range(2)]
                    groups.append(([k.z[:, MISC, c * P:(c + 1) * P] for c in range(TT)], k.misc_tok[:, :, :]))
                    turn(k, "mix_turn", groups)
                    retention(k)
                    if reached("retention"):
                        return k
                    used = k.z[:, 0:10, :].rearrange("p (h a) x -> p h (a x)", h=2)
                    idle = k.high[:, :, :, :].rearrange("p a b x -> p (a b x)")[:, 0:TT * (T + P)]
                    scores = [used[:, 0, :], used[:, 1, :], idle, k.sb("scores", [P, TT * (T + P)], ctx=b)[:]]
                    gated_scores(k, "gla", k.cum[:, 0, :], k.z[:, CQ, :], k.z[:, CK, :], 32, scores)
                    mix_values(k, "gla", 2, scores)
                    for i in range(2):
                        gated_scores(k, f"hgrn{i}", k.cum[:, 1 + i, :], k.z[:, DQ + i, :], k.z[:, DF + i, :],
                                     HD, scores[2 * i:2 * i + 2])
                    mix_values(k, "hgrn", 3, scores)
                if reached("gated"):
                    return k
                with ExitStack() as b:
                    k.gamma, k.q_sb, k.qg = k.z[:, 0:4, :], k.z[:, 4:6, :], k.z[:, 6:8, :]
                    k.nt, k.inv_n = k.z[:, 8:12, :], k.z[:, DQ:DQ + 4, :]
                    k.ratio = k.sb("ratio", [P, HEADS, T], ctx=b)
                    k.nb = k.sb("nb", [P, HEADS, T], ctx=b)
                    k.inv_t = k.high[:, :, :, :].rearrange("p a b x -> p (a b x)")[:, 0:HEADS * T].rearrange(
                        "p (h x) -> p h x", h=HEADS)
                    k.g_tok, k.gc_tok, k.gamma_tok, k.beta, k.tail = (
                        k.sb(s, [P, 16], ctx=b)[:] for s in ("g_tok", "gc_tok", "gamma_tok", "beta", "tail"))
                    k.whole = k.sb("whole", [P, 2, TT], ctx=b)
                    k.state = k.sb("state", [P, 2, HD], ctx=b)
                    delta_prepare(k)
                    if reached("delta_prepare"):
                        return k
                    delta_inverse(k)
                    if reached("delta_inverse"):
                        return k
                    delta_scan(k)
                    if reached("delta"):
                        return k
                gates = [RG, RG + 1, BG, BG + 1, CG, CG + 1, DG, DG + 1]
                gains = [1.0, 1.0] + [k.vec(s) for s in ("gdn_norm", "gla_norm", "hgrn_norm") for _ in range(2)]
                k.clear_stage_semaphores()
                lows = list(range(0, 8))
                highs = list(range(8, 12)) + [BQ, BQ + 1, BK, BK + 1]
                with ExitStack() as b:
                    k.head_sq = k.sb("head_sq", [P, 8, T], ctx=b)
                    head_norm(k, "mix_out_norm", [(k.o[:, i, :], k.z[:, lows[i], :], gains[i],
                                                   k.z[:, gates[i], :]) for i in range(8)], 1.0 / HD,
                              [k.z[:, t, :] for t in highs])
                with ExitStack() as b:
                    modulation_buffers(k, b, "b")
                    residual_product(k, "mix_out", lambda kk: (k.z[:, highs[kk], :], k.z[:, lows[kk], :]),
                                     k.vec("att_norm"), Modulation(k, "mix_out", 24, 8))
            if reached("mix"):
                return k
            with ExitStack() as a:
                modulation_buffers(k, a, "c")
                k.mem_k = k.sb("mem_k", [P, KT, MEM], ctx=a)
                k.mem_v = k.sb("mem_v", [P, 2, D], ctx=a)
                k.sum_sq, kept = k.sb("mem_sum_sq", [P, T], ctx=a), k.sum_sq
                with ExitStack() as b:
                    k.mem = k.sb("mem", [P, KT, MEM], ctx=b)
                    k.mem_high = k.sb("mem_high", [P, KT, MEM], ctx=b)
                    k.mem_low = k.sb("mem_low", [P, KT, MEM], ctx=b)
                    k.mem_vt = k.sb("mem_vt", [P, KT, MEM], ctx=b)
                    load(k, "mem", [(k.mem[:], "mem_t")])
                    prepare(k, "mem_norm", k.mem, k.vec("mem_norm"), k.mem_high, k.mem_low, MEM)
                    memory_projections(k)
                k.sum_sq = kept
                k.z = k.sb("z_att", [P, KT, T], ctx=a)
                k.probs_t = k.sb("probs_t", [P, 8, T], ctx=a)
                k.att_high = k.sb("att_high", [P, KT, T], ctx=a)
                k.att_low = k.z
                cross_attention(k)
                residual_product(k, "att_o", lambda kk: (k.att_high[:, kk, :], k.att_low[:, kk, :]),
                                 k.vec("ffn_norm"), Modulation(k, "att_o", 40, 8))
            if reached("att"):
                return k
        k.tables.pop()
        k.clear_stage_semaphores()
        modulation(k)
        with ExitStack() as a:
            ffn_buffers(k, a, 0)
            ffn_up(k, 0)
            residual_product(k, "down_0", k.hidden)
        boundary(k, "ab_norm", k.vec("final_norm"), False, mod_part(k, 0, 1), mod_part(k, 0, 0))
        if reached("block1"):
            return k

        with ExitStack() as a:
            k.tables.append((k.sb("consts_2", [P, dram["consts_2"].shape[1]], ctx=a), wheres[2]))
            load(k, "consts_2", [(k.tables[1][0][:], "consts_2")])
            k.z = k.sb("z2", [P, 37, T], ctx=a)
            with ExitStack() as b:
                k.conv_in = k.sb("conv_in2", [P, 2, T + 3], ctx=b)
                ab_projection(k)
            k.ab_low = k.sb("ab_low", [P, KT, T], ctx=a)
            k.lru_w = k.scratch[:, 2:6, :].rearrange("p (g a) (i x) -> p g (a i) x", g=2, x=P)
            k.lru_r, k.lru_i, k.lru_t = k.ab_low, k.n_low, k.n
            load(k, "lru", [(k.lru_w, "lru_w")])
            recurrence(k)
            if reached("lru"):
                return k
            k.cmp_k = k.sb("cmp_k", [P, 2, 32], ctx=a)
            k.cmp_v = k.sb("cmp_v", [P, NG, HD], ctx=a)
            k.block_bias = k.sb("block_bias", [P, TT, NG, NBLK], ctx=a)
            with ExitStack() as b:
                k.pairs = k.ab_low[:, :, :].rearrange("p (a g) x -> p a g x", a=2)
                k.cmp_w1 = k.z[:, XR:XR + KT, :].rearrange("p (a j) (i x) -> p a (j i) x", a=2, x=P)
                k.cmp_w2 = k.sb("cmp_w2", [P, 2, HD], ctx=b)
                k.cmp_hid = k.scratch[:, 0, 0:2 * NG * 32].rearrange("p (a g n) -> p a g n", a=2, g=NG)
                k.cmp_hid4 = k.scratch[:, 1, :].rearrange("p (g r n) -> p g r n", g=NG, r=4)
                compress(k)
            k.gate_tok = k.sb("gate_tok", [P, TT, P], ctx=a)
            k.vs_tok = k.z[:, KC:KC + 2, :].rearrange("p a (b x) -> p (a b) x", x=256)
            k.vw_tok = k.z[:, VC:VC + 2, :].rearrange("p a (b x) -> p (a b) x", x=256)
            turn(k, "nsa_turn", [([k.z[:, GL, c * P:(c + 1) * P] for c in range(TT)], k.gate_tok[:, :, :])]
                 + [([k.z[:, t + i % 2, (2 * g + i // 2) * P:(2 * g + i // 2 + 1) * P] for i in range(4)],
                     dst[:, 2 * g:2 * g + 2, :]) for t, dst in ((VS, k.vs_tok), (VW, k.vw_tok)) for g in range(2)])
            k.cmp_pt = [k.z[:, t, :] for t in (VS, VS + 1, VW, VW + 1)]
            compressed_attention(k)
            if reached("cmp"):
                return k
            partial_rotary(k)
            k.pt = k.z[:, 0:16, :].rearrange("p (a b j) x -> p a b j x", a=2, b=2)
            k.rows = k.scratch[:, 0:4, :]
            k.stats = k.sb("stats", [P, 2, 4], ctx=a)
            idle = k.high[:, :, :, :].rearrange("p a b x -> p (a b x)")
            per = TT * (TT + 1) // 2 * P
            k.sel_bias = [[idle[:, a * per + i * (i + 1) // 2 * P:a * per + (i + 1) * (i + 2) // 2 * P]
                           for i in range(TT)] for a in range(2)]
            sparse_attention(k)
            if reached("nsa"):
                return k
            plain_product(k, "ab_out", lambda kk: (
                (k.n_low[:, kk, :], k.n[:, kk, :]) if kk < KT
                else (k.z[:, NQT + kk - KT, :], k.ab_low[:, kk - KT, :])), k.z[:, 0:KT, :])
            boundary(k, "ffn_norm_1", mod_part(k, 0, 2), True, mod_part(k, 0, 4), mod_part(k, 0, 3),
                     k.z[:, 0:KT, :])
        if reached("ab"):
            return k
        k.tables.pop()
        k.clear_stage_semaphores()
        with ExitStack() as a:
            ffn_buffers(k, a, 1)
            ffn_up(k, 1)
            plain_product(k, "down_1", k.hidden, k.n)
        boundary(k, "sc_norm", mod_part(k, 0, 5), True, mod_part(k, 1, 1), mod_part(k, 1, 0))
        if reached("ffn1"):
            return k
        with ExitStack() as a:
            ffn_buffers(k, a, "sc", KT)
            k.conv_g = k.sb("conv_sc", [P, 1, T], ctx=a)
            short_conv_mixer(k)
            plain_product(k, "sc_out", k.hidden, k.n)
        boundary(k, "ffn_norm_2", mod_part(k, 1, 2), True, mod_part(k, 1, 4), mod_part(k, 1, 3))
        if reached("sc2"):
            return k
        with ExitStack() as a:
            ffn_buffers(k, a, 2)
            ffn_up(k, 2)
            plain_product(k, "down_2", k.hidden, k.n)
        boundary(k, "last_norm", mod_part(k, 1, 5), True)
        store_output(k)
    return k


def modulation_buffers(k, ctx, name):
    k.mod_w = k.sb("mod_w_" + name, [P, 2, KT, 256], ctx=ctx)
    k.mod_acc = k.sb("mod_acc_" + name, [P, 2, 256], ctx=ctx)


def ffn_buffers(k, ctx, idx, tiles=FT):
    k.up_in = k.sb(f"up_in{idx}", [P, 2, 2, T + 2], ctx=ctx)
    k.conv_g, k.conv_v = k.scratch[:, 2:4, :], k.scratch[:, 4:6, :]
    k.hid_high = k.sb(f"hid_high{idx}", [P, tiles, T], ctx=ctx)
    k.hid_low = k.sb(f"hid_low{idx}", [P, tiles, T], ctx=ctx)
    k.hidden = lambda kk: (k.hid_high[:, kk, :], k.hid_low[:, kk, :])


def tiled(w):
    kk, n = w.shape
    if n % P:
        w = np.concatenate([w, np.zeros((kk, P - n % P), w.dtype)], axis=1)
    return np.ascontiguousarray(w.reshape(kk // P, P, -1, P).transpose(2, 1, 0, 3))


def columns(v):
    v = np.asarray(v)
    return np.ascontiguousarray(v.reshape(-1, P).T)


def laid_out(x, mem, positions, mix_norm_w, w_in, gdn_conv_w, gdn_a_log, gdn_dt_bias, gdn_norm_w,
             gla_gk_up, gla_gk_bias, gla_norm_w, hgrn_lb_logits, hgrn_norm_w, w_out, xattn_norm_w,
             mem_norm_w, xattn_wq, xattn_wk, xattn_wv, xattn_wo, ffn_norm_w, ffn_up, ffn_conv_w,
             ffn_down, final_norm_w, c_2, mod_w_2, mod_b_2, norm_mix_pre_2, norm_mix_post_2,
             norm_ffn_pre_2, norm_ffn_post_2, ab_w_in_2, ab_conv_w_2, ab_conv_b_2, lru_w_r_2, lru_b_r_2,
             lru_w_i_2, lru_b_i_2, lru_lam_2, cmp_pe_k_2, cmp_pe_v_2, cmp_wk1_2, cmp_wk2_2, cmp_wv1_2,
             cmp_wv2_2, ab_w_out_2, sc_w_in_2, sc_conv_w_2, sc_conv_b_2, sc_w_out_2, ffn_w_gate_2,
             ffn_w_up_2, ffn_conv_w_2, ffn_conv_b_2, ffn_w_down_2):
    a = {}
    tables = constants()
    for i, (table, _) in enumerate(tables):
        a[f"consts_{i}"] = table
    wheres = [where for _, where in tables]
    a["masks"] = level_masks()

    def feature_major(v):
        return np.ascontiguousarray(v[0].T.reshape(KT, P, -1).transpose(1, 0, 2))

    a["x_t"], a["mem_t"] = feature_major(x), feature_major(mem)
    a["positions"] = np.ascontiguousarray(np.broadcast_to(positions, (P, T)))

    sizes = [256] * 7 + [4, 4, 256, 128, 128, 256, 16, 256] + [256] * 4
    parts = np.split(w_in[0], np.cumsum(sizes)[:-1], axis=1)
    (rq, rk, rv, rg, bq, bk, bv, ba, bb, bg, cq, ck, cv, c_lr, cg, dq, df, di, dg) = parts
    misc = np.zeros((D, P), np.float32)
    misc[:, 0:4], misc[:, 32:36], misc[:, 64:80] = ba, bb, c_lr
    a["w_mix_in"] = tiled(np.concatenate([rq, rk, rv, bv, cv, di, rg, bq, bk, bg, cg, dq, df, dg,
                                          cq, ck, misc], axis=1))
    a["w_mem_k"], a["w_mem_v"] = tiled(xattn_wk[0]), tiled(xattn_wv[0])
    a["w_mix_out"], a["w_att_q"], a["w_att_o"] = tiled(w_out[0]), tiled(xattn_wq[0]), tiled(xattn_wo[0])
    gate, val = tiled(ffn_up[0][:, :FF]), tiled(ffn_up[0][:, FF:])
    a["w_up_0"] = np.stack([gate, val], axis=1).reshape(2 * FT, P, KT, P)
    a["w_down_0"] = tiled(ffn_down[0])
    up = np.zeros((32, P), np.float32)
    up[0:16] = gla_gk_up[0]
    a["gla_up"] = up

    a["mod_w"] = np.ascontiguousarray(
        mod_w_2.reshape(2, KT, P, 24, 256).transpose(0, 3, 2, 1, 4).reshape(48, P, KT, 256))

    heads = [4 * (2 * gp + odd) + r for gp in range(2) for r in range(4) for odd in range(2)]
    order = np.concatenate([np.arange(HD) + HD * h for h in heads])
    sizes = [1024, 1024, 1024] + [256] * 6 + [48]
    parts = np.split(ab_w_in_2[0], np.cumsum(sizes)[:-1], axis=1)
    parts[2] = parts[2][:, order]
    a["w_ab_in"] = tiled(np.concatenate(parts, axis=1))
    wo = ab_w_out_2[0]
    a["w_ab_out"] = tiled(np.concatenate([wo[:1024], wo[1024:][order]], axis=0))
    for i in range(2):
        gate, val = tiled(ffn_w_gate_2[i]), tiled(ffn_w_up_2[i])
        a[f"w_up_{i + 1}"] = np.stack([gate, val], axis=1).reshape(2 * FT, P, KT, P)
        a[f"w_down_{i + 1}"] = tiled(ffn_w_down_2[i])
    b_part, c_part, v_part = (tiled(sc_w_in_2[0][:, i * D:(i + 1) * D]) for i in range(3))
    a["w_sc_in"] = np.stack([c_part, v_part, b_part], axis=1).reshape(3 * KT, P, KT, P)
    a["w_sc_out"] = tiled(sc_w_out_2[0])

    lru = np.zeros((P, 2, KT, P), np.float32)
    for g, w in enumerate((lru_w_r_2[0], lru_w_i_2[0])):
        for n in range(16):
            s = slice(64 * (n % 2), 64 * (n % 2) + 64)
            lru[s, g, n // 2, s] = w[n]
    a["lru_w"] = lru
    a["cmp_w1"] = np.ascontiguousarray(
        np.stack([w[0].reshape(16, P, P) for w in (cmp_wk1_2, cmp_wv1_2)]).transpose(2, 0, 1, 3))
    a["cmp_w2"] = np.ascontiguousarray(np.stack([cmp_wk2_2[0], cmp_wv2_2[0]], axis=1))

    v = {
        "mix_norm": columns(mix_norm_w), "att_norm": columns(xattn_norm_w), "mem_norm": columns(mem_norm_w),
        "ffn_norm": columns(ffn_norm_w), "final_norm": columns(final_norm_w),
        "gdn_conv": columns(gdn_conv_w[0]), "ffn_conv_0": columns(ffn_conv_w[0]),
        "gla_bias": columns(gla_gk_bias[0]),
        "gdn_norm": columns(np.tile(gdn_norm_w[0], 2)), "gla_norm": columns(np.tile(gla_norm_w[0], 2)),
        "hgrn_norm": columns(np.tile(hgrn_norm_w[0], 2)),
        "a_log": np.broadcast_to(gdn_a_log, (P, HEADS)), "dt_bias": np.broadcast_to(gdn_dt_bias, (P, HEADS)),
        "ab_conv": columns(ab_conv_w_2[0]), "ab_conv_b": columns(ab_conv_b_2),
        "lru_b_r": columns(lru_b_r_2), "lru_b_i": columns(lru_b_i_2), "lru_lam": columns(lru_lam_2),
        "sc_conv": columns(sc_conv_w_2[0]), "sc_conv_b": columns(sc_conv_b_2), "cond": columns(c_2),
        "pe_k": columns(cmp_pe_k_2), "pe_v": columns(cmp_pe_v_2),
    }
    v["mod_b"] = columns(mod_b_2)
    for i in range(2):
        v[f"mix_pre_{i}"], v[f"mix_post_{i}"] = columns(norm_mix_pre_2[i]), columns(norm_mix_post_2[i])
        v[f"ffn_pre_{i}"], v[f"ffn_post_{i}"] = columns(norm_ffn_pre_2[i]), columns(norm_ffn_post_2[i])
        v[f"ffn_conv_{i + 1}"] = columns(ffn_conv_w_2[i])
        v[f"ffn_conv_b_{i + 1}"] = columns(ffn_conv_b_2[i])
    at, vec_at = 0, {}
    for name, n in VECTORS.items():
        assert v[name].shape == (P, n), name
        vec_at[name] = (at, at + n)
        at += n
    a["vecs"] = np.ascontiguousarray(np.concatenate([v[name] for name in VECTORS], axis=1))
    return a, wheres, vec_at


def program(nc, arrays, wheres, vec_at, last_stage=None):
    dram = {name: nc.dram_tensor("in_" + name, v.shape, mybir.dt.from_np(v.dtype), kind="ExternalInput").ap()
            for name, v in arrays.items()}
    dram["out"] = nc.dram_tensor("out_t", (P, KT, T), F32, kind="ExternalOutput").ap()
    return build(nc, dram, wheres, vec_at, last_stage)


def kernel(**inputs):
    import concourse.bacc as bacc
    from concourse.bass_utils import run_bass_kernel_spmd

    arrays, wheres, vec_at = laid_out(**{name: np.asarray(v) for name, v in inputs.items()})
    nc = bacc.Bacc("TRN2", target_bir_lowering=False, num_devices=1)
    program(nc, arrays, wheres, vec_at)
    result = run_bass_kernel_spmd(nc, [{"in_" + name: v for name, v in arrays.items()}], core_ids=[0])
    out = result.results[0]["out_t"]
    return np.ascontiguousarray(out.transpose(2, 1, 0)).reshape(1, T, D)
```
